# Optimizing a Trainium2 kernel written in Bass

```python
import math
import jax, jax.numpy as jnp
from jax import lax
import numpy as np

D_MODEL = 1024
BATCH = 1
SEQ = 256
DEPTH = 1
DEC_BATCH = 8
DEC_SEQ = 4
PAST_LEN = 2048
PAGE_SIZE = 128

SSM_WIDTH = D_MODEL // 2
SSM_GROUP = 16
SSM_GROUPS = SSM_WIDTH // SSM_GROUP
SSM_STATE = 64
DT_MIN = 0.001
DT_MAX = 0.1
ATT_WIDTH = D_MODEL // 2
ATT_HEADS = 4
V_DIM = ATT_WIDTH // ATT_HEADS
HEAD_DIM = V_DIM // 2
QK_DIM = 2 * HEAD_DIM
IN_COLS = SSM_WIDTH + 3 * ATT_WIDTH
ROPE_THETA = 10000.0
Q_BLOCK = 128
NEG_INF = -1e30
N_EXPERTS = 32
TOP_K = 4
D_EXPERT = D_MODEL
SWIGLU_LIMIT = 7.0
SWIGLU_ALPHA = 1.702
MOE_BLOCK = 128
NORM_EPS = 1e-6

kernel_name = 'hybrid_s5_diffattn_moe_step'

def rms_norm(x, g):
    xf = x.astype(jnp.float32)
    y = xf * lax.rsqrt(jnp.mean(xf * xf, axis=-1, keepdims=True) + NORM_EPS)
    return (y * g.astype(jnp.float32)).astype(x.dtype)

def rotary(x, pos):
    half = HEAD_DIM // 2
    inv_freq = ROPE_THETA ** (-jnp.arange(half, dtype=jnp.float32) / half)
    ang = pos.astype(jnp.float32)[:, None] * inv_freq[None, :]
    cos = jnp.cos(ang)[None, :, None, None, :]
    sin = jnp.sin(ang)[None, :, None, None, :]
    xf = x.astype(jnp.float32)
    x1, x2 = xf[..., :half], xf[..., half:]
    return jnp.concatenate([x1 * cos - x2 * sin, x2 * cos + x1 * sin], axis=-1).astype(x.dtype)

def _complex_affine_combine(e1, e2):
    a1r, a1i, b1r, b1i = e1
    a2r, a2i, b2r, b2i = e2
    return (a2r * a1r - a2i * a1i,
            a2r * a1i + a2i * a1r,
            a2r * b1r - a2i * b1i + b2r,
            a2r * b1i + a2i * b1r + b2i)

def s5_scan(u, x0_re, x0_im, lam_re, lam_im, log_dt, b_re, b_im, c_re, c_im, d_skip):
    f32 = jnp.float32
    lam_re = lam_re.astype(f32)
    lam_im = lam_im.astype(f32)
    dt = jnp.exp(log_dt.astype(f32))[:, None]
    mag = jnp.exp(lam_re * dt)
    a_re = mag * jnp.cos(lam_im * dt)
    a_im = mag * jnp.sin(lam_im * dt)
    den = lam_re * lam_re + lam_im * lam_im
    f_re = ((a_re - 1.0) * lam_re + a_im * lam_im) / den
    f_im = (a_im * lam_re - (a_re - 1.0) * lam_im) / den
    br = b_re.astype(f32)
    bi = b_im.astype(f32)
    bb_re = f_re[..., None] * br - f_im[..., None] * bi
    bb_im = f_re[..., None] * bi + f_im[..., None] * br
    uf = u.astype(f32)
    z_re = jnp.einsum('btgh,gph->btgp', uf, bb_re)
    z_im = jnp.einsum('btgh,gph->btgp', uf, bb_im)
    A_re = jnp.broadcast_to(a_re, z_re.shape)
    A_im = jnp.broadcast_to(a_im, z_im.shape)
    P_re, P_im, S_re, S_im = lax.associative_scan(
        _complex_affine_combine, (A_re, A_im, z_re, z_im), axis=1)
    x0r = x0_re.astype(f32)[:, None]
    x0i = x0_im.astype(f32)[:, None]
    x_re = P_re * x0r - P_im * x0i + S_re
    x_im = P_re * x0i + P_im * x0r + S_im
    y = (jnp.einsum('btgp,ghp->btgh', x_re, c_re.astype(f32))
         - jnp.einsum('btgp,ghp->btgh', x_im, c_im.astype(f32))
         + d_skip.astype(f32) * uf)
    return y, x_re[:, -1], x_im[:, -1]

def diff_attend(q, q_pos, k_segs, v_segs, kpos_segs, lam):
    scale = HEAD_DIM ** -0.5
    scores = []
    for k, kp in zip(k_segs, kpos_segs):
        s = jnp.einsum('bqhcd,bkhcd->bhcqk', q, k, preferred_element_type=jnp.float32) * scale
        causal = kp[None, :] <= q_pos[:, None]
        scores.append(jnp.where(causal[None, None, None], s, NEG_INF))
    p = jax.nn.softmax(jnp.concatenate(scores, axis=-1), axis=-1)
    w = p[:, :, 0] - lam * p[:, :, 1]
    outs = []
    off = 0
    for v in v_segs:
        n = v.shape[1]
        outs.append(jnp.einsum('bhqk,bkhe->bqhe', w[..., off:off + n].astype(v.dtype), v,
                               preferred_element_type=jnp.float32))
        off += n
    return sum(outs)

def moe(h, w_router, b_router, w_gu, b_gu, w_down, b_down):
    n_tok = h.shape[0]
    logits = (h @ w_router + b_router).astype(jnp.float32)
    top_val, top_idx = lax.top_k(logits, TOP_K)
    gate = jax.nn.softmax(top_val, axis=-1)
    m = n_tok * TOP_K
    e_flat = top_idx.reshape(m).astype(jnp.int32)
    t_flat = jnp.repeat(jnp.arange(n_tok, dtype=jnp.int32), TOP_K)
    g_flat = gate.reshape(m)
    order = jnp.argsort(e_flat)
    e_sorted = e_flat[order]
    t_sorted = t_flat[order]
    g_sorted = g_flat[order]
    counts = jnp.bincount(e_flat, length=N_EXPERTS)
    padded = (counts + MOE_BLOCK - 1) // MOE_BLOCK * MOE_BLOCK
    start = jnp.cumsum(counts) - counts
    pend = jnp.cumsum(padded)
    pstart = pend - padded
    dest = pstart[e_sorted] + jnp.arange(m, dtype=jnp.int32) - start[e_sorted]
    n_rows = (m + MOE_BLOCK - 1) // MOE_BLOCK * MOE_BLOCK + N_EXPERTS * MOE_BLOCK
    n_blocks = n_rows // MOE_BLOCK
    row_tok = jnp.full((n_rows,), n_tok, jnp.int32).at[dest].set(t_sorted)
    row_gate = jnp.zeros((n_rows,), jnp.float32).at[dest].set(g_sorted)
    blk_start = jnp.arange(n_blocks, dtype=jnp.int32) * MOE_BLOCK
    blk_expert = jnp.minimum(jnp.searchsorted(pend, blk_start, side='right'), N_EXPERTS - 1)
    h_pad = jnp.concatenate([h, jnp.zeros((1, h.shape[1]), h.dtype)], axis=0)
    xs = h_pad[row_tok].reshape(n_blocks, MOE_BLOCK, h.shape[1])

    def expert_block(args):
        xb, e = args
        gu = xb @ w_gu[e] + b_gu[e]
        g_lin = jnp.minimum(gu[:, 0::2], SWIGLU_LIMIT)
        up = jnp.clip(gu[:, 1::2], -SWIGLU_LIMIT, SWIGLU_LIMIT)
        act = (up + 1.0) * (g_lin * jax.nn.sigmoid(SWIGLU_ALPHA * g_lin))
        return act @ w_down[e] + b_down[e]

    ys = lax.map(expert_block, (xs, blk_expert)).reshape(n_rows, h.shape[1])
    out = jax.ops.segment_sum(ys.astype(jnp.float32) * row_gate[:, None], row_tok,
                              num_segments=n_tok + 1)[:n_tok]
    return out.astype(h.dtype)

def trunk_layer(x, pos, ssm_x0_re, ssm_x0_im, past_k, past_v, past_pos, lp, lambda_init):
    bsz, t_len, _ = x.shape
    h = rms_norm(x, lp['norm_mix_g'])
    proj = h @ lp['w_in']
    u = proj[..., :SSM_WIDTH]
    q = proj[..., SSM_WIDTH:SSM_WIDTH + ATT_WIDTH].reshape(bsz, t_len, ATT_HEADS, 2, HEAD_DIM)
    k = proj[..., SSM_WIDTH + ATT_WIDTH:SSM_WIDTH + 2 * ATT_WIDTH].reshape(
        bsz, t_len, ATT_HEADS, 2, HEAD_DIM)
    v = proj[..., SSM_WIDTH + 2 * ATT_WIDTH:].reshape(bsz, t_len, ATT_HEADS, V_DIM)

    y_ssm, st_re, st_im = s5_scan(
        u.reshape(bsz, t_len, SSM_GROUPS, SSM_GROUP), ssm_x0_re, ssm_x0_im,
        lp['ssm_lambda_re'], lp['ssm_lambda_im'], lp['ssm_log_dt'],
        lp['ssm_b_re'], lp['ssm_b_im'], lp['ssm_c_re'], lp['ssm_c_im'], lp['ssm_d'])
    y_ssm = jax.nn.gelu(y_ssm.reshape(bsz, t_len, SSM_WIDTH)).astype(x.dtype)
    y_ssm = y_ssm * jax.nn.sigmoid(y_ssm @ lp['ssm_w_glu'] + lp['ssm_b_glu'])

    q = rotary(q, pos)
    k = rotary(k, pos)
    f32 = jnp.float32
    lam = (jnp.exp(jnp.sum(lp['lambda_q1'].astype(f32) * lp['lambda_k1'].astype(f32)))
           - jnp.exp(jnp.sum(lp['lambda_q2'].astype(f32) * lp['lambda_k2'].astype(f32)))
           + lambda_init)
    if past_k is None:
        n_blk = t_len // Q_BLOCK
        q_blocks = jnp.moveaxis(q.reshape(bsz, n_blk, Q_BLOCK, ATT_HEADS, 2, HEAD_DIM), 1, 0)
        pos_blocks = pos.reshape(n_blk, Q_BLOCK)
        o = lax.map(lambda qp: diff_attend(qp[0], qp[1], [k], [v], [pos], lam),
                    (q_blocks, pos_blocks))
        o = jnp.moveaxis(o, 0, 1).reshape(bsz, t_len, ATT_HEADS, V_DIM)
    else:
        o = diff_attend(q, pos, [past_k, k], [past_v, v], [past_pos, pos], lam)
    o = rms_norm(o.astype(x.dtype), lp['attn_subln_g']) * (1.0 - lambda_init)
    o = o.reshape(bsz, t_len, ATT_WIDTH)

    gates = jax.nn.sigmoid(h @ lp['w_gate'] + lp['b_gate']).reshape(bsz, t_len, 2, D_MODEL)
    merged = (gates[:, :, 0] * (y_ssm @ lp['w_branch_ssm'])
              + gates[:, :, 1] * (o @ lp['w_branch_attn']))
    x = x + merged @ lp['w_out']

    h2 = rms_norm(x, lp['norm_ffn_g']).reshape(bsz * t_len, D_MODEL)
    x = x + moe(h2, lp['w_router'], lp['b_router'], lp['w_gate_up'], lp['b_gate_up'],
                lp['w_down'], lp['b_down']).reshape(bsz, t_len, D_MODEL)
    new_k = k.reshape(bsz, t_len, ATT_HEADS, QK_DIM)
    return x, new_k, v, st_re.astype(x.dtype), st_im.astype(x.dtype)

def setup_inputs(seed: int = 0) -> dict:
    key = jax.random.key(seed)
    ks = jax.random.split(key, 40)
    f32 = jnp.float32
    n_pages = PAST_LEN // PAGE_SIZE
    n_used = DEC_BATCH * n_pages
    n_phys = n_used + max(1, n_used // 4)

    def normal(k, shape, scale):
        return jax.random.normal(k, shape, f32) * scale

    def gain(k, shape):
        return 1.0 + 0.05 * jax.random.normal(k, shape, f32)

    page_table = jax.random.permutation(ks[6], n_phys)[:n_used].reshape(
        DEC_BATCH, n_pages).astype(jnp.int32)
    lam_im_base = jnp.pi * jnp.arange(SSM_STATE, dtype=f32)
    return {
        'x_prompt': normal(ks[0], (BATCH, SEQ, D_MODEL), 1.0),
        'x_sample': normal(ks[1], (DEC_BATCH, DEC_SEQ, D_MODEL), 1.0),
        'cache_k': normal(ks[2], (DEPTH, n_phys, PAGE_SIZE, ATT_HEADS, QK_DIM), 1.0),
        'cache_v': normal(ks[3], (DEPTH, n_phys, PAGE_SIZE, ATT_HEADS, V_DIM), 1.0),
        'state_ssm_re': normal(ks[4], (DEPTH, DEC_BATCH, SSM_GROUPS, SSM_STATE), 0.3),
        'state_ssm_im': normal(ks[5], (DEPTH, DEC_BATCH, SSM_GROUPS, SSM_STATE), 0.3),
        'page_table': page_table,
        'norm_mix_g': gain(ks[7], (DEPTH, D_MODEL)),
        'w_in': normal(ks[8], (DEPTH, D_MODEL, IN_COLS), D_MODEL ** -0.5),
        'ssm_lambda_re': -0.5 + 0.01 * jax.random.normal(ks[9], (DEPTH, SSM_GROUPS, SSM_STATE), f32),
        'ssm_lambda_im': lam_im_base + 0.01 * jax.random.normal(ks[10], (DEPTH, SSM_GROUPS, SSM_STATE), f32),
        'ssm_log_dt': jax.random.uniform(ks[11], (DEPTH, SSM_GROUPS), dtype=f32,
                                         minval=math.log(DT_MIN), maxval=math.log(DT_MAX)),
        'ssm_b_re': normal(ks[12], (DEPTH, SSM_GROUPS, SSM_STATE, SSM_GROUP), (2 * SSM_GROUP) ** -0.5),
        'ssm_b_im': normal(ks[13], (DEPTH, SSM_GROUPS, SSM_STATE, SSM_GROUP), (2 * SSM_GROUP) ** -0.5),
        'ssm_c_re': normal(ks[14], (DEPTH, SSM_GROUPS, SSM_GROUP, SSM_STATE), SSM_STATE ** -0.5),
        'ssm_c_im': normal(ks[15], (DEPTH, SSM_GROUPS, SSM_GROUP, SSM_STATE), SSM_STATE ** -0.5),
        'ssm_d': normal(ks[16], (DEPTH, SSM_GROUPS, SSM_GROUP), 1.0),
        'ssm_w_glu': normal(ks[17], (DEPTH, SSM_WIDTH, SSM_WIDTH), SSM_WIDTH ** -0.5),
        'ssm_b_glu': normal(ks[18], (DEPTH, SSM_WIDTH), 0.01),
        'lambda_q1': normal(ks[19], (DEPTH, HEAD_DIM), 0.1),
        'lambda_k1': normal(ks[20], (DEPTH, HEAD_DIM), 0.1),
        'lambda_q2': normal(ks[21], (DEPTH, HEAD_DIM), 0.1),
        'lambda_k2': normal(ks[22], (DEPTH, HEAD_DIM), 0.1),
        'attn_subln_g': gain(ks[23], (DEPTH, V_DIM)),
        'w_branch_ssm': normal(ks[24], (DEPTH, SSM_WIDTH, D_MODEL), SSM_WIDTH ** -0.5),
        'w_branch_attn': normal(ks[25], (DEPTH, ATT_WIDTH, D_MODEL), ATT_WIDTH ** -0.5),
        'w_gate': normal(ks[26], (DEPTH, D_MODEL, 2 * D_MODEL), D_MODEL ** -0.5),
        'b_gate': normal(ks[27], (DEPTH, 2 * D_MODEL), 0.01),
        'w_out': normal(ks[28], (DEPTH, D_MODEL, D_MODEL), D_MODEL ** -0.5),
        'norm_ffn_g': gain(ks[29], (DEPTH, D_MODEL)),
        'w_router': normal(ks[30], (DEPTH, D_MODEL, N_EXPERTS), D_MODEL ** -0.5),
        'b_router': normal(ks[31], (DEPTH, N_EXPERTS), 0.01),
        'w_gate_up': normal(ks[32], (DEPTH, N_EXPERTS, D_MODEL, 2 * D_EXPERT), D_MODEL ** -0.5),
        'b_gate_up': normal(ks[33], (DEPTH, N_EXPERTS, 2 * D_EXPERT), 0.01),
        'w_down': normal(ks[34], (DEPTH, N_EXPERTS, D_EXPERT, D_MODEL), D_EXPERT ** -0.5),
        'b_down': normal(ks[35], (DEPTH, N_EXPERTS, D_MODEL), 0.01),
        'norm_final_g': gain(ks[36], (D_MODEL,)),
    }

def reference(x_prompt, x_sample, cache_k, cache_v, state_ssm_re, state_ssm_im, page_table,
              norm_mix_g, w_in, ssm_lambda_re, ssm_lambda_im, ssm_log_dt, ssm_b_re, ssm_b_im,
              ssm_c_re, ssm_c_im, ssm_d, ssm_w_glu, ssm_b_glu, lambda_q1, lambda_k1, lambda_q2,
              lambda_k2, attn_subln_g, w_branch_ssm, w_branch_attn, w_gate, b_gate, w_out,
              norm_ffn_g, w_router, b_router, w_gate_up, b_gate_up, w_down, b_down, norm_final_g):
    n_pages = PAST_LEN // PAGE_SIZE
    past_len = n_pages * PAGE_SIZE
    dec_b = x_sample.shape[0]
    pos_prompt = jnp.arange(x_prompt.shape[1], dtype=jnp.int32)
    pos_sample = past_len + jnp.arange(x_sample.shape[1], dtype=jnp.int32)
    past_pos = jnp.arange(past_len, dtype=jnp.int32)
    zero_state = jnp.zeros((x_prompt.shape[0], SSM_GROUPS, SSM_STATE), jnp.float32)

    xp = x_prompt
    xs = x_sample
    kp_l, vp_l, srp_l, sip_l = [], [], [], []
    ks_l, vs_l, srs_l, sis_l = [], [], [], []
    for l in range(DEPTH):
        lp = {
            'norm_mix_g': norm_mix_g[l], 'w_in': w_in[l],
            'ssm_lambda_re': ssm_lambda_re[l], 'ssm_lambda_im': ssm_lambda_im[l],
            'ssm_log_dt': ssm_log_dt[l], 'ssm_b_re': ssm_b_re[l], 'ssm_b_im': ssm_b_im[l],
            'ssm_c_re': ssm_c_re[l], 'ssm_c_im': ssm_c_im[l], 'ssm_d': ssm_d[l],
            'ssm_w_glu': ssm_w_glu[l], 'ssm_b_glu': ssm_b_glu[l],
            'lambda_q1': lambda_q1[l], 'lambda_k1': lambda_k1[l],
            'lambda_q2': lambda_q2[l], 'lambda_k2': lambda_k2[l],
            'attn_subln_g': attn_subln_g[l],
            'w_branch_ssm': w_branch_ssm[l], 'w_branch_attn': w_branch_attn[l],
            'w_gate': w_gate[l], 'b_gate': b_gate[l], 'w_out': w_out[l],
            'norm_ffn_g': norm_ffn_g[l], 'w_router': w_router[l], 'b_router': b_router[l],
            'w_gate_up': w_gate_up[l], 'b_gate_up': b_gate_up[l],
            'w_down': w_down[l], 'b_down': b_down[l],
        }
        lambda_init = 0.8 - 0.6 * math.exp(-0.3 * l)
        xp, kp, vp, srp, sip = trunk_layer(xp, pos_prompt, zero_state, zero_state,
                                           None, None, None, lp, lambda_init)
        past_k = cache_k[l][page_table].reshape(dec_b, past_len, ATT_HEADS, 2, HEAD_DIM)
        past_v = cache_v[l][page_table].reshape(dec_b, past_len, ATT_HEADS, V_DIM)
        xs, ks_, vs_, srs, sis = trunk_layer(xs, pos_sample, state_ssm_re[l], state_ssm_im[l],
                                             past_k, past_v, past_pos, lp, lambda_init)
        kp_l.append(kp); vp_l.append(vp); srp_l.append(srp); sip_l.append(sip)
        ks_l.append(ks_); vs_l.append(vs_); srs_l.append(srs); sis_l.append(sis)

    y_prompt = rms_norm(xp, norm_final_g)
    y_sample = rms_norm(xs, norm_final_g)
    k_prompt = jnp.stack(kp_l)
    v_prompt = jnp.stack(vp_l)
    ssm_re_prompt = jnp.stack(srp_l)
    ssm_im_prompt = jnp.stack(sip_l)
    k_sample = jnp.stack(ks_l)
    v_sample = jnp.stack(vs_l)
    ssm_re_sample = jnp.stack(srs_l)
    ssm_im_sample = jnp.stack(sis_l)
    return (y_prompt, y_sample, k_prompt, v_prompt, ssm_re_prompt, ssm_im_prompt,
            k_sample, v_sample, ssm_re_sample, ssm_im_sample)


_drawn_inputs = setup_inputs


def setup_inputs(seed=0):
    import zlib

    import numpy as np

    out = dict(_drawn_inputs(seed))
    spreads = {}
    factors = {'ssm_lambda_re': 4.441, 'ssm_b_glu': 6.669, 'b_gate': 8.0, 'b_gate_up': 8.0, 'b_down': 8.0}
    for name, (base, spread) in spreads.items():
        noise = np.random.default_rng([zlib.crc32(name.encode()), seed]).standard_normal(out[name].shape)
        drawn = base * np.exp(spread * noise) if base else spread * noise
        out[name] = __import__('jax').numpy.asarray(drawn.astype(out[name].dtype))
    for name, factor in factors.items():
        out[name] = (out[name] * factor).astype(out[name].dtype)
    return out
```

```python
import math
from contextlib import ExitStack

import numpy as np

import concourse.bass as bass
from concourse import mybir

ALU = mybir.AluOpType
ACT = mybir.ActivationFunctionType
AX = mybir.AxisListType
F32 = mybir.dt.float32
I32 = mybir.dt.int32
U32 = mybir.dt.uint32
ds = bass.ds

P = 128
D = 1024
KD = D // P
SEQ = 256
NB = 8
NS = 4
NSMP = NB * NS
T = SEQ + NSMP
TILES = [(0, 128), (128, 128), (256, 32)]
PAST = 2048
PAGE = 128
NPG = PAST // PAGE
H = 4
DV = 128
HD = 64
QC = 2 * NS
G, GH, SP_ = 32, 16, 64
NJ = G * SP_ // P
NCT = 4
W5 = SEQ + NB * (NS + 1)
NE = 32
TOPK = 4
CAP = 72
GCAP = 96
GT = T // GCAP
ROWS = T
LIMIT = 7.0
ALPHA = 1.702
EPS = 1e-6
LAM_INIT = 0.8 - 0.6 * math.exp(0.0)
RND = 12582912.0
SCALE = HD ** -0.5
NEG = -1e30
NSLOT = 12

CONST_COLS = {}
_at = 0
for _name, _n in [("ident", 128), ("tri", 128), ("iota", GCAP), ("ropec", 96), ("ropes", 96), ("tau", W5), ("keep", W5),
                  ("causal", 256), ("newmask", NB * NSMP), ("ones", 128), ("tile0", GT)]:
    CONST_COLS[_name] = (_at, _n)
    _at += _n
NCONST = _at


def constants():
    c = np.zeros((P, NCONST), np.float32)

    def put(name, a):
        o, n = CONST_COLS[name]
        c[:a.shape[0], o:o + n] = a.reshape(a.shape[0], n)

    i = np.arange(P)
    put("ident", np.eye(P))
    put("tri", (i[:, None] < i[None, :]).astype(np.float32))
    put("iota", np.broadcast_to(np.arange(GCAP), (P, GCAP)))
    pos = np.concatenate([np.arange(SEQ), np.tile(PAST + np.arange(NS), NB)]).astype(np.float32)
    half = HD // 2
    inv = (np.float32(10000.0) ** (-np.arange(half, dtype=np.float32) / np.float32(half))).astype(np.float32)
    ang = (pos[:, None] * inv[None, :]).astype(np.float32)
    rc, rs = np.zeros((P, 3, half)), np.zeros((P, 3, half))
    for t, (t0, n) in enumerate(TILES):
        rc[:n, t], rs[:n, t] = np.cos(ang[t0:t0 + n].astype(np.float64)), np.sin(ang[t0:t0 + n].astype(np.float64))
    put("ropec", rc)
    put("ropes", rs)
    put("tau", np.broadcast_to(np.concatenate([np.arange(1, SEQ + 1), np.tile(np.arange(NS + 1), NB)]), (P, W5)))
    keep = np.ones(W5)
    keep[0] = 0
    keep[SEQ::NS + 1] = 0
    put("keep", np.broadcast_to(keep, (P, W5)))
    causal = np.zeros((P, 256))
    causal[:, 128:] = np.where(i[None, :] <= i[:, None], 0, NEG)
    put("causal", causal)
    key = np.arange(NSMP)
    m = np.full((NSMP, NB, H, 2, NS), NEG)
    for b in range(NB):
        for q in range(NS):
            m[(key // NS == b) & (key % NS <= q), b, :, :, q] = 0
    put("newmask", m)
    put("ones", np.ones((P, 128)))
    put("tile0", np.broadcast_to(np.arange(GT) * GCAP, (P, GT)))
    return c


RING = [(f"w_in{k}", k, 1, 1) for k in range(8)]
RING += [(f"w_gate{k}", (8 + k) % 12, 1, 1) for k in range(8)]
RING += [(f"K{s}", s, 4, NB) for s in range(4)] + [(f"V{s}", 4 + s, 4, NB) for s in range(4)]
RING += [("w_glu", 8, 1, 1), ("w_bs0", 9, 1, 1), ("w_bs1", 10, 1, 1), ("w_ba0", 11, 1, 1), ("w_ba1", 0, 1, 1)]
RING += [(f"w_out{k}", 1 + k, 1, 1) for k in range(4)]
RING += [(f"moe{c}", (5 + c) % 12, 1, NE) for c in range(12)]
SLOT, USE0, LOAD0, NDMA = {}, {}, {}, {}
_uses, _loads = [0] * NSLOT, [0] * NSLOT
for _name, _s, _d, _r in RING:
    SLOT[_name], USE0[_name], LOAD0[_name], NDMA[_name] = _s, _uses[_s], _loads[_s], _d
    _uses[_s] += _r
    _loads[_s] += 16 * _d * _r


def loaded_at(name, i=0):
    return LOAD0[name] + 16 * NDMA[name] + i * (16 * NDMA[name])


def free_at(name, i=0):
    return USE0[name] + i


def numbered(stages):
    at, out = 0, {}
    for name, n in stages:
        out[name] = at
        at += n
    return out


ACT_JOB = numbered([("u", 4), ("z0", 8)] + [q for ct in range(4) for q in (
    [(f"gate{ct}", 4)] + [(f"z{ct + 1}", 8)] * (ct < 3))] + [("wT", 8), ("glu", 4), ("end", 0)])
DVE_JOB = numbered([("hT", 5), ("vec", 1), ("prm", 1), ("x0", 1), ("qkv", 9), ("B", 8), ("C", 2), ("y", 4), ("fin", 1),
                    ("qk", 6), ("s", 8), ("oS", 1), ("oT", 3), ("bs", 8), ("ba", 8), ("out", 6), ("h2T", 5), ("lg", 3),
                    ("pos", 3), ("cnt", 1), ("bias", 2), ("end", 0)])


def build(nc, A, force_general=False):
    with ExitStack() as ctx:
        def sb(name, shape, dt=F32):
            return ctx.enter_context(nc.sbuf_tensor(name, shape, dt))

        def sem(name):
            return ctx.enter_context(nc.semaphore(name))

        psum = ctx.enter_context(nc.psum_tensor("psum", [P, 8, 512], F32))
        ring = sb("ring", [P, NSLOT, 2048])
        arena = sb("arena", [P, 25568])
        cst = sb("cst", [P, NCONST])
        ydram = nc.dram_tensor("expert_rows", (NE * ROWS, D), F32, kind="Internal").ap()

        def C(name, n=P):
            o, w = CONST_COLS[name]
            return cst[0:n, o:o + w]

        ident, ones = C("ident"), C("ones")

        def at(off, *dims, n=P):
            size = math.prod(dims)
            v = arena[0:n, off:off + size]
            if len(dims) == 1:
                return v
            names = [f"d{i}" for i in range(len(dims))]
            return v.rearrange(f"p ({' '.join(names)}) -> p {' '.join(names)}", **dict(zip(names, dims)))

        hT = at(0, KD, T)
        qz = at(0, H, 2, T)
        h2T = at(0, KD, T)
        x = at(2304, 3, D)
        qk = at(2304, 2, 3, 512)
        vt = at(5376, 3, 512)
        uT = at(6912, NCT, T)
        oth = 8064
        gates = at(oth, 16, T)
        h2 = at(oth, 3, D)
        yT = at(12672, NCT, T)
        I0 = 13824
        padr, padi = at(I0, NJ, P), at(I0 + 2048, NJ, P)
        bbT = at(I0 + 4096, 2, NJ, P)
        rows = at(oth, P)
        prm_in = at(oth + 128, 2, P, n=16)
        logdt = at(oth + 384, 4, n=16)
        pw = at(oth + 400, 12, P, n=16)
        prm = at(oth + 2000, 4, P, n=16)
        lamv = at(oth + 2512, 4, HD)
        x0rows = at(oth + 2768, 2, P)
        bin_ = at(oth + 3024, 2, NJ, GH)
        cdup = at(oth + 3536, 2, NCT, P)
        t16a = at(I0 + 8192 - 1024, NJ, GH)
        t16b = at(I0 + 8192 - 512, NJ, GH)
        normj = at(I0, D)
        K0 = I0 + 8192
        cosT, sinT, dec = at(K0, 4, W5), at(K0 + 1184, 4, W5), at(K0 + 2368, 4, W5)
        kT = at(K0, H, T)
        gvec = at(K0 + 1152, D)
        wr = at(K0 + 2176, KD, NE)
        brt = at(K0 + 2432, NE)
        subg = at(K0 + 2464, DV)
        frow = at(K0 + 2592, 4, P)
        sw = ring[:, 4:8, :].rearrange("p s n -> p (s n)")
        S5 = [sw[:, i * 1184:(i + 1) * 1184].rearrange("p (j w) -> p j w", j=4) for i in range(6)]
        zr, zi, t1, t2, t3, t4 = S5
        pS = at(I0, 2, 2, 256)
        pE = at(I0 + 1024, 2, 2, 256)
        pW = at(I0 + 2048, 2, 256)
        pWT = at(I0 + 2560, 2, 2, P)
        kt = at(I0 + 3072, 4, 512)
        s_sb = at(I0 + 5120, NPG, H * QC)
        E = at(I0 + 5632, NPG, H * QC)
        sm = I0 + 6144
        qb = at(sm, H, QC)
        sn = at(sm + 32, 32, n=32)
        mx = at(sm + 64, 32)
        mcol = at(sm + 96, 1, n=32)
        diag = at(sm + 100, 32, n=32)
        En = at(sm + 132, 32, n=32)
        Es = at(sm + 164, 32)
        rden = at(sm + 196, 32)
        on = at(sm + 228, H, 2, NS)
        oTs = at(sm + 260, H, NSMP)
        st4 = at(sm + 388, 4, 4)
        ot = at(I0 + 6656, 3, 512)
        oT = at(I0, H, T)
        mg = at(I0 + 1152, KD, T)
        tmp = at(I0 + 3456, T)
        tmp2 = at(I0 + 2560, 512)
        sg = at(I0 + 4256, NCT, T)
        R = I0 + 6500
        lg = at(R, 3, NE)
        mx8 = at(R + 96, 3, 8)
        idxf = at(R + 120, 3, 4)
        oneh = at(R + 132, 3, TOPK, NE)
        tk = at(R + 516, 3, TOPK, NE)
        mask = at(R + 900, 3, NE)
        posm = at(R + 996, 3, NE + 1)
        slotk = at(R + 1095, 3, 4)
        gk = at(R + 1107, 3, 4)
        nmx = at(R + 1119, 3, 1)
        gsum = at(R + 1122, 3, 1)
        stat = at(R + 1125, 3, 2)
        rowf = at(R + 1131, 3, 4)
        brow = at(I0, 2, 256)
        bdrow = at(I0 + 512, 2, P)
        bgT, buT, bdT = at(I0 + 768, NE * KD), at(I0 + 1024, NE * KD), at(I0 + 1280, NE * KD)
        M0 = I0 + 1536
        sel = at(M0, 3, GCAP)
        xg = at(M0 + 288, KD * GCAP)
        gg = at(M0 + 1056, KD * GCAP)
        uu = at(M0 + 1824, KD * GCAP)
        sig = at(M0 + 2592, KD * GCAP)
        aT = at(M0 + 3360, KD * GCAP)
        yS = at(M0 + 4128, KD * GCAP)
        yrow = at(oth + 3072, D)
        ycomb = ring[:, 0:6, :].rearrange("p s n -> p (s n)").rearrange("p (t k n) -> p t k n", t=3, k=4)
        junk = at(6912, D)

        eight = sb("eight", [P, 3, 8], U32)
        rowi = sb("rowi", [P, 3, 4], U32)
        cnti = sb("cnti", [P, 1], I32)
        vecT = sb("vecT", [P, 32])
        prmT = sb("prmT", [P, 4, NJ])
        x0T = sb("x0T", [P, 2, NB, NJ])
        finp = sb("finp", [P, 2, NJ])
        fins = sb("fins", [P, 2, NB, NJ])
        sc = sb("sc", [P, 16])
        halfpi = sb("halfpi", [P, 1])
        epsc = sb("epsc", [P, 1])
        pages = sb("pages", [1, NB * NPG], I32)

        loaded = [sem(f"loaded{s}") for s in range(NSLOT)]
        freed = [sem(f"freed{s}") for s in range(NSLOT)]
        s_const, s_x, s_par, s_pages = sem("consts_in"), sem("x_in"), sem("params_in"), sem("pages_in")
        s_late, s_xagain, s_bias, s_gfin = sem("late_params_in"), sem("x_again_in"), sem("biases_in"), sem("final_gain_in")
        s_kvout, s_out, s_yout = sem("kv_written"), sem("outputs_written"), sem("expert_rows_written")
        act_full, act_done = sem("act_bank_full"), sem("act_bank_emptied")
        dve_full, dve_done = sem("dve_bank_full"), sem("dve_bank_emptied")
        vs, as_, ps = sem("vector_step"), sem("scalar_step"), sem("pool_step")
        s_ssq, s_ssq2, s_gelu = sem("squares_summed"), sem("squares2_summed"), sem("gelu_done")
        s_rowf, s_hsum, s_hrms = sem("row_numbers"), sem("head_squares_summed"), sem("head_rms_ready")
        s_rows, s_ynorm, s_chain = sem("expert_rows_ready"), sem("y_normed"), sem("sample_vector_step")
        s_xn, s_dt, s_mag, s_fr, s_trig = sem("x_normed"), sem("dt_ready"), sem("decay_ready"), sem("angle_ready"), sem("trig_ready")
        s_lre = sem("decay_exponent_ready")
        s_prm, s_lamd, s_lame = sem("s5_params_ready"), sem("lambda_dots"), sem("lambda_exps")
        s_Bpad, s_angT, s_tabT, s_zfree, s_xT5, s_x5read = (sem("b_blocks_ready"), sem("table_angles"), sem("tables_ready"),
                                                            sem("z_used"), sem("states_ready"), sem("states_read"))
        s_s5, s_kvtok, s_qzero, s_fin = sem("s5_done"), sem("kv_tokens_ready"), sem("qz_zeroed"), sem("final_states_ready")
        s_nb, s_pexp, s_w, s_wt, s_pv, s_pvr = (sem("prompt_max"), sem("prompt_exps"), sem("prompt_weights"), sem("wT_read"),
                                                sem("prompt_pv"), sem("prompt_pv_read"))
        s_ktr, s_ktev, s_qb, s_sc, s_scc = (sem("k_transposed"), sem("k_emptied"), sem("q_block"), sem("scores_done"),
                                            sem("scores_copied"))
        s_mx, s_mxT, s_diag, s_mb, s_sh, s_ex, s_Es, s_den, s_dpv, s_do = (
            sem("max_by_key"), sem("max_turned"), sem("max_diagonal"), sem("max_broadcast"), sem("scores_shifted"),
            sem("sample_exps"), sem("exps_summed"), sem("denominators"), sem("sample_pv"), sem("sample_out"))
        s_ln, s_sg, s_yglu, s_mg = sem("heads_normed"), sem("glu_gate"), sem("glu_done"), sem("merged")
        s_h2, s_xres, s_gexp, s_mask, s_route = (sem("h2_ready"), sem("residual_done"), sem("gate_exps"), sem("mask_ready"),
                                                 sem("routing_ready"))
        s_nmx = sem("router_max")
        s_comb, s_gath = sem("combined"), [sem(f"rows_gathered{t}") for t in range(3)]

        def moe_sems(kind):
            names = ["sel", "gathered", "xg", "gu", "g", "sig", "act", "down", "y", "yt", "yrow", "step"]
            return {n: sem(f"{kind}_{n}") for n in names}

        fast, slow = moe_sems("fast"), moe_sems("general")

        block = ctx.enter_context(nc.Block())

        def slot(name):
            return ring[:, SLOT[name], :]

        def wait_loaded(eng, name, i=0):
            eng.wait_ge(loaded[SLOT[name]], loaded_at(name, i))

        ck = A["cache_k"][0].rearrange("n p h d -> n p (h d)")
        cv = A["cache_v"][0].rearrange("n p h d -> n p (h d)")
        wgu = A["w_gate_up"][0].rearrange("e (k p) n -> e k p n", p=P)
        wdn = A["w_down"][0].rearrange("e (c k p) n -> e c p k n", p=P, k=2)
        xp, xs = A["x_prompt"][0], A["x_sample"].rearrange("b s d -> (b s) d")
        xin = [xp[0:128, :], xp[128:256, :], xs]

        @block.sync
        def _(sp):
            def load(name, src, dst=None):
                if free_at(name):
                    sp.wait_ge(freed[SLOT[name]], free_at(name))
                sp.dma_start(slot(name) if dst is None else dst, src).then_inc(loaded[SLOT[name]], 16)

            sp.dma_start(pages[:, :], A["page_table"].rearrange("a b -> (a b)").unsqueeze(0)).then_inc(s_pages, 16)
            for k in range(8):
                load(f"w_in{k}", A["w_in"][0, k * P:(k + 1) * P, :])
            for k in range(8):
                load(f"w_gate{k}", A["w_gate"][0, k * P:(k + 1) * P, :])
            sp.wait_ge(s_pages, 16)

            def pages_of(kind, cache, b):
                for s in range(4):
                    name = f"{kind}{s}"
                    sp.wait_ge(freed[SLOT[name]], free_at(name, b))
                    for j in range(4):
                        page = sp.value_load(pages[0:1, ds(b * NPG + (4 * s + j), 1)], min_val=0, max_val=159)
                        sp.dma_start(ring[:, SLOT[name], j * 512:(j + 1) * 512],
                                     cache[ds(page, 1), :, :].rearrange("o p n -> p (o n)")).then_inc(loaded[SLOT[name]], 16)

            pages_of("K", ck, 0)
            load("w_glu", A["ssm_w_glu"][0].rearrange("(k p) n -> p k n", p=P),
                 slot("w_glu").rearrange("p (k n) -> p k n", k=4))
            for i in range(2):
                load(f"w_bs{i}", A["w_branch_ssm"][0, i * 256:(i + 1) * 256, :].rearrange("(k p) n -> p k n", p=P),
                     slot(f"w_bs{i}").rearrange("p (k n) -> p k n", k=2))
            load("w_ba0", A["w_branch_attn"][0, 0:256, :].rearrange("(k p) n -> p k n", p=P),
                 slot("w_ba0").rearrange("p (k n) -> p k n", k=2))
            sp.wait_ge(s_s5, 1)
            with sp.Fori(0, NB - 1) as b:
                pages_of("K", ck, b + 1)
                pages_of("V", cv, b)
            pages_of("V", cv, NB - 1)
            load("w_ba1", A["w_branch_attn"][0, 256:512, :].rearrange("(k p) n -> p k n", p=P),
                 slot("w_ba1").rearrange("p (k n) -> p k n", k=2))
            for i in range(4):
                load(f"w_out{i}", A["w_out"][0, i * 256:(i + 1) * 256, :].rearrange("(k p) n -> p k n", p=P),
                     slot(f"w_out{i}").rearrange("p (k n) -> p k n", k=2))

            def expert(e, waits):
                for c in range(12):
                    name = f"moe{c}"
                    if waits and c in (7, 11) and not isinstance(e, int):
                        sp.wait_ge(fast["gu" if c == 7 else "down"], e)
                    elif waits:
                        sp.wait_ge(freed[SLOT[name]], free_at(name, e))
                    if c < 8:
                        sp.dma_start(slot(name), wgu[ds(e, 1), c, :, :].rearrange("o p n -> p (o n)")
                                     ).then_inc(loaded[SLOT[name]], 16)
                    else:
                        sp.dma_start(slot(name).rearrange("p (k n) -> p k n", k=2),
                                     wdn[ds(e, 1), c - 8, :, :, :].rearrange("o p k n -> p (o k) n")
                                     ).then_inc(loaded[SLOT[name]], 16)

            expert(0, True)
            sp.wait_ge(s_route, 1)
            most = sp.value_load(cnti[0:1, 0:1], min_val=0, max_val=T)
            with sp.If(most > (-1 if force_general else CAP)):
                with sp.Fori(1, NE) as e:
                    sp.wait_ge(slow["down"], e * GT)
                    expert(e, False)
            with sp.Else():
                with sp.Fori(1, NE) as e:
                    expert(e, True)

        @block.scalar
        def _(act):
            n_step = [0]

            def step(ins):
                n_step[0] += 1
                ins.then_inc(as_, 1)
                act.wait_ge(as_, n_step[0])

            act.dma_start(cst[:, :], A["consts"]).then_inc(s_const, 16)
            for t, (t0, n) in enumerate(TILES):
                act.dma_start(x[0:n, t, :], xin[t]).then_inc(s_x, 16)
            small = [
                (rows[0:8, :], A["norm_mix_g"][0].rearrange("(r n) -> r n", n=P)),
                (rows[8:24, :], A["b_gate"][0].rearrange("(r n) -> r n", n=P)),
                (rows[24:28, :], A["ssm_b_glu"][0].rearrange("(r n) -> r n", n=P)),
                (rows[28:32, :], A["ssm_d"][0].rearrange("(r a) h -> r (a h)", r=4)),
                (prm_in[:, 0, :], A["ssm_lambda_re"][0].rearrange("(j a) p -> j (a p)", a=2)),
                (prm_in[:, 1, :], A["ssm_lambda_im"][0].rearrange("(j a) p -> j (a p)", a=2)),
                (logdt[:, 0:2], A["ssm_log_dt"][0].rearrange("(j a) -> j a", a=2)),
                (x0rows[:, 0, :], A["state_ssm_re"][0].rearrange("b (j a) p -> (b j) (a p)", a=2)),
                (x0rows[:, 1, :], A["state_ssm_im"][0].rearrange("b (j a) p -> (b j) (a p)", a=2)),
                (bin_[:, 0], A["ssm_b_re"][0].rearrange("(j a) p h -> (a p) j h", a=2)),
                (bin_[:, 1], A["ssm_b_im"][0].rearrange("(j a) p h -> (a p) j h", a=2)),
            ]
            for i, name in enumerate(["ssm_c_re", "ssm_c_im"]):
                src = A[name][0].rearrange("(c g) h p -> (g h) c p", c=NCT)
                for a in range(2):
                    small.append((cdup[:, i, :, a * 64:(a + 1) * 64], src))
            for i, name in enumerate(["lambda_q1", "lambda_k1", "lambda_q2", "lambda_k2"]):
                small.append((lamv[:, i, :], A[name][0].partition_broadcast(P)))
            for dst, src in small:
                act.dma_start(dst, src).then_inc(s_par, 16)
            n_small = len(small)
            assert n_small == 19

            act.wait_ge(s_x, 48)
            act.wait_ge(ps, 2)

            def rms(t, n, dump, done):
                step(nc.scalar.activation(dump[0:n, :], x[0:n, t, :], ACT.Square, accum_out=sc[0:n, t:t + 1]))
                nc.scalar.activation(sc[0:n, t:t + 1], sc[0:n, t:t + 1], ACT.Sqrt, scale=1.0 / D, bias=epsc[0:n, :]).then_inc(done, 1)

            for t, (t0, n) in enumerate(TILES):
                rms(t, n, normj, s_ssq)

            act.wait_ge(s_par, 16 * n_small)
            nc.scalar.activation(logdt[:, 2:4], logdt[:, 0:2], ACT.Exp).then_inc(s_dt, 1)
            act.wait_ge(s_lre, 1)
            nc.scalar.activation(prm[:, 0, :], pw[:, 1, :], ACT.Exp).then_inc(s_mag, 1)
            act.wait_ge(s_lamd, 1)
            nc.scalar.activation(sc[:, 8:10], sc[:, 6:8], ACT.Exp).then_inc(s_lame, 1)
            act.wait_ge(s_fr, 1)
            nc.scalar.activation(pw[:, 4, :], prm[:, 1, :], ACT.Sin, scale=2 * math.pi * (1 - 2e-7))
            step(nc.scalar.activation(pw[:, 5, :], prm[:, 1, :], ACT.Abs))
            nc.scalar.activation(pw[:, 6, :], pw[:, 5, :], ACT.Sin, bias=halfpi[0:16, :], scale=-2 * math.pi * (1 - 2e-7)
                                 ).then_inc(s_trig, 1)

            def job(i):
                act.wait_ge(act_full, i + 1)
                return psum[:, i % 4, :]

            def tables(ct):
                act.wait_ge(s_angT, ct + 1)
                nc.scalar.activation(sinT[:, :, :], cosT[:, :, :], ACT.Sin, scale=2 * math.pi * (1 - 2e-7))
                step(nc.scalar.activation(cosT[:, :, :], cosT[:, :, :], ACT.Abs))
                nc.scalar.activation(cosT[:, :, :], cosT[:, :, :], ACT.Sin, bias=halfpi[:, :],
                                     scale=-2 * math.pi * (1 - 2e-7)).then_inc(s_tabT, 1)

            for i in range(4):
                nc.scalar.activation(uT[:, i, :], job(ACT_JOB["u"] + i)[:, 0:T], ACT.Copy).then_inc(act_done, 1)
            act.wait_ge(s_prm, 1)

            def inputs(ct):
                if ct:
                    act.wait_ge(s_zfree, ct)
                for jj in range(4):
                    for c, z in enumerate((zr, zi)):
                        pz = job(ACT_JOB[f"z{ct}"] + 2 * jj + c)
                        nc.scalar.activation(z[:, jj, 0:SEQ], pz[:, 0:SEQ], ACT.Copy)
                        nc.scalar.activation(z[:, jj, SEQ:W5].rearrange("p (b s) -> p b s", s=NS + 1)[:, :, 1:],
                                             pz[:, SEQ:T].rearrange("p (b s) -> p b s", s=NS), ACT.Copy).then_inc(act_done, 1)

            tables(0)
            inputs(0)
            for ct in range(NCT):
                for i in range(4 * ct, 4 * ct + 4):
                    nc.scalar.activation(gates[:, i, :], job(ACT_JOB[f"gate{ct}"] + i % 4)[:, 0:T], ACT.Sigmoid,
                                         bias=vecT[:, 8 + i:9 + i]).then_inc(act_done, 1)
                if ct + 1 < NCT:
                    inputs(ct + 1)
                    tables(ct + 1)

            act.wait_ge(s_kvtok, 1)
            kvo = [(A["o_k_prompt"], A["o_k_sample"], qk[:, 1]), (A["o_v_prompt"], A["o_v_sample"], vt)]
            for o_p, o_s, src in kvo:
                op = o_p[0, 0].rearrange("s h d -> s (h d)")
                for t in range(2):
                    act.dma_start(op[t * 128:(t + 1) * 128, :], src[:, t, :]).then_inc(s_kvout, 16)
                act.dma_start(o_s[0].rearrange("b s h d -> (b s) (h d)"), src[0:NSMP, 2, :]).then_inc(s_kvout, 16)
            act.wait_ge(s_fin, 1)
            for c, (o_p, o_s) in enumerate([(A["o_re_prompt"], A["o_re_sample"]), (A["o_im_prompt"], A["o_im_sample"])]):
                act.dma_start(o_p[0, 0].rearrange("(j a) p -> j (a p)", a=2), frow[0:NJ, c, :]).then_inc(s_out, 16)
                act.dma_start(o_s[0].rearrange("b (j a) p -> (b j) (a p)", a=2), frow[:, 2 + c, :]).then_inc(s_out, 16)
            act.wait_ge(s_s5, 1)
            late = [(gvec, A["norm_ffn_g"][0].partition_broadcast(P)),
                    (wr, A["w_router"][0].rearrange("(k p) n -> p k n", p=P)),
                    (brt, A["b_router"][0].partition_broadcast(P)),
                    (subg, A["attn_subln_g"][0].partition_broadcast(P))]
            for dst, src in late:
                act.dma_start(dst, src).then_inc(s_late, 16)

            nc.scalar.activation(yT[:, :, :], yT[:, :, :], ACT.Gelu_apprx_tanh).then_inc(s_gelu, 1)

            def p_exp(n):
                act.wait_ge(s_nb, n + 1)
                w = 128 * (n // 4 + 1)
                for c in range(2):
                    ins = nc.scalar.activation(pE[:, n % 2, c, 0:w], pS[:, n % 2, c, 0:w], ACT.Exp, scale=SCALE,
                                               bias=st4[:, n % 2, c:c + 1], accum_out=st4[:, n % 2, 2 + c:3 + c])
                step(ins)
                nc.scalar.activation(sc[:, 14:15], C("ones")[:, 0:1], ACT.Copy).then_inc(s_pexp, 1)

            p_exp(0)
            for n in range(8):
                if n + 1 < 8:
                    p_exp(n + 1)
                w = 128 * (n // 4 + 1)
                nc.scalar.activation(pWT[:, n % 2, 0:w // 128, :],
                                     job(ACT_JOB["wT"] + n)[:, 0:w].rearrange("p (k q) -> p k q", q=P),
                                     ACT.Copy).then_inc(act_done, 1)

            def keys(i, lo, hi):
                for pg in range(lo, hi):
                    act.wait_ge(s_ktr, i * NPG + (pg + 1))
                    nc.scalar.activation(kt[:, pg % 4, :], psum[:, pg % 4, :], ACT.Copy).then_inc(s_ktev, 1)

            def exps(i):
                act.wait_ge(s_sh, i + 1)
                nc.scalar.activation(En[:, :], sn[:, :], ACT.Exp, scale=SCALE)
                nc.scalar.activation(E[:, :, :], s_sb[:, :, :], ACT.Exp, scale=SCALE).then_inc(s_ex, 1)

            def head_rms(t, n):
                act.wait_ge(s_hsum, t + 1)
                nc.scalar.activation(st4[0:n, 2, :], st4[0:n, 0, :], ACT.Sqrt, scale=1.0 / DV, bias=epsc[0:n, :]).then_inc(s_hrms, 1)

            for t in range(2):
                head_rms(t, 128)
            keys(0, 0, NPG)
            with act.Fori(1, NB) as i:
                keys(i, 0, 9)
                exps(i - 1)
                keys(i, 9, NPG)
            exps(NB - 1)
            head_rms(2, NSMP)

            act.wait_ge(s_kvout, 96)
            act.wait_ge(dve_done, DVE_JOB["s"])
            for t, (t0, n) in enumerate(TILES):
                act.dma_start(x[0:n, t, :], xin[t]).then_inc(s_xagain, 16)
            for i in range(4):
                nc.scalar.activation(sg[:, i, :], job(ACT_JOB["glu"] + i)[:, 0:T], ACT.Sigmoid,
                                     bias=vecT[:, 24 + i:25 + i]).then_inc(act_done, 1)

            for t, (t0, n) in enumerate(TILES):
                act.wait_ge(s_xres, t + 1)
                rms(t, n, junk, s_ssq2)
            act.wait_ge(dve_done, DVE_JOB["h2T"])
            bgu = A["b_gate_up"][0].rearrange("(t e) (k m) -> t (e k) m", t=2, m=256)
            bdn = A["b_down"][0].rearrange("(t e) (k m) -> t (e k) m", t=2, m=128)
            for t in range(2):
                act.dma_start(brow[:, t, :], bgu[t]).then_inc(s_bias, 16)
                act.dma_start(bdrow[:, t, :], bdn[t]).then_inc(s_bias, 16)
            act.wait_ge(s_h2, 3)
            act.dma_start(gvec, A["norm_final_g"].partition_broadcast(P)).then_inc(s_gfin, 16)
            for t, (t0, n) in enumerate(TILES):
                act.wait_ge(s_nmx, t + 1)
                step(nc.scalar.activation(gk[0:n, t, :], mx8[0:n, t, 0:TOPK], ACT.Exp, bias=nmx[0:n, t, :],
                                          accum_out=gsum[0:n, t, :]))
                nc.scalar.activation(sc[:, 14:15], C("ones")[:, 0:1], ACT.Copy).then_inc(s_gexp, 1)

            def xg_empty(m, g, cap):
                act.wait_ge(m["gathered"], g)
                nc.scalar.activation(xg[:, 0:KD * cap].rearrange("p (b r) -> p b r", b=2), psum[:, 0:2, 0:4 * cap],
                                     ACT.Copy).then_inc(m["xg"], 1)

            def sigm(m, it, cap):
                act.wait_ge(m["g"], it + 1)
                nc.scalar.activation(sig[:, 0:KD * cap], gg[:, 0:KD * cap], ACT.Sigmoid, scale=ALPHA).then_inc(m["sig"], 1)

            def rows_out(m, it, cap, row0):
                act.wait_ge(s_yout, it * 16)
                act.wait_ge(m["yt"], it + 1)
                nc.scalar.activation(yrow[0:cap, :].rearrange("r (b n) -> r b n", b=2), psum[0:cap, 0:2, :], ACT.Copy).then_inc(m["yrow"], 1)
                act.wait_ge(m["yrow"], it + 1)
                act.dma_start(ydram[ds(row0, cap), :], yrow[0:cap, :]).then_inc(s_yout, 16)

            act.wait_ge(s_route, 1)
            most = act.value_load(cnti[0:1, 0:1], min_val=0, max_val=T)
            with act.If(most > (-1 if force_general else CAP)):
                with act.Fori(0, NE) as e:
                    with act.Fori(0, GT) as t:
                        it = act.snap(e * GT + t)
                        xg_empty(slow, it + 1, GCAP)
                        sigm(slow, it, GCAP)
                        rows_out(slow, it, GCAP, it * GCAP)
                act.wait_ge(s_yout, 16 * NE * GT)
            with act.Else():
                xg_empty(fast, 1, CAP)
                with act.Fori(0, NE) as e:
                    sigm(fast, e, CAP)
                    xg_empty(fast, e + 2, CAP)
                    rows_out(fast, e, CAP, e * CAP)
                act.wait_ge(s_yout, 16 * NE)
            nc.scalar.activation(sc[:, 13:14], C("ones")[:, 0:1], ACT.Copy).then_inc(s_rows, 1)
            for t, (t0, n) in enumerate(TILES):
                act.wait_ge(s_comb, t + 1)
                rms(t, n, junk, s_ssq2)
            outs = [A["o_y_prompt"][0, 0:128, :], A["o_y_prompt"][0, 128:256, :], A["o_y_sample"].rearrange("b s d -> (b s) d")]
            for t, (t0, n) in enumerate(TILES):
                act.wait_ge(s_ynorm, t + 1)
                act.dma_start(outs[t], x[0:n, t, :]).then_inc(s_out, 16)
            act.wait_ge(s_kvout, 96)
            act.wait_ge(s_out, 16 * 7)

        @block.gpsimd
        def _(pool):
            pool.memset(halfpi[:, :], math.pi / 2).then_inc(ps, 1)
            pool.memset(epsc[:, :], EPS).then_inc(ps, 1)

            def gather(table):
                for t, (t0, n) in enumerate(TILES):
                    for k in range(TOPK):
                        pool.indirect_dma_start(ycomb[0:n, t, k, :], None, table,
                                                bass.IndirectOffsetOnAxis(rowi[0:n, t, k:k + 1], 0),
                                                bounds_check=table.shape[0] - 1).then_inc(s_gath[t], 16)

            pool.wait_ge(s_rows, 1)
            most = pool.value_load(cnti[0:1, 0:1], min_val=0, max_val=T)
            with pool.If(most > (-1 if force_general else CAP)):
                gather(ydram)
            with pool.Else():
                gather(ydram[0:NE * CAP, :])

        @block.tensor
        def _(pe):
            na, nd = [0], [0]

            def abank():
                i = na[0]
                na[0] += 1
                if i >= 4:
                    pe.wait_ge(act_done, i - 3)
                return psum[:, i % 4, :]

            def dbank():
                i = nd[0]
                nd[0] += 1
                if i >= 3:
                    pe.wait_ge(dve_done, i - 2)
                return psum[:, 4 + i % 3, :]

            def mm(out, a, b, start, stop):
                return nc.tensor.matmul(out, lhsT=a, rhs=b, start=start, stop=stop, skip_group_check=True)

            def tr(out, in_, n=P):
                return nc.tensor.transpose(out, in_, ident[0:n, 0:n])

            pe.wait_ge(s_const, 16)
            for t, (t0, n) in enumerate(TILES):
                pe.wait_ge(s_xn, t + 1)
                for half in range(2 if n == 128 else 1):
                    b = dbank()
                    ks = range(4 * half, 4 * half + 4) if n == 128 else range(8)
                    for i, k in enumerate(ks):
                        last = tr(b[:, i * n:(i + 1) * n], x[0:n, t, k * P:(k + 1) * P], n)
                    last.then_inc(dve_full, 1)
            pe.wait_ge(s_par, 16 * 19)
            tr(dbank()[:, 0:32], rows[0:32, :], 32).then_inc(dve_full, 1)
            pe.wait_ge(s_prm, 1)
            b = dbank()
            for i in range(4):
                last = tr(b[:, i * 16:(i + 1) * 16], prm[:, i, :], 16)
            last.then_inc(dve_full, 1)
            b = dbank()
            for i in range(2):
                last = tr(b[:, i * P:(i + 1) * P], x0rows[:, i, :])
            last.then_inc(dve_full, 1)
            pe.wait_ge(dve_done, DVE_JOB["prm"])
            for k in range(8):
                wait_loaded(pe, f"w_in{k}")
            for i in range(4):
                b = abank()
                for k in range(KD):
                    last = mm(b[:, 0:T], slot(f"w_in{k}")[:, i * P:(i + 1) * P], hT[:, k, :], k == 0, k == KD - 1)
                last.then_inc(act_full, 1)
            for t, (t0, n) in enumerate(TILES):
                for c in range(3):
                    b = dbank()
                    for k in range(KD):
                        last = mm(b[0:n, :], hT[:, k, t0:t0 + n], slot(f"w_in{k}")[:, 512 * (c + 1):512 * (c + 2)],
                                  k == 0, k == KD - 1)
                        if t == 2 and c == 2 and k < KD - 1:
                            last.then_inc(freed[SLOT[f"w_in{k}"]], 1)
                    last.then_inc(dve_full, 1)
            pe.wait_ge(dve_full, nd[0])
            pe.sem_inc(freed[SLOT["w_in7"]], 1)
            for c in range(2):
                for q in range(4):
                    b = dbank()
                    pe.wait_ge(s_Bpad, 1)
                    for i in range(4):
                        last = tr(b[:, i * P:(i + 1) * P], (padr, padi)[c][:, 4 * q + i, :])
                    last.then_inc(dve_full, 1)
            for c in range(2):
                b = dbank()
                for i in range(4):
                    last = tr(b[:, i * P:(i + 1) * P], cdup[:, c, i, :])
                last.then_inc(dve_full, 1)
            pe.wait_ge(act_done, ACT_JOB["z0"])
            pe.wait_ge(dve_done, DVE_JOB["C"])

            def s5_in(ct):
                for j in range(4 * ct, 4 * ct + 4):
                    for c in range(2):
                        mm(abank()[:, 0:T], bbT[:, c, j, :], uT[:, ct, :], True, True).then_inc(act_full, 1)

            def s5_out(ct):
                b = dbank()
                pe.wait_ge(s_xT5, ct + 1)
                for jj in range(4):
                    j = 4 * ct + jj
                    mm(b[:, 0:W5], padr[:, j, :], t1[:, jj, :], jj == 0, False)
                    last = mm(b[:, 0:W5], padi[:, j, :], t3[:, jj, :], False, jj == 3)
                last.then_inc(dve_full, 1)

            s5_in(0)
            for k in range(8):
                wait_loaded(pe, f"w_gate{k}")
            for i in range(16):
                b = abank()
                for k in range(KD):
                    last = mm(b[:, 0:T], slot(f"w_gate{k}")[:, i * P:(i + 1) * P], hT[:, k, :], k == 0, k == KD - 1)
                    if i == 15 and k < KD - 1:
                        last.then_inc(freed[SLOT[f"w_gate{k}"]], 1)
                last.then_inc(act_full, 1)
                if i % 4 == 3:
                    ct = i // 4
                    if ct + 1 < NCT:
                        s5_in(ct + 1)
                    if ct + 1 == NCT:
                        n_gate = na[0]
                    s5_out(ct)
            pe.wait_ge(act_full, n_gate)
            pe.sem_inc(freed[SLOT["w_gate7"]], 1)
            pe.wait_ge(dve_done, DVE_JOB["fin"])
            b = dbank()
            for c in range(2):
                tr(b[0:NJ, c * P:(c + 1) * P], finp[:, c, :])
            for c in range(2):
                last = tr(b[:, (2 + c) * P:(3 + c) * P], fins[:, c].rearrange("p b j -> p (b j)"))
            last.then_inc(dve_full, 1)
            for t, (t0, n) in enumerate(TILES):
                for c in range(2):
                    b = dbank()
                    for h in range(H):
                        last = tr(b[:, h * n:(h + 1) * n], qk[0:n, c, t, h * P:(h + 1) * P], n)
                    last.then_inc(dve_full, 1)

            def p_scores(n):
                i, h = divmod(n, 4)
                b = dbank()
                w = 128 * (i + 1)
                for c in range(2):
                    last = mm(b[:, c * w:(c + 1) * w], qz[:, h, c, i * P:(i + 1) * P], kT[:, h, 0:w], True, True)
                last.then_inc(dve_full, 1)

            pe.wait_ge(dve_done, DVE_JOB["s"])
            p_scores(0)
            p_scores(1)
            for n in range(8):
                i, h = divmod(n, 4)
                if n + 2 < 8:
                    p_scores(n + 2)
                b = abank()
                pe.wait_ge(s_w, n + 1)
                for k in range(i + 1):
                    last = tr(b[:, k * P:(k + 1) * P], pW[:, n % 2, k * P:(k + 1) * P])
                last.then_inc(act_full, 1)
                pe.wait_ge(act_done, ACT_JOB["wT"] + n + 1)
                if n == 4:
                    pe.wait_ge(s_pvr, 1)
                for k in range(i + 1):
                    last = mm(psum[:, 7, h * P:(h + 1) * P], pWT[:, n % 2, k, :], vt[:, k, h * P:(h + 1) * P], k == 0, k == i)
                last.then_inc(s_pv, 1)

            def keys_turn(i, pg):
                if pg % 4 == 0:
                    pe.wait_ge(loaded[SLOT[f"K{pg // 4}"]], loaded_at(f"K{pg // 4}", i))
                for h in range(H):
                    last = tr(psum[:, pg % 4, h * P:(h + 1) * P], ring[:, SLOT[f"K{pg // 4}"], (pg % 4) * 512 + h * P:(pg % 4) * 512 + (h + 1) * P])
                last.then_inc(s_ktr, 1)

            def scores(i, pg):
                if pg == 0:
                    pe.wait_ge(s_qb, i + 1)
                pe.wait_ge(s_ktev, i * NPG + (pg + 1))
                for h in range(H):
                    last = mm(psum[:, 4, pg * 32 + h * QC:pg * 32 + (h + 1) * QC], kt[:, pg % 4, h * P:(h + 1) * P], qb[:, h, :], True, True)
                if pg % 4 == 3:
                    last.then_inc(freed[SLOT[f"K{pg // 4}"]], 1)

            def new_scores():
                for h in range(H):
                    last = mm(psum[0:NSMP, 5, h * QC:(h + 1) * QC], kT[:, h, SEQ:T], qb[:, h, :], True, True)
                last.then_inc(s_sc, 1)

            def max_turn(j):
                pe.wait_ge(s_do, j)
                pe.wait_ge(s_mx, j + 1)
                tr(psum[0:32, 6, 0:128], mx[:, :])
                tr(psum[0:32, 6, 128:160], sn[:, :], 32).then_inc(s_mxT, 1)

            def max_bcast(j):
                pe.wait_ge(s_diag, j + 1)
                mm(psum[:, 6, 160:192], ones[0:32, :], diag[:, :], True, True).then_inc(s_mb, 1)

            def denominators(j):
                pe.wait_ge(s_Es, j + 1)
                mm(psum[:, 6, 192:224], ones[:, :], Es[:, :], True, False)
                mm(psum[:, 6, 192:224], ones[0:32, :], En[:, :], False, True).then_inc(s_den, 1)

            def values(j):
                for pg in range(NPG):
                    if pg % 4 == 0:
                        pe.wait_ge(loaded[SLOT[f"V{pg // 4}"]], loaded_at(f"V{pg // 4}", j))
                    for h in range(H):
                        last = mm(psum[:, 7, h * QC:(h + 1) * QC], ring[:, SLOT[f"V{pg // 4}"], (pg % 4) * 512 + h * P:(pg % 4) * 512 + (h + 1) * P],
                                  E[:, pg, h * QC:(h + 1) * QC], pg == 0 and h == 0, False)
                    if pg % 4 == 3:
                        last.then_inc(freed[SLOT[f"V{pg // 4}"]], 1)
                for h in range(H):
                    last = mm(psum[:, 7, h * QC:(h + 1) * QC], vt[0:NSMP, 2, h * P:(h + 1) * P], En[:, h * QC:(h + 1) * QC], False, True)
                last.then_inc(s_dpv, 1)

            def batch(i, j):
                for pg in range(NPG + 1):
                    if pg < NPG:
                        if j is not None or pg >= 4:
                            pe.wait_ge(s_ktev, i * NPG + (pg - 3))
                        keys_turn(i, pg)
                    if pg:
                        scores(i, pg - 1)
                    if j is not None and pg == 2:
                        max_turn(j)
                    if j is not None and pg == 5:
                        max_bcast(j)
                    if j is not None and pg == 13:
                        denominators(j)
                new_scores()
                if j is not None:
                    pe.wait_ge(s_do, j)
                    values(j)

            pe.wait_ge(s_pvr, 2)
            pe.wait_ge(act_done, ACT_JOB["glu"])
            pe.wait_ge(dve_done, DVE_JOB["oS"])
            batch(0, None)
            with pe.Fori(1, NB) as i:
                batch(i, i - 1)
            max_turn(NB - 1)
            max_bcast(NB - 1)
            denominators(NB - 1)
            pe.wait_ge(s_do, NB - 1)
            values(NB - 1)

            pe.wait_ge(s_do, NB)
            b = dbank()
            for h in range(H):
                last = tr(b[0:NSMP, h * P:(h + 1) * P], oTs[:, h, :])
            last.then_inc(dve_full, 1)
            wait_loaded(pe, "w_glu")
            pe.wait_ge(s_gelu, 1)
            for i in range(4):
                b = abank()
                for k in range(4):
                    last = mm(b[:, 0:T], slot("w_glu")[:, k * 512 + i * P:k * 512 + (i + 1) * P], yT[:, k, :], k == 0, k == 3)
                last.then_inc(act_full, 1)
            for t, (t0, n) in enumerate(TILES):
                pe.wait_ge(s_ln, t + 1)
                b = dbank()
                for h in range(H):
                    last = tr(b[:, h * n:(h + 1) * n], ot[0:n, t, h * P:(h + 1) * P], n)
                last.then_inc(dve_full, 1)
            for name, src, ready in (("w_bs", yT, 1), ("w_ba", oT, None)):
                wait_loaded(pe, name + "0")
                wait_loaded(pe, name + "1")
                if ready:
                    pe.wait_ge(s_yglu, ready)
                else:
                    pe.wait_ge(dve_done, DVE_JOB["bs"])
                for i in range(KD):
                    b = dbank()
                    for k in range(4):
                        last = mm(b[:, 0:T], slot(f"{name}{k // 2}")[:, (k % 2) * D + i * P:(k % 2) * D + (i + 1) * P],
                                  src[:, k, :], k == 0, k == 3)
                    last.then_inc(dve_full, 1)
            pe.wait_ge(s_mg, 1)
            pe.sem_inc(freed[SLOT["w_glu"]], 1)
            for name in ("w_bs0", "w_bs1", "w_ba0", "w_ba1"):
                pe.sem_inc(freed[SLOT[name]], 1)
            for i in range(4):
                wait_loaded(pe, f"w_out{i}")
            for t, (t0, n) in enumerate(TILES):
                for half in range(2):
                    b = dbank()
                    for k in range(KD):
                        last = mm(b[0:n, :], mg[:, k, t0:t0 + n],
                                  slot(f"w_out{k // 2}")[:, (k % 2) * D + half * 512:(k % 2) * D + (half + 1) * 512],
                                  k == 0, k == KD - 1)
                    last.then_inc(dve_full, 1)
            pe.wait_ge(dve_done, DVE_JOB["h2T"])
            for i in range(4):
                pe.sem_inc(freed[SLOT[f"w_out{i}"]], 1)
            for t, (t0, n) in enumerate(TILES):
                pe.wait_ge(s_h2, t + 1)
                for half in range(2 if n == 128 else 1):
                    b = dbank()
                    ks = range(4 * half, 4 * half + 4) if n == 128 else range(8)
                    for i, k in enumerate(ks):
                        last = tr(b[:, i * n:(i + 1) * n], h2[0:n, t, k * P:(k + 1) * P], n)
                    last.then_inc(dve_full, 1)
            pe.wait_ge(s_late, 64)
            pe.wait_ge(dve_done, DVE_JOB["lg"])
            for t, (t0, n) in enumerate(TILES):
                b = dbank()
                for k in range(KD):
                    last = mm(b[0:n, 0:NE], h2T[:, k, t0:t0 + n], wr[:, k, :], k == 0, k == KD - 1)
                last.then_inc(dve_full, 1)
            for t, (t0, n) in enumerate(TILES):
                b = dbank()
                pe.wait_ge(s_mask, 3)
                for s in range(t):
                    mm(b[0:n, 0:NE], ones[:, 0:n], mask[:, s, :], s == 0, False)
                mm(b[0:n, 0:NE], C("tri", n)[:, 0:n], mask[0:n, t, :], t == 0, True).then_inc(dve_full, 1)
            b = dbank()
            for t, (t0, n) in enumerate(TILES):
                last = mm(b[:, 0:NE], ones[0:n, :], mask[0:n, t, :], t == 0, t == 2)
            last.then_inc(dve_full, 1)
            pe.wait_ge(s_bias, 64)
            b = dbank()
            for half in range(2):
                for t in range(2):
                    last = tr(b[:, (2 * half + t) * P:(2 * half + t + 1) * P], brow[:, t, half::2])
            last.then_inc(dve_full, 1)
            b = dbank()
            for t in range(2):
                last = tr(b[:, t * P:(t + 1) * P], bdrow[:, t, :])
            last.then_inc(dve_full, 1)

            def part(bank, i, cap):
                return psum[:, bank + i // 4, (i % 4) * cap:(i % 4 + 1) * cap]

            def gather(m, g, cap, turned):
                if turned is not None:
                    pe.wait_ge(m["yrow"], turned)
                pe.wait_ge(m["sel"], g)
                for k in range(KD):
                    for t, (t0, n) in enumerate(TILES):
                        last = mm(part(0, k, cap), h2[0:n, t, k * P:(k + 1) * P], sel[0:n, t, 0:cap], t == 0, t == 2)
                last.then_inc(m["gathered"], 1)

            def gate_up(m, it, e, cap, frees):
                pe.wait_ge(m["xg"], it + 1)
                for c in range(KD):
                    name = f"moe{c}"
                    wait_loaded(pe, name, e)
                    for half in range(2):
                        for i in range(KD):
                            last = mm(part(2 + 2 * half, i, cap), slot(name)[:, 256 * i + half:256 * (i + 1):2],
                                      xg[:, c * cap:(c + 1) * cap], c == 0 and i % 4 == 0, c == KD - 1)
                    if c < KD - 1 and frees:
                        last.then_inc(freed[SLOT[name]], 1)
                last.then_inc(m["gu"], 1)

            def down(m, it, e, cap, frees):
                pe.wait_ge(m["act"], it + 1)
                for c in range(4):
                    name = f"moe{8 + c}"
                    wait_loaded(pe, name, e)
                    for kk in range(2):
                        for i in range(KD):
                            last = mm(part(6, i, cap), slot(name)[:, kk * D + i * P:kk * D + (i + 1) * P],
                                      aT[:, (2 * c + kk) * cap:(2 * c + kk + 1) * cap], c == 0 and kk == 0 and i % 4 == 0,
                                      c == 3 and kk == 1)
                    if c < 3 and frees:
                        last.then_inc(freed[SLOT[name]], 1)
                last.then_inc(m["down"], 1)

            def turn_rows(m, it, cap, ahead):
                pe.wait_ge(m["xg"], it + 1 + ahead)
                pe.wait_ge(m["y"], it + 1)
                for i in range(KD):
                    last = tr(psum[0:cap, i // 4, (i % 4) * P:(i % 4 + 1) * P], yS[:, i * cap:(i + 1) * cap])
                last.then_inc(m["yt"], 1)

            pe.wait_ge(act_done, ACT_JOB["end"])
            pe.wait_ge(dve_done, DVE_JOB["end"])
            pe.wait_ge(s_route, 1)
            most = pe.value_load(cnti[0:1, 0:1], min_val=0, max_val=T)
            with pe.If(most > (-1 if force_general else CAP)):
                with pe.Fori(0, NE) as e:
                    with pe.Fori(0, GT) as t:
                        it = pe.snap(e * GT + t)
                        gather(slow, it + 1, GCAP, it)
                        gate_up(slow, it, e, GCAP, False)
                        down(slow, it, e, GCAP, False)
                        turn_rows(slow, it, GCAP, 0)
            with pe.Else():
                gather(fast, 1, CAP, None)
                with pe.Fori(0, NE) as e:
                    gate_up(fast, e, e, CAP, True)
                    gather(fast, e + 2, CAP, e)
                    down(fast, e, e, CAP, True)
                    turn_rows(fast, e, CAP, 1)

        @block.vector
        def _(v):
            n_step, n_bank = [0], [0]

            def step(ins):
                n_step[0] += 1
                ins.then_inc(vs, 1)
                v.wait_ge(vs, n_step[0])

            def job(stage, i):
                assert DVE_JOB[stage] + i == n_bank[0], (stage, i, n_bank[0])
                v.wait_ge(dve_full, n_bank[0] + 1)
                b = psum[:, 4 + n_bank[0] % 3, :]
                n_bank[0] += 1
                return b

            TT, TS, STT, CP = nc.vector.tensor_tensor, nc.vector.tensor_scalar, nc.vector.scalar_tensor_tensor, nc.vector.tensor_copy

            def bc(ap, axis, shape):
                return ap.unsqueeze(axis).to_broadcast(shape)

            def inverse(out, in_):
                step(nc.vector.reciprocal(out, in_))

            v.wait_ge(s_const, 16)
            for t, (t0, n) in enumerate(TILES):
                v.wait_ge(s_ssq, t + 1)
                inverse(sc[0:n, 3 + t:4 + t], sc[0:n, t:t + 1])
                TS(x[0:n, t, :], x[0:n, t, :], sc[0:n, 3 + t:4 + t], None, ALU.mult).then_inc(s_xn, 1)

            lr_, li_ = prm_in[:, 0, :], prm_in[:, 1, :]
            v.wait_ge(s_dt, 1)
            step(CP(pw[:, 0, :].rearrange("p (a q) -> p a q", a=2), bc(logdt[:, 2:4], 2, [16, 2, 64])))
            TT(pw[:, 1, :], lr_, pw[:, 0, :], ALU.mult).then_inc(s_lre, 1)
            step(STT(pw[:, 2, :], li_, 1.0 / (2 * math.pi), pw[:, 0, :], ALU.mult, ALU.mult))
            step(TS(pw[:, 3, :], pw[:, 2, :], RND, RND, ALU.add, ALU.subtract))
            TT(prm[:, 1, :], pw[:, 2, :], pw[:, 3, :], ALU.subtract).then_inc(s_fr, 1)
            lw = pw[:, 7:9, :]
            v.wait_ge(s_par, 16 * 19)
            step(TT(lamv[:, 0:3:2, :], lamv[:, 0:3:2, :], lamv[:, 1:4:2, :], ALU.mult))
            nc.vector.tensor_reduce(sc[:, 6:8], lamv[:, 0:3:2, :], AX.X, ALU.add).then_inc(s_lamd, 1)
            v.wait_ge(s_lame, 1)
            step(TT(sc[:, 10:11], sc[:, 8:9], sc[:, 9:10], ALU.subtract))
            step(TS(sc[:, 11:12], sc[:, 10:11], LAM_INIT, -1.0, ALU.add, ALU.mult))
            v.wait_ge(s_mag, 1)
            v.wait_ge(s_trig, 1)
            mag, sin1, cos1 = prm[:, 0, :], pw[:, 4, :], pw[:, 6, :]
            are, aim, t7, t8, den = pw[:, 7, :], pw[:, 8, :], pw[:, 9, :], pw[:, 10, :], pw[:, 11, :]
            step(TT(are, mag, cos1, ALU.mult))
            step(TS(are, are, -1.0, None, ALU.add))
            step(TT(aim, mag, sin1, ALU.mult))
            step(TT(t7, lr_, lr_, ALU.mult))
            step(TT(t8, li_, li_, ALU.mult))
            step(TT(t7, t7, t8, ALU.add))
            step(nc.vector.reciprocal(den, t7))
            step(TT(t7, are, lr_, ALU.mult))
            step(TT(t8, aim, li_, ALU.mult))
            step(TT(t7, t7, t8, ALU.add))
            step(TT(prm[:, 2, :], t7, den, ALU.mult))
            step(TT(t7, aim, lr_, ALU.mult))
            step(TT(t8, are, li_, ALU.mult))
            step(TT(t7, t7, t8, ALU.subtract))
            TT(prm[:, 3, :], t7, den, ALU.mult).then_inc(s_prm, 1)

            at_h = 0
            for t, (t0, n) in enumerate(TILES):
                for half in range(2 if n == 128 else 1):
                    b = job("hT", at_h)
                    kk = 4 if n == 128 else 8
                    CP(hT[:, 4 * half:4 * half + kk, t0:t0 + n], b[:, 0:kk * n].rearrange("p (k q) -> p k q", k=kk)
                       ).then_inc(dve_done, 1)
                    at_h += 1
            b = job("vec", 0)
            v.wait_ge(dve_done, 5)
            step(CP(vecT[:, :], b[:, 0:32]))
            TT(hT[:, :, :], hT[:, :, :], bc(vecT[:, 0:8], 2, [P, KD, T]), ALU.mult).then_inc(dve_done, 1)
            b = job("prm", 0)
            step(CP(prmT[:, :, :], b[:, 0:64].rearrange("p (i j) -> p i j", i=4)))
            v.sem_inc(dve_done, 1)
            b = job("x0", 0)
            CP(x0T[:, :, :, :].rearrange("p c b j -> p c (b j)"), b[:, 0:256].rearrange("p (c r) -> p c r", c=2)).then_inc(dve_done, 1)

            step(nc.vector.memset(at(I0, 4096), 0.0))
            fre, fim = bc(prmT[:, 2, :], 2, [P, NJ, GH]), bc(prmT[:, 3, :], 2, [P, NJ, GH])
            for c, (pad, ta, tb, op) in enumerate([(padr, 0, 1, ALU.subtract), (padi, 1, 0, ALU.add)]):
                step(TT(t16a, bin_[:, ta], fre, ALU.mult))
                step(TT(t16b, bin_[:, tb], fim, ALU.mult))
                pv = pad[:, :, :].rearrange("p (c j) q -> p c j q", c=NCT)
                ta4, tb4 = (q.rearrange("p (c j) h -> p c j h", c=NCT) for q in (t16a, t16b))
                for a in range(2):
                    for j in range(4):
                        o = (2 * j + a) * GH
                        pr = slice(64 * a, 64 * a + 64)
                        ins = TT(pv[pr, :, j, o:o + GH], ta4[pr, :, j, :], tb4[pr, :, j, :], op)
                step(ins)
            v.sem_inc(s_Bpad, 1)

            qt = at(I0 + 4096, 4, 256)
            for t, (t0, n) in enumerate(TILES):
                cs, sn_ = (C(q, n)[:, t * 32:(t + 1) * 32].unsqueeze(1).to_broadcast([n, 8, 32]) for q in ("ropec", "ropes"))
                for c in range(3):
                    b = job("qkv", 3 * t + c)
                    if c == 2:
                        CP(vt[0:n, t, :], b[0:n, :]).then_inc(dve_done, 1)
                        continue
                    pv = b[0:n, :].rearrange("p (g w i) -> p g w i", w=2, i=32)
                    qv = qk[0:n, c, t, :].rearrange("p (g w i) -> p g w i", w=2, i=32)
                    ta, tb, tc, td = (qt[0:n, i, :].rearrange("p (g i) -> p g i", i=32) for i in range(4))
                    TT(ta, pv[:, :, 0, :], cs, ALU.mult)
                    TT(tb, pv[:, :, 1, :], sn_, ALU.mult)
                    TT(tc, pv[:, :, 1, :], cs, ALU.mult)
                    step(TT(td, pv[:, :, 0, :], sn_, ALU.mult))
                    TT(qv[:, :, 0, :], ta, tb, ALU.subtract)
                    step(TT(qv[:, :, 1, :], tc, td, ALU.add))
                    v.sem_inc(dve_done, 1)
            v.wait_ge(vs, n_step[0])
            v.sem_inc(s_kvtok, 1)

            for i in range(8):
                b = job("B", i)
                CP(bbT[:, i // 4, 4 * (i % 4):4 * (i % 4) + 4, :], b.rearrange("p (j q) -> p j q", j=4)).then_inc(dve_done, 1)
            for c in range(2):
                b = job("C", c).rearrange("p (c q) -> p c q", c=NCT)
                pv = (padr, padi)[c][:, :, :].rearrange("p (c j) q -> p c j q", c=NCT)
                for a in range(2):
                    for j in range(4):
                        o = (2 * j + a) * GH
                        pr = slice(64 * a, 64 * a + 64)
                        ins = TS(pv[pr, :, j, o:o + GH], b[pr, :, o:o + GH], 1.0 if c == 0 else -1.0, None, ALU.mult)
                ins.then_inc(dve_done, 1)

            v.wait_ge(act_done, ACT_JOB["z0"])
            for k in range(8):
                v.wait_ge(freed[k], 1)
            for ct in range(NCT):
                J = slice(4 * ct, 4 * ct + 4)
                tau = C("tau").unsqueeze(1).to_broadcast([P, 4, W5])
                fr = bc(prmT[:, 1, J], 2, [P, 4, W5])
                step(TT(t2, tau, fr, ALU.mult))
                step(TS(t4, t2, RND, RND, ALU.add, ALU.subtract))
                TT(cosT, t2, t4, ALU.subtract).then_inc(s_angT, 1)
                TT(dec, C("keep").unsqueeze(1).to_broadcast([P, 4, W5]), bc(prmT[:, 0, J], 2, [P, 4, W5]), ALU.mult)
                for c, z in enumerate((zr, zi)):
                    ins = CP(z[:, :, SEQ:W5].rearrange("p j (b s) -> p j b s", s=NS + 1)[:, :, :, 0],
                             x0T[:, c, :, J].rearrange("p b j -> p j b"))
                step(ins)
                v.wait_ge(s_tabT, ct + 1)
                v.wait_ge(act_done, ACT_JOB[f"z{ct}"] + 8)
                if ct:
                    v.wait_ge(dve_full, DVE_JOB["y"] + ct)
                TT(t1, cosT, zr, ALU.mult)
                TT(t2, sinT, zi, ALU.mult)
                TT(t3, cosT, zi, ALU.mult)
                step(TT(t4, sinT, zr, ALU.mult))
                TT(t1, t1, t2, ALU.add)
                step(TT(t3, t3, t4, ALU.subtract))

                def flat(a):
                    return a.rearrange("p j w -> p (j w)")
                nc.vector.tensor_tensor_scan(flat(zr), flat(dec), flat(t1), 0.0, ALU.mult, ALU.add)
                step(nc.vector.tensor_tensor_scan(flat(zi), flat(dec), flat(t3), 0.0, ALU.mult, ALU.add))
                TT(t1, cosT, zr, ALU.mult)
                TT(t2, sinT, zi, ALU.mult)
                TT(t3, cosT, zi, ALU.mult)
                step(TT(t4, sinT, zr, ALU.mult))
                v.sem_inc(s_zfree, 1)
                TT(t1, t1, t2, ALU.subtract)
                step(TT(t3, t3, t4, ALU.add))
                v.sem_inc(s_xT5, 1)
                for c, q in enumerate((t1, t3)):
                    CP(finp[:, c, J], q[:, :, SEQ - 1])
                    ins = CP(fins[:, c, :, J].rearrange("p b j -> p j b"),
                             q[:, :, SEQ:W5].rearrange("p j (b s) -> p j b s", s=NS + 1)[:, :, :, NS])
                step(ins)
                b = job("y", ct)
                d = vecT[:, 28 + ct:29 + ct]
                STT(yT[:, ct, 0:SEQ], uT[:, ct, 0:SEQ], d, b[:, 0:SEQ], ALU.mult, ALU.add)
                step(STT(yT[:, ct, SEQ:T].rearrange("p (b s) -> p b s", s=NS), uT[:, ct, SEQ:T].rearrange("p (b s) -> p b s", s=NS),
                         d, b[:, SEQ:W5].rearrange("p (b s) -> p b s", s=NS + 1)[:, :, 1:], ALU.mult, ALU.add))
                v.sem_inc(dve_done, 1)
            v.sem_inc(s_s5, 1)
            b = job("fin", 0)
            CP(frow[0:NJ, 0:2, :], b[0:NJ, 0:256].rearrange("p (c q) -> p c q", c=2))
            step(CP(frow[:, 2:4, :], b[:, 256:512].rearrange("p (c q) -> p c q", c=2)))
            v.sem_inc(s_fin, 1)
            v.sem_inc(dve_done, 1)

            v.wait_ge(act_full, ACT_JOB["wT"])
            step(nc.vector.memset(qz, 0.0))
            for t, (t0, n) in enumerate(TILES):
                b = job("qk", 2 * t)[:, 0:H * n].rearrange("p (h q) -> p h q", h=H)
                CP(qz[0:64, :, 0, t0:t0 + n], b[0:64])
                CP(qz[64:128, :, 1, t0:t0 + n], b[64:128]).then_inc(dve_done, 1)
                b = job("qk", 2 * t + 1)[:, 0:H * n].rearrange("p (h q) -> p h q", h=H)
                CP(kT[:, :, t0:t0 + n], b).then_inc(dve_done, 1)

            def p_first(n):
                w = 128 * (n // 4 + 1)
                b = job("s", n)[:, 0:2 * w].rearrange("p (c k) -> p c k", c=2)
                m = C("causal")[:, 256 - w:256].unsqueeze(1).to_broadcast([P, 2, w])
                step(TT(pS[:, n % 2, :, 0:w], b, m, ALU.add))
                v.sem_inc(dve_done, 1)
                step(nc.vector.tensor_reduce(st4[:, n % 2, 0:2], pS[:, n % 2, :, 0:w], AX.X, ALU.max))
                step(TS(st4[:, n % 2, 0:2], st4[:, n % 2, 0:2], -SCALE, None, ALU.mult))
                v.sem_inc(s_nb, 1)

            def p_second(n):
                w = 128 * (n // 4 + 1)
                v.wait_ge(s_pexp, n + 1)
                if n >= 2:
                    v.wait_ge(act_full, ACT_JOB["wT"] + n - 1)
                r = st4[:, 2 + n % 2, 0:2]
                step(nc.vector.reciprocal(r, st4[:, n % 2, 2:4]))
                step(TT(r[:, 1:2], r[:, 1:2], sc[:, 11:12], ALU.mult))
                step(TS(pW[:, n % 2, 0:w], pE[:, n % 2, 0, 0:w], r[:, 0:1], None, ALU.mult))
                STT(pW[:, n % 2, 0:w], pE[:, n % 2, 1, 0:w], r[:, 1:2], pW[:, n % 2, 0:w], ALU.mult, ALU.add).then_inc(s_w, 1)

            p_first(0)
            for n in range(8):
                if n + 1 < 8:
                    p_first(n + 1)
                p_second(n)
                if n in (4, 7):
                    i = n // 5
                    v.wait_ge(s_pv, 4 * (i + 1))
                    CP(ot[:, i, :], psum[:, 7, :]).then_inc(s_pvr, 1)
            v.wait_ge(s_late, 64)
            step(TS(subg, subg, 1.0 - LAM_INIT, None, ALU.mult))

            def head_norm(t, n):
                o = ot[0:n, t, :].rearrange("p (h d) -> p h d", h=H)
                sq = tmp2[0:n, :].rearrange("p (h d) -> p h d", h=H)
                step(TT(sq, o, o, ALU.mult))
                nc.vector.tensor_reduce(st4[0:n, 0, :], sq, AX.X, ALU.add).then_inc(s_hsum, 1)
                v.wait_ge(s_hrms, t + 1)
                inverse(st4[0:n, 1, :], st4[0:n, 2, :])
                step(TT(o, o, bc(st4[0:n, 1, :], 2, [n, H, DV]), ALU.mult))
                TT(o, o, subg[0:n, :].unsqueeze(1).to_broadcast([n, H, DV]), ALU.mult).then_inc(s_ln, 1)

            v.wait_ge(s_pvr, 2)
            STEPS = 6

            def cstep(ins, base, k):
                ins.then_inc(s_chain, 1)
                v.wait_ge(s_chain, base + (k + 1))

            def q_block(i):
                if not isinstance(i, int):
                    v.wait_ge(s_sc, i)
                CP(qb[:, :, :].rearrange("p h (c s) -> p h c s", c=2), qz[:, :, :, ds(i * NS + SEQ, NS)]).then_inc(s_qb, 1)

            def copy_max(i, base, k):
                v.wait_ge(s_sc, i + 1)
                cstep(CP(s_sb.rearrange("p g c -> p (g c)"), psum[:, 4, :]), base, k)
                cstep(TT(sn[:, :], psum[0:NSMP, 5, 0:32], C("newmask", NSMP)[:, ds(i * 32, 32)], ALU.add), base, k + 1)
                nc.vector.tensor_reduce(mx[:, :], s_sb.rearrange("p g c -> p c g"), AX.X, ALU.max).then_inc(s_mx, 1)

            def softmax(j, base, k):
                v.wait_ge(s_mxT, j + 1)
                cstep(nc.vector.tensor_reduce(mcol, psum[0:32, 6, 0:160], AX.X, ALU.max), base, k)
                TS(diag, ident[0:32, 0:32], mcol[:, 0:1], None, ALU.mult).then_inc(s_diag, 1)
                v.wait_ge(s_mb, j + 1)
                TT(s_sb, s_sb, psum[:, 6, 160:192].unsqueeze(1).to_broadcast([P, NPG, 32]), ALU.subtract)
                cstep(TT(sn[:, :], sn[:, :], psum[0:32, 6, 160:192], ALU.subtract), base, k + 1)
                v.sem_inc(s_sh, 1)
                v.wait_ge(s_ex, j + 1)
                nc.vector.tensor_reduce(Es, E.rearrange("p g c -> p c g"), AX.X, ALU.add).then_inc(s_Es, 1)

            def finish(j, base, k):
                v.wait_ge(s_den, j + 1)
                cstep(nc.vector.reciprocal(rden, psum[:, 6, 192:224]), base, k)
                v.wait_ge(s_dpv, j + 1)
                cstep(TT(on.rearrange("p h c s -> p (h c s)"), psum[:, 7, 0:32], rden, ALU.mult), base, k + 1)
                STT(oTs[:, :, ds(j * NS, NS)], on[:, :, 1, :], sc[:, 11:12], on[:, :, 0, :], ALU.mult, ALU.add).then_inc(s_do, 1)

            for t in range(2):
                head_norm(t, 128)
            q_block(0)
            copy_max(0, 0, 0)
            with v.Fori(1, NB) as i:
                base = (i - 1) * STEPS + 2
                q_block(i)
                softmax(i - 1, base, 0)
                copy_max(i, base, 2)
                finish(i - 1, base, 4)
            softmax(NB - 1, 2 + (NB - 1) * STEPS, 0)
            finish(NB - 1, 2 + (NB - 1) * STEPS, 2)

            step(CP(ot[0:NSMP, 2, :], job("oS", 0)[0:NSMP, :]))
            v.sem_inc(dve_done, 1)
            head_norm(2, NSMP)
            for t, (t0, n) in enumerate(TILES):
                CP(oT[:, :, t0:t0 + n], job("oT", t)[:, 0:H * n].rearrange("p (h q) -> p h q", h=H)).then_inc(dve_done, 1)
            v.wait_ge(act_done, ACT_JOB["glu"] + 4)
            TT(yT, yT, sg, ALU.mult).then_inc(s_yglu, 1)
            for i in range(KD):
                TT(mg[:, i, :], gates[:, i, :], job("bs", i)[:, 0:T], ALU.mult).then_inc(dve_done, 1)
            for i in range(KD):
                step(TT(tmp, gates[:, KD + i, :], job("ba", i)[:, 0:T], ALU.mult))
                v.sem_inc(dve_done, 1)
                step(TT(mg[:, i, :], mg[:, i, :], tmp, ALU.add))
            v.sem_inc(s_mg, 1)
            v.wait_ge(s_xagain, 48)
            for t, (t0, n) in enumerate(TILES):
                for half in range(2):
                    xx = x[0:n, t, half * 512:(half + 1) * 512]
                    step(TT(xx, xx, job("out", 2 * t + half)[0:n, :], ALU.add))
                    v.sem_inc(dve_done, 1)
                v.sem_inc(s_xres, 1)
            for t, (t0, n) in enumerate(TILES):
                v.wait_ge(s_ssq2, t + 1)
                inverse(sc[0:n, 3:4], sc[0:n, t:t + 1])
                step(STT(h2[0:n, t, :], x[0:n, t, :], sc[0:n, 3:4], gvec[0:n, :], ALU.mult, ALU.mult))
                v.sem_inc(s_h2, 1)
            at_h = 0
            for t, (t0, n) in enumerate(TILES):
                for half in range(2 if n == 128 else 1):
                    kk = 4 if n == 128 else 8
                    CP(h2T[:, 4 * half:4 * half + kk, t0:t0 + n],
                       job("h2T", at_h)[:, 0:kk * n].rearrange("p (k q) -> p k q", k=kk)).then_inc(dve_done, 1)
                    at_h += 1
            for t, (t0, n) in enumerate(TILES):
                step(TT(lg[0:n, t, :], job("lg", t)[0:n, 0:NE], brt[0:n, :], ALU.add))
                v.sem_inc(dve_done, 1)
                step(nc.vector.max(mx8[0:n, t, :], lg[0:n, t, :]))
                step(nc.vector.max_index(eight[0:n, t, :], mx8[0:n, t, :], lg[0:n, t, :]))
                TS(nmx[0:n, t, :], mx8[0:n, t, 0:1], -1.0, None, ALU.mult).then_inc(s_nmx, 1)
                step(CP(idxf[0:n, t, :], eight[0:n, t, 0:TOPK]))
                step(TT(oneh[0:n, t], C("iota", n)[:, 0:NE].unsqueeze(1).to_broadcast([n, TOPK, NE]),
                        bc(idxf[0:n, t, :], 2, [n, TOPK, NE]), ALU.is_equal))
                step(nc.vector.tensor_reduce(mask[0:n, t, :], oneh[0:n, t].rearrange("p k e -> p e k"), AX.X, ALU.add))
                v.sem_inc(s_mask, 1)
            for t, (t0, n) in enumerate(TILES):
                v.wait_ge(s_gexp, t + 1)
                step(nc.vector.reciprocal(gsum[0:n, t, :], gsum[0:n, t, :]))
                TS(gk[0:n, t, :], gk[0:n, t, :], gsum[0:n, t, :], None, ALU.mult)
            for t, (t0, n) in enumerate(TILES):
                b = job("pos", t)[0:n, 0:NE]
                step(STT(posm[0:n, t, 0:NE], b, 1.0, mask[0:n, t, :], ALU.add, ALU.mult))
                TS(posm[0:n, t, 0:NE], posm[0:n, t, 0:NE], -1.0, None, ALU.add)
                nc.vector.memset(posm[0:n, t, NE:NE + 1], -1.0)
                step(TT(tk[0:n, t], oneh[0:n, t], b.unsqueeze(1).to_broadcast([n, TOPK, NE]), ALU.mult))
                v.sem_inc(dve_done, 1)
                step(nc.vector.tensor_reduce(slotk[0:n, t, :], tk[0:n, t], AX.X, ALU.add))
            step(nc.vector.tensor_reduce(sc[:, 12:13], job("cnt", 0)[:, 0:NE], AX.X, ALU.max))
            v.sem_inc(dve_done, 1)
            step(CP(cnti[:, :], sc[:, 12:13]))
            b = job("bias", 0)
            CP(bgT, b[:, 0:256])
            CP(buT, b[:, 256:512]).then_inc(dve_done, 1)
            step(CP(bdT, job("bias", 1)[:, 0:256]))
            v.sem_inc(dve_done, 1)
            v.sem_inc(s_route, 1)

            def select(m, g, e, t, cap):
                v.wait_ge(m["gathered"], g)
                for s, (t0, n) in enumerate(TILES):
                    if t is None:
                        ins = TS(sel[0:n, s, 0:cap], C("iota", n)[:, 0:cap], posm[0:n, s, ds(e, 1)], None, ALU.is_equal)
                    else:
                        ins = TS(sel[0:n, s, 0:cap], C("iota", n)[:, 0:cap], C("tile0", n)[:, ds(t, 1)],
                                 posm[0:n, s, ds(e, 1)], ALU.add, ALU.is_equal)
                ins.then_inc(m["sel"], 1)

            def swiglu(m, it, e, cap):
                def mstep(ins, k):
                    ins.then_inc(m["step"], 1)
                    v.wait_ge(m["step"], it * 4 + (k + 1))

                def bias(a):
                    return a.rearrange("p (n b k) -> p n b k", b=2, k=4)[:, ds(e, 1), :, :].rearrange(
                        "p o b k -> p (o b) k").unsqueeze(3).to_broadcast([P, 2, 4, cap])

                def by_k(a):
                    return a[:, 0:KD * cap].rearrange("p (b k c) -> p b k c", b=2, k=4)

                def banks(b):
                    return psum[:, b:b + 2, 0:4 * cap].rearrange("p b (k c) -> p b k c", k=4)

                g, u, s_ = gg[:, 0:KD * cap], uu[:, 0:KD * cap], sig[:, 0:KD * cap]
                v.wait_ge(m["gu"], it + 1)
                mstep(TT(by_k(gg), banks(2), bias(bgT), ALU.add), 0)
                TS(g, g, LIMIT, None, ALU.min).then_inc(m["g"], 1)
                mstep(TT(by_k(uu), banks(4), bias(buT), ALU.add), 1)
                mstep(TS(u, u, LIMIT, -LIMIT, ALU.min, ALU.max), 2)
                v.wait_ge(m["sig"], it + 1)
                mstep(TT(g, g, s_, ALU.mult), 3)
                STT(aT[:, 0:KD * cap], u, 1.0, g, ALU.add, ALU.mult).then_inc(m["act"], 1)
                v.wait_ge(m["down"], it + 1)
                TT(by_k(yS), banks(6), bias(bdT), ALU.add).then_inc(m["y"], 1)

            def rows_of(stride):
                for t, (t0, n) in enumerate(TILES):
                    STT(rowf[0:n, t, :], idxf[0:n, t, :], float(stride), slotk[0:n, t, :], ALU.mult, ALU.add).then_inc(s_rowf, 1)
                v.wait_ge(s_rowf, 3)
                for t, (t0, n) in enumerate(TILES):
                    CP(rowi[0:n, t, :], rowf[0:n, t, :])

            most = v.value_load(cnti[0:1, 0:1], min_val=0, max_val=T)
            with v.If(most > (-1 if force_general else CAP)):
                rows_of(ROWS)
                with v.Fori(0, NE) as e:
                    with v.Fori(0, GT) as t:
                        it = v.snap(e * GT + t)
                        select(slow, it, e, t, GCAP)
                        swiglu(slow, it, e, GCAP)
            with v.Else():
                select(fast, 0, 0, None, CAP)
                rows_of(CAP)
                with v.Fori(0, NE) as e:
                    select(fast, e + 1, e + 1, None, CAP)
                    swiglu(fast, e, e, CAP)

            for t, (t0, n) in enumerate(TILES):
                v.wait_ge(s_gath[t], 16 * TOPK)
                for k in range(TOPK):
                    step(STT(x[0:n, t, :], ycomb[0:n, t, k, :], gk[0:n, t, k:k + 1], x[0:n, t, :], ALU.mult, ALU.add))
                v.sem_inc(s_comb, 1)
            v.wait_ge(s_gfin, 16)
            for t, (t0, n) in enumerate(TILES):
                v.wait_ge(s_ssq2, 3 + t + 1)
                inverse(sc[0:n, 3:4], sc[0:n, t:t + 1])
                step(STT(x[0:n, t, :], x[0:n, t, :], sc[0:n, 3:4], gvec[0:n, :], ALU.mult, ALU.mult))
                v.sem_inc(s_ynorm, 1)


_UNUSED = ()
_OUTS = [
    ("o_y_prompt", (1, SEQ, D)), ("o_y_sample", (NB, NS, D)),
    ("o_k_prompt", (1, 1, SEQ, H, DV)), ("o_v_prompt", (1, 1, SEQ, H, DV)),
    ("o_re_prompt", (1, 1, G, SP_)), ("o_im_prompt", (1, 1, G, SP_)),
    ("o_k_sample", (1, NB, NS, H, DV)), ("o_v_sample", (1, NB, NS, H, DV)),
    ("o_re_sample", (1, NB, G, SP_)), ("o_im_sample", (1, NB, G, SP_)),
]


def kernel(**inputs):
    import concourse.bacc as bacc
    from concourse.bass_utils import run_bass_kernel_spmd as run

    nc = bacc.Bacc("TRN2", target_bir_lowering=False, num_devices=1)
    arrays, A = {}, {}
    for name, a in {**inputs, "consts": constants()}.items():
        arrays[f"in_{name}"] = a = np.ascontiguousarray(a)
        A[name] = nc.dram_tensor(f"in_{name}", a.shape, mybir.dt.from_np(a.dtype), kind="ExternalInput").ap()
    for name, shape in _OUTS:
        A[name] = nc.dram_tensor(name, shape, F32, kind="ExternalOutput").ap()
    build(nc, A)
    r = run(nc, [arrays], core_ids=[0])
    return tuple(r.results[0][name] for name, _ in _OUTS)
```

```python
import math
from contextlib import ExitStack

import numpy as np

import concourse.bass as bass
from concourse import mybir

ALU = mybir.AluOpType
ACT = mybir.ActivationFunctionType
AX = mybir.AxisListType
F32 = mybir.dt.float32
I32 = mybir.dt.int32
U32 = mybir.dt.uint32
ds = bass.ds

P = 128
D = 1024
KD = D // P
SEQ = 256
NB = 8
NS = 4
NSMP = NB * NS
T = SEQ + NSMP
TILES = [(0, 128), (128, 128), (256, 32)]
PAST = 2048
PAGE = 128
NPG = PAST // PAGE
H = 4
DV = 128
HD = 64
QC = 2 * NS
G, GH, SP_ = 32, 16, 64
NJ = G * SP_ // P
NCT = 4
W5 = SEQ + NB * (NS + 1)
NE = 32
TOPK = 4
CAP = 64
NOVER = 17
NJOB = NE + NOVER
LIMIT = 7.0
ALPHA = 1.702
EPS = 1e-6
LAM_INIT = 0.8 - 0.6 * math.exp(0.0)
RND = 12582912.0
SCALE = HD ** -0.5
NEG = -1e30
NSLOT = 12

CONST_COLS = {}
_at = 0
for _name, _n in [("ident", 128), ("tri", 128), ("iota", CAP), ("ropec", 96), ("ropes", 96), ("tau", W5), ("keep", W5),
                  ("causal", 256), ("newmask", NB * NSMP), ("ones", 128), ("tile0", 5), ("expert", NE + 1),
                  ("upper", P), ("jobs", NOVER)]:
    CONST_COLS[_name] = (_at, _n)
    _at += _n
NCONST = _at


def constants():
    c = np.zeros((P, NCONST), np.float32)

    def put(name, a):
        o, n = CONST_COLS[name]
        c[:a.shape[0], o:o + n] = a.reshape(a.shape[0], n)

    i = np.arange(P)
    put("ident", np.eye(P))
    put("tri", (i[:, None] < i[None, :]).astype(np.float32))
    put("iota", np.broadcast_to(np.arange(CAP), (P, CAP)))
    pos = np.concatenate([np.arange(SEQ), np.tile(PAST + np.arange(NS), NB)]).astype(np.float32)
    half = HD // 2
    inv = (np.float32(10000.0) ** (-np.arange(half, dtype=np.float32) / np.float32(half))).astype(np.float32)
    ang = (pos[:, None] * inv[None, :]).astype(np.float32)
    rc, rs = np.zeros((P, 3, half)), np.zeros((P, 3, half))
    for t, (t0, n) in enumerate(TILES):
        rc[:n, t], rs[:n, t] = np.cos(ang[t0:t0 + n].astype(np.float64)), np.sin(ang[t0:t0 + n].astype(np.float64))
    put("ropec", rc)
    put("ropes", rs)
    put("tau", np.broadcast_to(np.concatenate([np.arange(1, SEQ + 1), np.tile(np.arange(NS + 1), NB)]), (P, W5)))
    keep = np.ones(W5)
    keep[0] = 0
    keep[SEQ::NS + 1] = 0
    put("keep", np.broadcast_to(keep, (P, W5)))
    causal = np.zeros((P, 256))
    causal[:, 128:] = np.where(i[None, :] <= i[:, None], 0, NEG)
    put("causal", causal)
    key = np.arange(NSMP)
    m = np.full((NSMP, NB, H, 2, NS), NEG)
    for b in range(NB):
        for q in range(NS):
            m[(key // NS == b) & (key % NS <= q), b, :, :, q] = 0
    put("newmask", m)
    put("ones", np.ones((P, 128)))
    put("tile0", np.broadcast_to(np.arange(5) * CAP, (P, 5)))
    put("expert", (np.arange(64)[:, None] % NE == np.arange(NE + 1)[None, :]).astype(np.float32))
    put("upper", np.broadcast_to((i < CAP).astype(np.float32), (64, P)))
    put("jobs", np.broadcast_to(np.arange(NOVER), (P, NOVER)))
    return c


RING = [(f"w_in{k}", k, 1, 1) for k in range(8)]
RING += [(f"w_gate{k}", (8 + k) % 12, 1, 1) for k in range(8)]
RING += [(f"K{s}", s, 4, NB) for s in range(4)] + [(f"V{s}", 4 + s, 4, NB) for s in range(4)]
RING += [("w_glu", 8, 1, 1), ("w_bs0", 9, 1, 1), ("w_bs1", 10, 1, 1), ("w_ba0", 11, 1, 1), ("w_ba1", 0, 1, 1)]
RING += [(f"w_out{k}", 1 + k, 1, 1) for k in range(4)]
SLOT, USE0, LOAD0, NDMA = {}, {}, {}, {}
_uses, _loads = [0] * NSLOT, [0] * NSLOT
for _name, _s, _d, _r in RING:
    SLOT[_name], USE0[_name], LOAD0[_name], NDMA[_name] = _s, _uses[_s], _loads[_s], _d
    _uses[_s] += _r
    _loads[_s] += 16 * _d * _r


NRAW, NSPLIT = 6, 3
RAW0 = NSLOT - NRAW
POOL_CHUNKS = (3, 6, 11)


def chunk_raw(i):
    return RAW0 + i % NRAW


def chunk_loaded(q, i):
    return (q * 2 + (i // NRAW - (i % NRAW < 4))) * 16 + (_loads[chunk_raw(i)] + 16)


def chunk_used(q, i):
    return q * 12 + (i - 3)


def chunk_low(q, i):
    pool = i in POOL_CHUNKS
    mine = [k for k in range(12) if (k in POOL_CHUNKS) == pool]
    return pool, q * len(mine) + (mine.index(i) + 1 - sum(k < 4 for k in mine))


def loaded_at(name, i=0):
    return LOAD0[name] + 16 * NDMA[name] + i * (16 * NDMA[name])


def free_at(name, i=0):
    return USE0[name] + i


def numbered(stages):
    at, out = 0, {}
    for name, n in stages:
        out[name] = at
        at += n
    return out


ACT_JOB = numbered([("u", 4), ("z0", 8)] + [q for ct in range(4) for q in (
    [(f"gate{ct}", 4)] + [(f"z{ct + 1}", 8)] * (ct < 3))] + [("wT", 8), ("glu", 4), ("end", 0)])
DVE_JOB = numbered([("hT", 5), ("vec", 1), ("prm", 1), ("x0", 1), ("qkv", 9), ("B", 8), ("C", 2), ("y", 4), ("fin", 1),
                    ("qk", 6), ("s", 8), ("oS", 1), ("oT", 3), ("bs", 8), ("ba", 8), ("out", 6), ("h2T", 5), ("lg", 3),
                    ("pos", 3), ("cnt", 1), ("end", 0)])


def build(nc, A):
    with ExitStack() as ctx:
        def sb(name, shape, dt=F32):
            return ctx.enter_context(nc.sbuf_tensor(name, shape, dt))

        def sem(name):
            return ctx.enter_context(nc.semaphore(name))

        psum = ctx.enter_context(nc.psum_tensor("psum", [P, 8, 512], F32))
        def base():
            return (nc.sbuf_base + 31) // 32 * 32

        ring_at = base()
        ring = sb("ring", [P, NSLOT, 2048])
        arena_at = base()
        arena = sb("arena", [P, 25568])

        def rounded(name, byte, shape):
            return nc.alloc_sbuf_tensor_at(name, shape, mybir.dt.float32r, offset=byte)

        cst = sb("cst", [P, NCONST])
        ydram = nc.dram_tensor("expert_rows", (NJOB * CAP, D), F32, kind="Internal").ap()

        def C(name, n=P):
            o, w = CONST_COLS[name]
            return cst[0:n, o:o + w]

        ident, ones = C("ident"), C("ones")

        def at(off, *dims, n=P):
            size = math.prod(dims)
            v = arena[0:n, off:off + size]
            if len(dims) == 1:
                return v
            names = [f"d{i}" for i in range(len(dims))]
            return v.rearrange(f"p ({' '.join(names)}) -> p {' '.join(names)}", **dict(zip(names, dims)))

        hT = at(0, KD, T)
        qz = at(0, H, 2, T)
        h2T = at(0, KD, T)
        x = at(2304, 3, D)
        qk = at(2304, 2, 3, 512)
        vt = at(5376, 3, 512)
        uT = at(6912, NCT, T)
        oth = 8064
        gates = at(oth, 16, T)
        h2 = at(oth, 3, D)
        yT = at(12672, NCT, T)
        I0 = 13824
        padr, padi = at(I0, NJ, P), at(I0 + 2048, NJ, P)
        bbT = at(I0 + 4096, 2, NJ, P)
        rows = at(oth, P)
        prm_in = at(oth + 128, 2, P, n=16)
        logdt = at(oth + 384, 4, n=16)
        pw = at(oth + 400, 12, P, n=16)
        prm = at(oth + 2000, 4, P, n=16)
        lamv = at(oth + 2512, 4, HD)
        x0rows = at(oth + 2768, 2, P)
        bin_ = at(oth + 3024, 2, NJ, GH)
        cdup = at(oth + 3536, 2, NCT, P)
        t16a = at(I0 + 8192 - 1024, NJ, GH)
        t16b = at(I0 + 8192 - 512, NJ, GH)
        normj = at(I0, D)
        K0 = I0 + 8192
        cosT, sinT, dec = at(K0, 4, W5), at(K0 + 1184, 4, W5), at(K0 + 2368, 4, W5)
        kT = at(K0, H, T)
        gvec = at(K0 + 1152, D)
        wr = at(K0 + 2176, KD, NE)
        brt = at(K0 + 2432, NE)
        subg = at(K0 + 2464, DV)
        frow = at(K0 + 2592, 4, P)
        sw = ring[:, 4:8, :].rearrange("p s n -> p (s n)")
        S5 = [sw[:, i * 1184:(i + 1) * 1184].rearrange("p (j w) -> p j w", j=4) for i in range(6)]
        zr, zi, t1, t2, t3, t4 = S5
        pS = at(I0, 2, 2, 256)
        pE = at(I0 + 1024, 2, 2, 256)
        pW = at(I0 + 2048, 2, 256)
        pWT = at(I0 + 2560, 2, 2, P)
        kt = at(I0 + 3072, 4, 512)
        s_sb = at(I0 + 5120, NPG, H * QC)
        E = at(I0 + 5632, NPG, H * QC)
        sm = I0 + 6144
        qb = at(sm, H, QC)
        sn = at(sm + 32, 32, n=32)
        mx = at(sm + 64, 32)
        mcol = at(sm + 96, 1, n=32)
        diag = at(sm + 100, 32, n=32)
        En = at(sm + 132, 32, n=32)
        Es = at(sm + 164, 32)
        rden = at(sm + 196, 32)
        on = at(sm + 228, H, 2, NS)
        oTs = at(sm + 260, H, NSMP)
        st4 = at(sm + 388, 4, 4)
        ot = at(I0 + 6656, 3, 512)
        oT = at(I0, H, T)
        mg = at(I0 + 1152, KD, T)
        tmp = at(I0 + 3456, T)
        tmp2 = at(I0 + 2560, 512)
        sg = at(I0 + 4256, NCT, T)
        R = I0 + 6144
        lg = at(R, 3, NE)
        mx8 = at(R + 96, 3, 8)
        idxf = at(R + 120, 3, 4)
        oneh = at(R + 132, 3, TOPK, NE)
        tk = at(R + 516, 3, TOPK, NE)
        mask = at(R + 900, 3, NE)
        posm = at(R + 996, 3, NE + 2)
        slotk = at(R + 1098, 3, 4)
        gk = at(R + 1110, 3, 4)
        nmx = at(R + 1122, 3, 1)
        gsum = at(R + 1125, 3, 1)
        rowf = at(R + 1128, 3, 4)
        big = at(R + 1140, 3, 4)
        basek = at(R + 1152, 3, 4)
        cnt = at(R + 1164, 6, NE)
        ytab = at(5376, NOVER, NE)
        whi = rounded("w_high", ring_at, [P, NSPLIT, 2048])
        wlo = rounded("w_low", ring_at + NSPLIT * 8192, [P, NSPLIT, 2048])
        xs_ = rounded("x_split", arena_at, [P, KD, 2 * CAP])
        as2 = rounded("act_split", arena_at + 4 * 1024, [P, KD, 2 * CAP])
        sel = rounded("selection", arena_at + 4 * 2048, [P, 3, CAP])
        bias_s = rounded("bias_split", arena_at + 4 * 5376, [64, 3 * D])
        bsg = rounded("bias_of_gate_up", arena_at + 4 * 13568, [64, P])
        bsd = rounded("bias_of_down", arena_at + 4 * 13696, [64, P])
        h2s = rounded("h2_split", arena_at + 4 * I0, [P, 2, 3, D])
        braw = at(8448, 3 * D, n=64)
        guL = at(8448, 2 * D, n=CAP)
        sig = at(8448, D, n=CAP)
        xa = at(8448 + D, D)
        gus = at(10496, 2 * D, n=CAP)
        yL = at(10496, D, n=CAP)
        gg = at(12544, D, n=CAP)
        uu = at(K0 + 2176, D, n=CAP)
        yS = arena[CAP:P, 10496:10496 + D]
        zeros = yT.rearrange("p c t -> p (c t)")[0:64, 0:D]
        ycomb = ring[:, 0:6, :].rearrange("p s n -> p (s n)").rearrange("p (t k n) -> p t k n", t=3, k=4)
        junk = at(6912, D)

        eight = sb("eight", [P, 3, 8], U32)
        rowi = sb("rowi", [P, 3, 4], U32)
        jobi = sb("jobi", [P, 2 * NOVER + 1], I32)
        jobf = sb("jobf", [P, 2 * NOVER + 1])
        vecT = sb("vecT", [P, 32])
        prmT = sb("prmT", [P, 4, NJ])
        x0T = sb("x0T", [P, 2, NB, NJ])
        finp = sb("finp", [P, 2, NJ])
        fins = sb("fins", [P, 2, NB, NJ])
        sc = sb("sc", [P, 16])
        halfpi = sb("halfpi", [P, 1])
        epsc = sb("epsc", [P, 1])
        pages = sb("pages", [1, NB * NPG], I32)

        loaded = [sem(f"loaded{s}") for s in range(NSLOT)]
        freed = [sem(f"freed{s}") for s in range(NSLOT)]
        s_const, s_x, s_par, s_pages = sem("consts_in"), sem("x_in"), sem("params_in"), sem("pages_in")
        s_late, s_xagain, s_bias, s_gfin = sem("late_params_in"), sem("x_again_in"), sem("biases_in"), sem("final_gain_in")
        s_kvout, s_out, s_yout = sem("kv_written"), sem("outputs_written"), sem("expert_rows_written")
        act_full, act_done = sem("act_bank_full"), sem("act_bank_emptied")
        dve_full, dve_done = sem("dve_bank_full"), sem("dve_bank_emptied")
        vs, as_, ps = sem("vector_step"), sem("scalar_step"), sem("pool_step")
        s_ssq, s_ssq2, s_gelu = sem("squares_summed"), sem("squares2_summed"), sem("gelu_done")
        s_rowf, s_hsum, s_hrms = sem("row_numbers"), sem("head_squares_summed"), sem("head_rms_ready")
        s_rows, s_ynorm, s_chain = sem("expert_rows_ready"), sem("y_normed"), sem("sample_vector_step")
        s_xn, s_dt, s_mag, s_fr, s_trig = sem("x_normed"), sem("dt_ready"), sem("decay_ready"), sem("angle_ready"), sem("trig_ready")
        s_lre = sem("decay_exponent_ready")
        s_prm, s_lamd, s_lame = sem("s5_params_ready"), sem("lambda_dots"), sem("lambda_exps")
        s_Bpad, s_angT, s_tabT, s_zfree, s_xT5, s_x5read = (sem("b_blocks_ready"), sem("table_angles"), sem("tables_ready"),
                                                            sem("z_used"), sem("states_ready"), sem("states_read"))
        s_s5, s_kvtok, s_qzero, s_fin = sem("s5_done"), sem("kv_tokens_ready"), sem("qz_zeroed"), sem("final_states_ready")
        s_nb, s_pexp, s_w, s_wt, s_pv, s_pvr = (sem("prompt_max"), sem("prompt_exps"), sem("prompt_weights"), sem("wT_read"),
                                                sem("prompt_pv"), sem("prompt_pv_read"))
        s_ktr, s_ktev, s_qb, s_sc, s_scc = (sem("k_transposed"), sem("k_emptied"), sem("q_block"), sem("scores_done"),
                                            sem("scores_copied"))
        s_mx, s_mxT, s_diag, s_mb, s_sh, s_ex, s_Es, s_den, s_dpv, s_do = (
            sem("max_by_key"), sem("max_turned"), sem("max_diagonal"), sem("max_broadcast"), sem("scores_shifted"),
            sem("sample_exps"), sem("exps_summed"), sem("denominators"), sem("sample_pv"), sem("sample_out"))
        s_ln, s_sg, s_yglu, s_mg = sem("heads_normed"), sem("glu_gate"), sem("glu_done"), sem("merged")
        s_h2, s_xres, s_gexp, s_mask, s_route = (sem("h2_ready"), sem("residual_done"), sem("gate_exps"), sem("mask_ready"),
                                                 sem("routing_ready"))
        s_nmx = sem("router_max")
        s_comb, s_gath = sem("combined"), [sem(f"rows_gathered{t}") for t in range(3)]

        s_zero, s_h2h, s_h2s, s_bsplit = (sem("rows_zeroed"), sem("h2_high"), sem("h2_split_done"), sem("bias_split_done"))
        s_tab = sem("job_table_step")
        e_sel, e_bg, e_bd, e_gath, e_xg, e_xh, e_xs = (sem("selection_ready"), sem("gate_bias_row_ready"), sem("down_bias_row_ready"),
                                                             sem("rows_selected"), sem("rows_copied"),
                                                             sem("x_high"), sem("x_split_ready"))
        e_guL, e_sum, e_g, e_u, e_sig, e_m, e_act, e_turn, e_ah, e_as = (
            sem("gate_up_low_copied"), sem("gate_up_summed"), sem("gate_clamped"), sem("up_clamped"), sem("sigmoid_done"),
            sem("gate_times_sigmoid"), sem("activation_ready"), sem("rows_turned"), sem("act_high"), sem("act_split_ready"))
        e_extra = sem("extra_job_done")
        e_yL, e_y, e_out = sem("down_low_copied"), sem("rows_summed"), sem("rows_written")
        c_hi, c_lov, c_lop, c_free = sem("chunk_high"), sem("chunk_low_by_vector"), sem("chunk_low_by_gpsimd"), sem("chunk_used")

        block = ctx.enter_context(nc.Block())

        def slot(name):
            return ring[:, SLOT[name], :]

        def wait_loaded(eng, name, i=0):
            eng.wait_ge(loaded[SLOT[name]], loaded_at(name, i))

        ck = A["cache_k"][0].rearrange("n p h d -> n p (h d)")
        cv = A["cache_v"][0].rearrange("n p h d -> n p (h d)")
        wgu = A["w_gate_up"][0].rearrange("e (k p) n -> e k p n", p=P)
        wdn = A["w_down"][0].rearrange("e (c k p) n -> e c p k n", p=P, k=2)

        turned = psum[:, 6:8, :].rearrange("p b (k c) -> p (b k) c", c=P)
        turned_x, turned_a = turned[:, :, 0:CAP], turned[:, :, CAP:]

        def wait_low(eng, q, i):
            pool, n = chunk_low(q, i)
            eng.wait_ge(c_lop if pool else c_lov, n)

        def extra_jobs(eng):
            eng.wait_ge(s_route, 1)
            return eng.value_load(jobi[0:1, 2 * NOVER:2 * NOVER + 1], min_val=0, max_val=NOVER)

        xp, xs = A["x_prompt"][0], A["x_sample"].rearrange("b s d -> (b s) d")
        xin = [xp[0:128, :], xp[128:256, :], xs]

        @block.sync
        def _(sp):
            def load(name, src, dst=None):
                if free_at(name):
                    sp.wait_ge(freed[SLOT[name]], free_at(name))
                sp.dma_start(slot(name) if dst is None else dst, src).then_inc(loaded[SLOT[name]], 16)

            sp.dma_start(pages[:, :], A["page_table"].rearrange("a b -> (a b)").unsqueeze(0)).then_inc(s_pages, 16)
            for k in range(8):
                load(f"w_in{k}", A["w_in"][0, k * P:(k + 1) * P, :])
            for k in range(8):
                load(f"w_gate{k}", A["w_gate"][0, k * P:(k + 1) * P, :])
            sp.wait_ge(s_pages, 16)

            def pages_of(kind, cache, b):
                for s in range(4):
                    name = f"{kind}{s}"
                    sp.wait_ge(freed[SLOT[name]], free_at(name, b))
                    for j in range(4):
                        page = sp.value_load(pages[0:1, ds(b * NPG + (4 * s + j), 1)], min_val=0, max_val=159)
                        sp.dma_start(ring[:, SLOT[name], j * 512:(j + 1) * 512],
                                     cache[ds(page, 1), :, :].rearrange("o p n -> p (o n)")).then_inc(loaded[SLOT[name]], 16)

            pages_of("K", ck, 0)
            load("w_glu", A["ssm_w_glu"][0].rearrange("(k p) n -> p k n", p=P),
                 slot("w_glu").rearrange("p (k n) -> p k n", k=4))
            for i in range(2):
                load(f"w_bs{i}", A["w_branch_ssm"][0, i * 256:(i + 1) * 256, :].rearrange("(k p) n -> p k n", p=P),
                     slot(f"w_bs{i}").rearrange("p (k n) -> p k n", k=2))
            load("w_ba0", A["w_branch_attn"][0, 0:256, :].rearrange("(k p) n -> p k n", p=P),
                 slot("w_ba0").rearrange("p (k n) -> p k n", k=2))
            sp.wait_ge(s_s5, 1)
            with sp.Fori(0, NB - 1) as b:
                pages_of("K", ck, b + 1)
                pages_of("V", cv, b)
            pages_of("V", cv, NB - 1)
            load("w_ba1", A["w_branch_attn"][0, 256:512, :].rearrange("(k p) n -> p k n", p=P),
                 slot("w_ba1").rearrange("p (k n) -> p k n", k=2))
            for i in range(4):
                load(f"w_out{i}", A["w_out"][0, i * 256:(i + 1) * 256, :].rearrange("(k p) n -> p k n", p=P),
                     slot(f"w_out{i}").rearrange("p (k n) -> p k n", k=2))

            def chunk(q, i, e):
                s = chunk_raw(i)
                qq, ii = (q, i - NRAW) if i >= NRAW else (q - 1, i + NRAW)
                wait_low(sp, qq, ii)
                if i < 8:
                    sp.dma_start(ring[:, s, :], wgu[ds(e, 1), i, :, :].rearrange("o p n -> p (o n)")).then_inc(loaded[s], 16)
                else:
                    sp.dma_start(ring[:, s, :].rearrange("p (k n) -> p k n", k=2),
                                 wdn[ds(e, 1), i - 8, :, :, :].rearrange("o p k n -> p (o k) n")).then_inc(loaded[s], 16)

            def first_chunk(c):
                s = chunk_raw(c + 4)
                if c < NRAW:
                    sp.wait_ge(freed[s], _uses[s])
                else:
                    wait_low(sp, 0, c + 4 - NRAW)
                sp.dma_start(ring[:, s, :], wgu[0, c, :, :]).then_inc(loaded[s], 16)

            for c in range(8):
                first_chunk(c)
            with sp.Fori(1, NE) as e:
                for i in range(8):
                    chunk(e, i, e)
                for i in range(8, 12):
                    chunk(e, i, e - 1)
            for i in range(4):
                s = chunk_raw(i)
                wait_low(sp, NE - 1, i + NRAW)
                sp.dma_start(ring[:, s, :].rearrange("p (k n) -> p k n", k=2), wdn[NE - 1, i, :, :, :]).then_inc(loaded[s], 16)
            extra = extra_jobs(sp)
            with sp.Fori(0, NOVER) as o:
                with sp.If(extra > o):
                    e = sp.value_load(jobi[0:1, ds(o, 1)], min_val=0, max_val=NE - 1)
                    for c in range(12):
                        i, q = (c + 4) % 12, o + (NE + (c + 4) // 12)
                        s = chunk_raw(i)
                        wait_low(sp, *((q, i - NRAW) if i >= NRAW else (q - 1, i + NRAW)))
                        if c < 8:
                            sp.dma_start(ring[:, s, :], wgu[ds(e, 1), c, :, :].rearrange("o p n -> p (o n)")).then_inc(loaded[s], 16)
                        else:
                            sp.dma_start(ring[:, s, :].rearrange("p (k n) -> p k n", k=2),
                                         wdn[ds(e, 1), c - 8, :, :, :].rearrange("o p k n -> p (o k) n")).then_inc(loaded[s], 16)
                with sp.Else():
                    sp.wait_ge(s_route, 1)

        @block.scalar
        def _(act):
            n_step = [0]

            def step(ins):
                n_step[0] += 1
                ins.then_inc(as_, 1)
                act.wait_ge(as_, n_step[0])

            act.dma_start(cst[:, :], A["consts"]).then_inc(s_const, 16)
            for t, (t0, n) in enumerate(TILES):
                act.dma_start(x[0:n, t, :], xin[t]).then_inc(s_x, 16)
            small = [
                (rows[0:8, :], A["norm_mix_g"][0].rearrange("(r n) -> r n", n=P)),
                (rows[8:24, :], A["b_gate"][0].rearrange("(r n) -> r n", n=P)),
                (rows[24:28, :], A["ssm_b_glu"][0].rearrange("(r n) -> r n", n=P)),
                (rows[28:32, :], A["ssm_d"][0].rearrange("(r a) h -> r (a h)", r=4)),
                (prm_in[:, 0, :], A["ssm_lambda_re"][0].rearrange("(j a) p -> j (a p)", a=2)),
                (prm_in[:, 1, :], A["ssm_lambda_im"][0].rearrange("(j a) p -> j (a p)", a=2)),
                (logdt[:, 0:2], A["ssm_log_dt"][0].rearrange("(j a) -> j a", a=2)),
                (x0rows[:, 0, :], A["state_ssm_re"][0].rearrange("b (j a) p -> (b j) (a p)", a=2)),
                (x0rows[:, 1, :], A["state_ssm_im"][0].rearrange("b (j a) p -> (b j) (a p)", a=2)),
                (bin_[:, 0], A["ssm_b_re"][0].rearrange("(j a) p h -> (a p) j h", a=2)),
                (bin_[:, 1], A["ssm_b_im"][0].rearrange("(j a) p h -> (a p) j h", a=2)),
            ]
            for i, name in enumerate(["ssm_c_re", "ssm_c_im"]):
                src = A[name][0].rearrange("(c g) h p -> (g h) c p", c=NCT)
                for a in range(2):
                    small.append((cdup[:, i, :, a * 64:(a + 1) * 64], src))
            for i, name in enumerate(["lambda_q1", "lambda_k1", "lambda_q2", "lambda_k2"]):
                small.append((lamv[:, i, :], A[name][0].partition_broadcast(P)))
            for dst, src in small:
                act.dma_start(dst, src).then_inc(s_par, 16)
            n_small = len(small)
            assert n_small == 19

            act.wait_ge(s_x, 48)
            act.wait_ge(ps, 2)

            def rms(t, n, dump, done):
                step(nc.scalar.activation(dump[0:n, :], x[0:n, t, :], ACT.Square, accum_out=sc[0:n, t:t + 1]))
                nc.scalar.activation(sc[0:n, t:t + 1], sc[0:n, t:t + 1], ACT.Sqrt, scale=1.0 / D, bias=epsc[0:n, :]).then_inc(done, 1)

            for t, (t0, n) in enumerate(TILES):
                rms(t, n, normj, s_ssq)

            act.wait_ge(s_par, 16 * n_small)
            nc.scalar.activation(logdt[:, 2:4], logdt[:, 0:2], ACT.Exp).then_inc(s_dt, 1)
            act.wait_ge(s_lre, 1)
            nc.scalar.activation(prm[:, 0, :], pw[:, 1, :], ACT.Exp).then_inc(s_mag, 1)
            act.wait_ge(s_lamd, 1)
            nc.scalar.activation(sc[:, 8:10], sc[:, 6:8], ACT.Exp).then_inc(s_lame, 1)
            act.wait_ge(s_fr, 1)
            nc.scalar.activation(pw[:, 4, :], prm[:, 1, :], ACT.Sin, scale=2 * math.pi * (1 - 2e-7))
            step(nc.scalar.activation(pw[:, 5, :], prm[:, 1, :], ACT.Abs))
            nc.scalar.activation(pw[:, 6, :], pw[:, 5, :], ACT.Sin, bias=halfpi[0:16, :], scale=-2 * math.pi * (1 - 2e-7)
                                 ).then_inc(s_trig, 1)

            def job(i):
                act.wait_ge(act_full, i + 1)
                return psum[:, i % 4, :]

            def tables(ct):
                act.wait_ge(s_angT, ct + 1)
                nc.scalar.activation(sinT[:, :, :], cosT[:, :, :], ACT.Sin, scale=2 * math.pi * (1 - 2e-7))
                step(nc.scalar.activation(cosT[:, :, :], cosT[:, :, :], ACT.Abs))
                nc.scalar.activation(cosT[:, :, :], cosT[:, :, :], ACT.Sin, bias=halfpi[:, :],
                                     scale=-2 * math.pi * (1 - 2e-7)).then_inc(s_tabT, 1)

            for i in range(4):
                nc.scalar.activation(uT[:, i, :], job(ACT_JOB["u"] + i)[:, 0:T], ACT.Copy).then_inc(act_done, 1)
            act.wait_ge(s_prm, 1)

            def inputs(ct):
                if ct:
                    act.wait_ge(s_zfree, ct)
                for jj in range(4):
                    for c, z in enumerate((zr, zi)):
                        pz = job(ACT_JOB[f"z{ct}"] + 2 * jj + c)
                        nc.scalar.activation(z[:, jj, 0:SEQ], pz[:, 0:SEQ], ACT.Copy)
                        nc.scalar.activation(z[:, jj, SEQ:W5].rearrange("p (b s) -> p b s", s=NS + 1)[:, :, 1:],
                                             pz[:, SEQ:T].rearrange("p (b s) -> p b s", s=NS), ACT.Copy).then_inc(act_done, 1)

            tables(0)
            inputs(0)
            for ct in range(NCT):
                for i in range(4 * ct, 4 * ct + 4):
                    nc.scalar.activation(gates[:, i, :], job(ACT_JOB[f"gate{ct}"] + i % 4)[:, 0:T], ACT.Sigmoid,
                                         bias=vecT[:, 8 + i:9 + i]).then_inc(act_done, 1)
                if ct + 1 < NCT:
                    inputs(ct + 1)
                    tables(ct + 1)

            act.wait_ge(s_kvtok, 1)
            kvo = [(A["o_k_prompt"], A["o_k_sample"], qk[:, 1]), (A["o_v_prompt"], A["o_v_sample"], vt)]
            for o_p, o_s, src in kvo:
                op = o_p[0, 0].rearrange("s h d -> s (h d)")
                for t in range(2):
                    act.dma_start(op[t * 128:(t + 1) * 128, :], src[:, t, :]).then_inc(s_kvout, 16)
                act.dma_start(o_s[0].rearrange("b s h d -> (b s) (h d)"), src[0:NSMP, 2, :]).then_inc(s_kvout, 16)
            act.wait_ge(s_fin, 1)
            for c, (o_p, o_s) in enumerate([(A["o_re_prompt"], A["o_re_sample"]), (A["o_im_prompt"], A["o_im_sample"])]):
                act.dma_start(o_p[0, 0].rearrange("(j a) p -> j (a p)", a=2), frow[0:NJ, c, :]).then_inc(s_out, 16)
                act.dma_start(o_s[0].rearrange("b (j a) p -> (b j) (a p)", a=2), frow[:, 2 + c, :]).then_inc(s_out, 16)
            act.wait_ge(s_s5, 1)
            late = [(gvec, A["norm_ffn_g"][0].partition_broadcast(P)),
                    (wr, A["w_router"][0].rearrange("(k p) n -> p k n", p=P)),
                    (brt, A["b_router"][0].partition_broadcast(P)),
                    (subg, A["attn_subln_g"][0].partition_broadcast(P))]
            for dst, src in late:
                act.dma_start(dst, src).then_inc(s_late, 16)

            nc.scalar.activation(yT[:, :, :], yT[:, :, :], ACT.Gelu_apprx_tanh).then_inc(s_gelu, 1)

            def p_exp(n):
                act.wait_ge(s_nb, n + 1)
                w = 128 * (n // 4 + 1)
                for c in range(2):
                    ins = nc.scalar.activation(pE[:, n % 2, c, 0:w], pS[:, n % 2, c, 0:w], ACT.Exp, scale=SCALE,
                                               bias=st4[:, n % 2, c:c + 1], accum_out=st4[:, n % 2, 2 + c:3 + c])
                step(ins)
                nc.scalar.activation(sc[:, 14:15], C("ones")[:, 0:1], ACT.Copy).then_inc(s_pexp, 1)

            p_exp(0)
            for n in range(8):
                if n + 1 < 8:
                    p_exp(n + 1)
                w = 128 * (n // 4 + 1)
                nc.scalar.activation(pWT[:, n % 2, 0:w // 128, :],
                                     job(ACT_JOB["wT"] + n)[:, 0:w].rearrange("p (k q) -> p k q", q=P),
                                     ACT.Copy).then_inc(act_done, 1)

            def keys(i, lo, hi):
                for pg in range(lo, hi):
                    act.wait_ge(s_ktr, i * NPG + (pg + 1))
                    nc.scalar.activation(kt[:, pg % 4, :], psum[:, pg % 4, :], ACT.Copy).then_inc(s_ktev, 1)

            def exps(i):
                act.wait_ge(s_sh, i + 1)
                nc.scalar.activation(En[:, :], sn[:, :], ACT.Exp, scale=SCALE)
                nc.scalar.activation(E[:, :, :], s_sb[:, :, :], ACT.Exp, scale=SCALE).then_inc(s_ex, 1)

            def head_rms(t, n):
                act.wait_ge(s_hsum, t + 1)
                nc.scalar.activation(st4[0:n, 2, :], st4[0:n, 0, :], ACT.Sqrt, scale=1.0 / DV, bias=epsc[0:n, :]).then_inc(s_hrms, 1)

            for t in range(2):
                head_rms(t, 128)
            keys(0, 0, NPG)
            with act.Fori(1, NB) as i:
                keys(i, 0, 9)
                exps(i - 1)
                keys(i, 9, NPG)
            exps(NB - 1)
            head_rms(2, NSMP)

            act.wait_ge(s_kvout, 96)
            act.wait_ge(dve_done, DVE_JOB["s"])
            for t, (t0, n) in enumerate(TILES):
                act.dma_start(x[0:n, t, :], xin[t]).then_inc(s_xagain, 16)
            for i in range(4):
                nc.scalar.activation(sg[:, i, :], job(ACT_JOB["glu"] + i)[:, 0:T], ACT.Sigmoid,
                                     bias=vecT[:, 24 + i:25 + i]).then_inc(act_done, 1)

            for t, (t0, n) in enumerate(TILES):
                act.wait_ge(s_xres, t + 1)
                rms(t, n, junk, s_ssq2)
            for t, (t0, n) in enumerate(TILES):
                act.wait_ge(s_h2, t + 1)
                nc.scalar.activation(h2s[0:n, 0, t, :], h2[0:n, t, :], ACT.Copy).then_inc(s_h2h, 1)
            act.wait_ge(s_h2, 3)
            act.dma_start(gvec, A["norm_final_g"].partition_broadcast(P)).then_inc(s_gfin, 16)
            act.wait_ge(dve_done, DVE_JOB["lg"])
            act.wait_ge(s_h2s, 3)
            for half in range(2):
                act.dma_start(braw[32 * half:32 * half + 32, 0:2 * D], A["b_gate_up"][0]).then_inc(s_bias, 16)
                act.dma_start(braw[32 * half:32 * half + 32, 2 * D:3 * D], A["b_down"][0]).then_inc(s_bias, 16)
            for t, (t0, n) in enumerate(TILES):
                act.wait_ge(s_nmx, t + 1)
                step(nc.scalar.activation(gk[0:n, t, :], mx8[0:n, t, 0:TOPK], ACT.Exp, bias=nmx[0:n, t, :],
                                          accum_out=gsum[0:n, t, :]))
                nc.scalar.activation(sc[:, 14:15], C("ones")[:, 0:1], ACT.Copy).then_inc(s_gexp, 1)

            def high(q, i):
                act.wait_ge(loaded[chunk_raw(i)], chunk_loaded(q, i))
                if not (isinstance(q, int) and q * 12 + i < 4 + NSPLIT):
                    act.wait_ge(c_free, q * 12 + (i - 3 - NSPLIT))
                nc.scalar.activation(whi[:, i % NSPLIT, :], ring[:, chunk_raw(i), :], ACT.Copy).then_inc(c_hi, 1)

            def copy_gu(q, i):
                act.wait_ge(c_free, chunk_used(q, i))
                nc.scalar.activation(guL.rearrange("p (b n) -> p b n", b=4), psum[CAP:P, 0:4, :], ACT.Copy).then_inc(e_guL, 1)

            def sigm(j):
                act.wait_ge(e_g, j + 1)
                nc.scalar.activation(sig, gg, ACT.Sigmoid, scale=ALPHA).then_inc(e_sig, 1)

            def copy_x(j, shift=0):
                act.wait_ge(e_gath, j + (1 + shift))
                nc.scalar.activation(xa[0:CAP, :].rearrange("p (b n) -> p b n", b=2), psum[0:CAP, 6:8, :], ACT.Copy).then_inc(e_xg, 1)

            def high_x(turn):
                act.wait_ge(e_turn, turn)
                nc.scalar.activation(xs_[:, :, 0:CAP], turned_x, ACT.Copy).then_inc(e_xh, 1)

            def high_a(turn):
                act.wait_ge(e_turn, turn)
                nc.scalar.activation(as2[:, :, 0:CAP], turned_a, ACT.Copy).then_inc(e_ah, 1)

            def copy_y(q, i):
                act.wait_ge(c_free, chunk_used(q, i))
                nc.scalar.activation(yL.rearrange("p (b n) -> p b n", b=2), psum[CAP:P, 4:6, :], ACT.Copy).then_inc(e_yL, 1)

            act.wait_ge(s_mg, 1)
            act.wait_ge(dve_done, DVE_JOB["h2T"])
            for c in range(NSPLIT):
                high(0, 4 + c)
            copy_x(0)
            high_x(1)
            high(0, 4 + NSPLIT)
            copy_x(1)
            for c in range(NSPLIT + 1, 8):
                high(0, 4 + c)
            copy_gu(0, 11)
            high_x(2)
            high(1, 0)
            sigm(0)
            high(1, 1)
            with act.Fori(1, NE) as j:
                high(j, 2)
                high(j, 3)
                copy_x(j + 1)
                for i in (4, 5, 6):
                    high(j, i)
                high_a(j + 2)
                for i in (7, 8, 9, 10):
                    high(j, i)
                copy_gu(j, 7)
                act.wait_ge(e_as, j)
                high_x(j + 2)
                high(j, 11)
                sigm(j)
                high(j + 1, 0)
                high(j + 1, 1)
                act.wait_ge(e_u, j + 1)
                copy_y(j, 11)
            high_a(NE + 2)
            for i in (2, 3):
                high(NE, i)
            copy_y(NE, 3)
            extra = extra_jobs(act)
            with act.Fori(0, NOVER) as o:
                with act.If(extra > o):
                    j = act.snap(o + NE)
                    copy_x(j, 1)
                    turn = act.snap(o * 2 + (NE + 3))
                    high_x(turn)
                    for c in range(12):
                        if c == 10:
                            copy_gu(o + NE, 11)
                            sigm(j)
                            high_a(turn + 1)
                        i = (c + 4) % 12
                        high(o + (NE + (c + 4) // 12), i)
                    copy_y(o + (NE + 1), 3)
                with act.Else():
                    act.wait_ge(s_route, 1)
            for t, (t0, n) in enumerate(TILES):
                act.wait_ge(s_comb, t + 1)
                rms(t, n, junk, s_ssq2)
            outs = [A["o_y_prompt"][0, 0:128, :], A["o_y_prompt"][0, 128:256, :], A["o_y_sample"].rearrange("b s d -> (b s) d")]
            for t, (t0, n) in enumerate(TILES):
                act.wait_ge(s_ynorm, t + 1)
                act.dma_start(outs[t], x[0:n, t, :]).then_inc(s_out, 16)
            act.wait_ge(s_kvout, 96)
            act.wait_ge(s_out, 16 * 7)

        @block.gpsimd
        def _(pool):
            pool.memset(halfpi[:, :], math.pi / 2).then_inc(ps, 1)
            pool.memset(epsc[:, :], EPS).then_inc(ps, 1)

            pool.memset(zeros, 0.0).then_inc(ps, 1)
            pool.wait_ge(ps, 3)
            pool.dma_start(ydram[NE * CAP:, :].rearrange("(p a) n -> p a n", p=64),
                           zeros.unsqueeze(1).to_broadcast([64, NOVER, D])).then_inc(s_zero, 16)
            pool.wait_ge(s_zero, 16)

            def low(q, i):
                pool.wait_ge(c_hi, q * 12 + (i - 3))
                nc.gpsimd.tensor_tensor(wlo[:, i % NSPLIT, :], ring[:, chunk_raw(i), :], whi[:, i % NSPLIT, :],
                                        ALU.subtract).then_inc(c_lop, 1)

            def rows_out(j):
                pool.wait_ge(e_y, j + 1)
                pool.dma_start(ydram[ds(j * CAP, CAP), :], yS).then_inc(e_out, 16)

            for i in POOL_CHUNKS:
                if i >= 4:
                    low(0, i)
            with pool.Fori(1, NE) as j:
                for i in POOL_CHUNKS:
                    low(j, i)
                rows_out(j - 1)
            for i in POOL_CHUNKS:
                if i < 4:
                    low(NE, i)
            rows_out(NE - 1)
            extra = extra_jobs(pool)
            with pool.Fori(0, NOVER) as o:
                with pool.If(extra > o):
                    for c in range(12):
                        if (c + 4) % 12 in POOL_CHUNKS:
                            low(o + (NE + (c + 4) // 12), (c + 4) % 12)
                    rows_out(o + NE)
                    pool.wait_ge(e_out, o * 16 + 16 * (NE + 1))
                    pool.sem_inc(e_extra, 1)
                with pool.Else():
                    pool.sem_inc(e_extra, 1)
            pool.wait_ge(e_out, 16 * NE)
            pool.wait_ge(e_extra, NOVER)
            for t, (t0, n) in enumerate(TILES):
                for k in range(TOPK):
                    pool.indirect_dma_start(ycomb[0:n, t, k, :], None, ydram,
                                            bass.IndirectOffsetOnAxis(rowi[0:n, t, k:k + 1], 0),
                                            bounds_check=NJOB * CAP - 1).then_inc(s_gath[t], 16)

        @block.tensor
        def _(pe):
            na, nd = [0], [0]

            def abank():
                i = na[0]
                na[0] += 1
                if i >= 4:
                    pe.wait_ge(act_done, i - 3)
                return psum[:, i % 4, :]

            def dbank():
                i = nd[0]
                nd[0] += 1
                if i >= 3:
                    pe.wait_ge(dve_done, i - 2)
                return psum[:, 4 + i % 3, :]

            def mm(out, a, b, start, stop):
                return nc.tensor.matmul(out, lhsT=a, rhs=b, start=start, stop=stop, skip_group_check=True)

            def tr(out, in_, n=P):
                return nc.tensor.transpose(out, in_, ident[0:n, 0:n])

            pe.wait_ge(s_const, 16)
            for t, (t0, n) in enumerate(TILES):
                pe.wait_ge(s_xn, t + 1)
                for half in range(2 if n == 128 else 1):
                    b = dbank()
                    ks = range(4 * half, 4 * half + 4) if n == 128 else range(8)
                    for i, k in enumerate(ks):
                        last = tr(b[:, i * n:(i + 1) * n], x[0:n, t, k * P:(k + 1) * P], n)
                    last.then_inc(dve_full, 1)
            pe.wait_ge(s_par, 16 * 19)
            tr(dbank()[:, 0:32], rows[0:32, :], 32).then_inc(dve_full, 1)
            pe.wait_ge(s_prm, 1)
            b = dbank()
            for i in range(4):
                last = tr(b[:, i * 16:(i + 1) * 16], prm[:, i, :], 16)
            last.then_inc(dve_full, 1)
            b = dbank()
            for i in range(2):
                last = tr(b[:, i * P:(i + 1) * P], x0rows[:, i, :])
            last.then_inc(dve_full, 1)
            pe.wait_ge(dve_done, DVE_JOB["prm"])
            for k in range(8):
                wait_loaded(pe, f"w_in{k}")
            for i in range(4):
                b = abank()
                for k in range(KD):
                    last = mm(b[:, 0:T], slot(f"w_in{k}")[:, i * P:(i + 1) * P], hT[:, k, :], k == 0, k == KD - 1)
                last.then_inc(act_full, 1)
            for t, (t0, n) in enumerate(TILES):
                for c in range(3):
                    b = dbank()
                    for k in range(KD):
                        last = mm(b[0:n, :], hT[:, k, t0:t0 + n], slot(f"w_in{k}")[:, 512 * (c + 1):512 * (c + 2)],
                                  k == 0, k == KD - 1)
                        if t == 2 and c == 2 and k < KD - 1:
                            last.then_inc(freed[SLOT[f"w_in{k}"]], 1)
                    last.then_inc(dve_full, 1)
            pe.wait_ge(dve_full, nd[0])
            pe.sem_inc(freed[SLOT["w_in7"]], 1)
            for c in range(2):
                for q in range(4):
                    b = dbank()
                    pe.wait_ge(s_Bpad, 1)
                    for i in range(4):
                        last = tr(b[:, i * P:(i + 1) * P], (padr, padi)[c][:, 4 * q + i, :])
                    last.then_inc(dve_full, 1)
            for c in range(2):
                b = dbank()
                for i in range(4):
                    last = tr(b[:, i * P:(i + 1) * P], cdup[:, c, i, :])
                last.then_inc(dve_full, 1)
            pe.wait_ge(act_done, ACT_JOB["z0"])
            pe.wait_ge(dve_done, DVE_JOB["C"])

            def s5_in(ct):
                for j in range(4 * ct, 4 * ct + 4):
                    for c in range(2):
                        mm(abank()[:, 0:T], bbT[:, c, j, :], uT[:, ct, :], True, True).then_inc(act_full, 1)

            def s5_out(ct):
                b = dbank()
                pe.wait_ge(s_xT5, ct + 1)
                for jj in range(4):
                    j = 4 * ct + jj
                    mm(b[:, 0:W5], padr[:, j, :], t1[:, jj, :], jj == 0, False)
                    last = mm(b[:, 0:W5], padi[:, j, :], t3[:, jj, :], False, jj == 3)
                last.then_inc(dve_full, 1)

            s5_in(0)
            for k in range(8):
                wait_loaded(pe, f"w_gate{k}")
            for i in range(16):
                b = abank()
                for k in range(KD):
                    last = mm(b[:, 0:T], slot(f"w_gate{k}")[:, i * P:(i + 1) * P], hT[:, k, :], k == 0, k == KD - 1)
                    if i == 15 and k < KD - 1:
                        last.then_inc(freed[SLOT[f"w_gate{k}"]], 1)
                last.then_inc(act_full, 1)
                if i % 4 == 3:
                    ct = i // 4
                    if ct + 1 < NCT:
                        s5_in(ct + 1)
                    if ct + 1 == NCT:
                        n_gate = na[0]
                    s5_out(ct)
            pe.wait_ge(act_full, n_gate)
            pe.sem_inc(freed[SLOT["w_gate7"]], 1)
            pe.wait_ge(dve_done, DVE_JOB["fin"])
            b = dbank()
            for c in range(2):
                tr(b[0:NJ, c * P:(c + 1) * P], finp[:, c, :])
            for c in range(2):
                last = tr(b[:, (2 + c) * P:(3 + c) * P], fins[:, c].rearrange("p b j -> p (b j)"))
            last.then_inc(dve_full, 1)
            for t, (t0, n) in enumerate(TILES):
                for c in range(2):
                    b = dbank()
                    for h in range(H):
                        last = tr(b[:, h * n:(h + 1) * n], qk[0:n, c, t, h * P:(h + 1) * P], n)
                    last.then_inc(dve_full, 1)

            def p_scores(n):
                i, h = divmod(n, 4)
                b = dbank()
                w = 128 * (i + 1)
                for c in range(2):
                    last = mm(b[:, c * w:(c + 1) * w], qz[:, h, c, i * P:(i + 1) * P], kT[:, h, 0:w], True, True)
                last.then_inc(dve_full, 1)

            pe.wait_ge(dve_done, DVE_JOB["s"])
            p_scores(0)
            p_scores(1)
            for n in range(8):
                i, h = divmod(n, 4)
                if n + 2 < 8:
                    p_scores(n + 2)
                b = abank()
                pe.wait_ge(s_w, n + 1)
                for k in range(i + 1):
                    last = tr(b[:, k * P:(k + 1) * P], pW[:, n % 2, k * P:(k + 1) * P])
                last.then_inc(act_full, 1)
                pe.wait_ge(act_done, ACT_JOB["wT"] + n + 1)
                if n == 4:
                    pe.wait_ge(s_pvr, 1)
                for k in range(i + 1):
                    last = mm(psum[:, 7, h * P:(h + 1) * P], pWT[:, n % 2, k, :], vt[:, k, h * P:(h + 1) * P], k == 0, k == i)
                last.then_inc(s_pv, 1)

            def keys_turn(i, pg):
                if pg % 4 == 0:
                    pe.wait_ge(loaded[SLOT[f"K{pg // 4}"]], loaded_at(f"K{pg // 4}", i))
                for h in range(H):
                    last = tr(psum[:, pg % 4, h * P:(h + 1) * P], ring[:, SLOT[f"K{pg // 4}"], (pg % 4) * 512 + h * P:(pg % 4) * 512 + (h + 1) * P])
                last.then_inc(s_ktr, 1)

            def scores(i, pg):
                if pg == 0:
                    pe.wait_ge(s_qb, i + 1)
                pe.wait_ge(s_ktev, i * NPG + (pg + 1))
                for h in range(H):
                    last = mm(psum[:, 4, pg * 32 + h * QC:pg * 32 + (h + 1) * QC], kt[:, pg % 4, h * P:(h + 1) * P], qb[:, h, :], True, True)
                if pg % 4 == 3:
                    last.then_inc(freed[SLOT[f"K{pg // 4}"]], 1)

            def new_scores():
                for h in range(H):
                    last = mm(psum[0:NSMP, 5, h * QC:(h + 1) * QC], kT[:, h, SEQ:T], qb[:, h, :], True, True)
                last.then_inc(s_sc, 1)

            def max_turn(j):
                pe.wait_ge(s_do, j)
                pe.wait_ge(s_mx, j + 1)
                tr(psum[0:32, 6, 0:128], mx[:, :])
                tr(psum[0:32, 6, 128:160], sn[:, :], 32).then_inc(s_mxT, 1)

            def max_bcast(j):
                pe.wait_ge(s_diag, j + 1)
                mm(psum[:, 6, 160:192], ones[0:32, :], diag[:, :], True, True).then_inc(s_mb, 1)

            def denominators(j):
                pe.wait_ge(s_Es, j + 1)
                mm(psum[:, 6, 192:224], ones[:, :], Es[:, :], True, False)
                mm(psum[:, 6, 192:224], ones[0:32, :], En[:, :], False, True).then_inc(s_den, 1)

            def values(j):
                for pg in range(NPG):
                    if pg % 4 == 0:
                        pe.wait_ge(loaded[SLOT[f"V{pg // 4}"]], loaded_at(f"V{pg // 4}", j))
                    for h in range(H):
                        last = mm(psum[:, 7, h * QC:(h + 1) * QC], ring[:, SLOT[f"V{pg // 4}"], (pg % 4) * 512 + h * P:(pg % 4) * 512 + (h + 1) * P],
                                  E[:, pg, h * QC:(h + 1) * QC], pg == 0 and h == 0, False)
                    if pg % 4 == 3:
                        last.then_inc(freed[SLOT[f"V{pg // 4}"]], 1)
                for h in range(H):
                    last = mm(psum[:, 7, h * QC:(h + 1) * QC], vt[0:NSMP, 2, h * P:(h + 1) * P], En[:, h * QC:(h + 1) * QC], False, True)
                last.then_inc(s_dpv, 1)

            def batch(i, j):
                for pg in range(NPG + 1):
                    if pg < NPG:
                        if j is not None or pg >= 4:
                            pe.wait_ge(s_ktev, i * NPG + (pg - 3))
                        keys_turn(i, pg)
                    if pg:
                        scores(i, pg - 1)
                    if j is not None and pg == 2:
                        max_turn(j)
                    if j is not None and pg == 5:
                        max_bcast(j)
                    if j is not None and pg == 13:
                        denominators(j)
                new_scores()
                if j is not None:
                    pe.wait_ge(s_do, j)
                    values(j)

            pe.wait_ge(s_pvr, 2)
            pe.wait_ge(act_done, ACT_JOB["glu"])
            pe.wait_ge(dve_done, DVE_JOB["oS"])
            batch(0, None)
            with pe.Fori(1, NB) as i:
                batch(i, i - 1)
            max_turn(NB - 1)
            max_bcast(NB - 1)
            denominators(NB - 1)
            pe.wait_ge(s_do, NB - 1)
            values(NB - 1)

            pe.wait_ge(s_do, NB)
            b = dbank()
            for h in range(H):
                last = tr(b[0:NSMP, h * P:(h + 1) * P], oTs[:, h, :])
            last.then_inc(dve_full, 1)
            wait_loaded(pe, "w_glu")
            pe.wait_ge(s_gelu, 1)
            for i in range(4):
                b = abank()
                for k in range(4):
                    last = mm(b[:, 0:T], slot("w_glu")[:, k * 512 + i * P:k * 512 + (i + 1) * P], yT[:, k, :], k == 0, k == 3)
                last.then_inc(act_full, 1)
            for t, (t0, n) in enumerate(TILES):
                pe.wait_ge(s_ln, t + 1)
                b = dbank()
                for h in range(H):
                    last = tr(b[:, h * n:(h + 1) * n], ot[0:n, t, h * P:(h + 1) * P], n)
                last.then_inc(dve_full, 1)
            for name, src, ready in (("w_bs", yT, 1), ("w_ba", oT, None)):
                wait_loaded(pe, name + "0")
                wait_loaded(pe, name + "1")
                if ready:
                    pe.wait_ge(s_yglu, ready)
                else:
                    pe.wait_ge(dve_done, DVE_JOB["bs"])
                for i in range(KD):
                    b = dbank()
                    for k in range(4):
                        last = mm(b[:, 0:T], slot(f"{name}{k // 2}")[:, (k % 2) * D + i * P:(k % 2) * D + (i + 1) * P],
                                  src[:, k, :], k == 0, k == 3)
                    last.then_inc(dve_full, 1)
            pe.wait_ge(s_mg, 1)
            pe.sem_inc(freed[SLOT["w_glu"]], 1)
            for name in ("w_bs0", "w_bs1", "w_ba0", "w_ba1"):
                pe.sem_inc(freed[SLOT[name]], 1)
            for i in range(4):
                wait_loaded(pe, f"w_out{i}")
            for t, (t0, n) in enumerate(TILES):
                for half in range(2):
                    b = dbank()
                    for k in range(KD):
                        last = mm(b[0:n, :], mg[:, k, t0:t0 + n],
                                  slot(f"w_out{k // 2}")[:, (k % 2) * D + half * 512:(k % 2) * D + (half + 1) * 512],
                                  k == 0, k == KD - 1)
                    last.then_inc(dve_full, 1)
            pe.wait_ge(dve_done, DVE_JOB["h2T"])
            for i in range(4):
                pe.sem_inc(freed[SLOT[f"w_out{i}"]], 1)
            for t, (t0, n) in enumerate(TILES):
                pe.wait_ge(s_h2, t + 1)
                for half in range(2 if n == 128 else 1):
                    b = dbank()
                    ks = range(4 * half, 4 * half + 4) if n == 128 else range(8)
                    for i, k in enumerate(ks):
                        last = tr(b[:, i * n:(i + 1) * n], h2[0:n, t, k * P:(k + 1) * P], n)
                    last.then_inc(dve_full, 1)
            pe.wait_ge(s_late, 64)
            pe.wait_ge(dve_done, DVE_JOB["lg"])
            for t, (t0, n) in enumerate(TILES):
                b = dbank()
                for k in range(KD):
                    last = mm(b[0:n, 0:NE], h2T[:, k, t0:t0 + n], wr[:, k, :], k == 0, k == KD - 1)
                last.then_inc(dve_full, 1)
            for t, (t0, n) in enumerate(TILES):
                b = dbank()
                pe.wait_ge(s_mask, 3)
                for s in range(t):
                    mm(b[0:n, 0:NE], ones[:, 0:n], mask[:, s, :], s == 0, False)
                mm(b[0:n, 0:NE], C("tri", n)[:, 0:n], mask[0:n, t, :], t == 0, True).then_inc(dve_full, 1)
            b = dbank()
            for t, (t0, n) in enumerate(TILES):
                last = mm(b[:, 0:NE], ones[0:n, :], mask[0:n, t, :], t == 0, t == 2)
            last.then_inc(dve_full, 1)
            def select(j, shift=0):
                pe.wait_ge(e_sel, j + (1 + 2 * shift))
                for t, (t0, n) in enumerate(TILES):
                    for p in range(2):
                        for half in range(2):
                            last = mm(psum[0:CAP, 6 + half, :], sel[0:n, t, :], h2s[0:n, p, t, half * 512:(half + 1) * 512],
                                      t == 0 and p == 0, t == 2 and p == 1)
                last.then_inc(e_gath, 1)

            def turn(j, shift=0):
                pe.wait_ge(e_xg, j + (1 + shift))
                for k in range(KD):
                    last = tr(turned[:, k, :], xa[:, k * P:(k + 1) * P])
                last.then_inc(e_turn, 1)

            def products(q, i, out, stat, steps, end=False):
                wait_low(pe, q, i)
                for r in range(steps):
                    for p, w in enumerate((whi, wlo)):
                        for b in range(4 // steps):
                            last = mm(psum[:, out + b, :], stat[:, r, :],
                                      w[:, i % NSPLIT, (r * (4 // steps) + b) * 512:(r * (4 // steps) + b + 1) * 512],
                                      False, end and r == steps - 1 and p == 1)
                last.then_inc(c_free, 1)

            def gate_up(j, chunks, shift=0, ahead=True):
                pe.wait_ge(e_xs, j + (1 + shift))
                pe.wait_ge(e_bg, j + (1 + shift))
                if not isinstance(j, int):
                    pe.wait_ge(e_sum, j)
                for b in range(4):
                    mm(psum[:, b, :], bsg[:, :], bias_s[:, b * 512:(b + 1) * 512], True, False)
                for k, (q, i) in enumerate(chunks):
                    if ahead and k == 2:
                        select(j + 1)
                    if ahead and k == 5:
                        if not isinstance(j, int):
                            pe.wait_ge(e_act, j)
                        turn(j + 1)
                    products(q, i, 0, xs_[:, k:k + 1, :], 1, k == KD - 1)

            def down(j, chunks):
                pe.wait_ge(e_as, j + 1)
                pe.wait_ge(e_bd, j + 1)
                pe.wait_ge(e_y, j)
                for b in range(2):
                    mm(psum[:, 4 + b, :], bsd[:, :], bias_s[:, (4 + b) * 512:(5 + b) * 512], True, False)
                for k, (q, i) in enumerate(chunks):
                    products(q, i, 4, as2[:, 2 * k:2 * k + 2, :], 2, k == 3)

            pe.wait_ge(act_done, ACT_JOB["end"])
            pe.wait_ge(dve_done, DVE_JOB["end"])
            pe.wait_ge(s_bsplit, 1)
            select(0)
            turn(0)
            gate_up(0, [(0, 4 + c) for c in range(8)])
            with pe.Fori(1, NE) as j:
                gate_up(j, [(j, i) for i in range(8)])
                down(j - 1, [(j, i) for i in range(8, 12)])
            pe.wait_ge(e_act, NE)
            turn(NE)
            down(NE - 1, [(NE, i) for i in range(4)])
            extra = extra_jobs(pe)
            with pe.Fori(0, NOVER) as o:
                with pe.If(extra > o):
                    j = pe.snap(o + NE)
                    pe.wait_ge(e_y, j)
                    select(j, 1)
                    turn(j, 1)
                    gate_up(j, [(o + (NE + (c + 4) // 12), (c + 4) % 12) for c in range(8)], 1, False)
                    pe.wait_ge(e_act, j + 1)
                    turn(j, 1)
                    down(j, [(o + (NE + (c + 4) // 12), (c + 4) % 12) for c in range(8, 12)])
                with pe.Else():
                    pe.wait_ge(s_route, 1)

        @block.vector
        def _(v):
            n_step, n_bank = [0], [0]

            def step(ins):
                n_step[0] += 1
                ins.then_inc(vs, 1)
                v.wait_ge(vs, n_step[0])

            def job(stage, i):
                assert DVE_JOB[stage] + i == n_bank[0], (stage, i, n_bank[0])
                v.wait_ge(dve_full, n_bank[0] + 1)
                b = psum[:, 4 + n_bank[0] % 3, :]
                n_bank[0] += 1
                return b

            TT, TS, STT, CP = nc.vector.tensor_tensor, nc.vector.tensor_scalar, nc.vector.scalar_tensor_tensor, nc.vector.tensor_copy

            def bc(ap, axis, shape):
                return ap.unsqueeze(axis).to_broadcast(shape)

            def inverse(out, in_):
                step(nc.vector.reciprocal(out, in_))

            v.wait_ge(s_const, 16)
            for t, (t0, n) in enumerate(TILES):
                v.wait_ge(s_ssq, t + 1)
                inverse(sc[0:n, 3 + t:4 + t], sc[0:n, t:t + 1])
                TS(x[0:n, t, :], x[0:n, t, :], sc[0:n, 3 + t:4 + t], None, ALU.mult).then_inc(s_xn, 1)

            lr_, li_ = prm_in[:, 0, :], prm_in[:, 1, :]
            v.wait_ge(s_dt, 1)
            step(CP(pw[:, 0, :].rearrange("p (a q) -> p a q", a=2), bc(logdt[:, 2:4], 2, [16, 2, 64])))
            TT(pw[:, 1, :], lr_, pw[:, 0, :], ALU.mult).then_inc(s_lre, 1)
            step(STT(pw[:, 2, :], li_, 1.0 / (2 * math.pi), pw[:, 0, :], ALU.mult, ALU.mult))
            step(TS(pw[:, 3, :], pw[:, 2, :], RND, RND, ALU.add, ALU.subtract))
            TT(prm[:, 1, :], pw[:, 2, :], pw[:, 3, :], ALU.subtract).then_inc(s_fr, 1)
            lw = pw[:, 7:9, :]
            v.wait_ge(s_par, 16 * 19)
            step(TT(lamv[:, 0:3:2, :], lamv[:, 0:3:2, :], lamv[:, 1:4:2, :], ALU.mult))
            nc.vector.tensor_reduce(sc[:, 6:8], lamv[:, 0:3:2, :], AX.X, ALU.add).then_inc(s_lamd, 1)
            v.wait_ge(s_lame, 1)
            step(TT(sc[:, 10:11], sc[:, 8:9], sc[:, 9:10], ALU.subtract))
            step(TS(sc[:, 11:12], sc[:, 10:11], LAM_INIT, -1.0, ALU.add, ALU.mult))
            v.wait_ge(s_mag, 1)
            v.wait_ge(s_trig, 1)
            mag, sin1, cos1 = prm[:, 0, :], pw[:, 4, :], pw[:, 6, :]
            are, aim, t7, t8, den = pw[:, 7, :], pw[:, 8, :], pw[:, 9, :], pw[:, 10, :], pw[:, 11, :]
            step(TT(are, mag, cos1, ALU.mult))
            step(TS(are, are, -1.0, None, ALU.add))
            step(TT(aim, mag, sin1, ALU.mult))
            step(TT(t7, lr_, lr_, ALU.mult))
            step(TT(t8, li_, li_, ALU.mult))
            step(TT(t7, t7, t8, ALU.add))
            step(nc.vector.reciprocal(den, t7))
            step(TT(t7, are, lr_, ALU.mult))
            step(TT(t8, aim, li_, ALU.mult))
            step(TT(t7, t7, t8, ALU.add))
            step(TT(prm[:, 2, :], t7, den, ALU.mult))
            step(TT(t7, aim, lr_, ALU.mult))
            step(TT(t8, are, li_, ALU.mult))
            step(TT(t7, t7, t8, ALU.subtract))
            TT(prm[:, 3, :], t7, den, ALU.mult).then_inc(s_prm, 1)

            at_h = 0
            for t, (t0, n) in enumerate(TILES):
                for half in range(2 if n == 128 else 1):
                    b = job("hT", at_h)
                    kk = 4 if n == 128 else 8
                    CP(hT[:, 4 * half:4 * half + kk, t0:t0 + n], b[:, 0:kk * n].rearrange("p (k q) -> p k q", k=kk)
                       ).then_inc(dve_done, 1)
                    at_h += 1
            b = job("vec", 0)
            v.wait_ge(dve_done, 5)
            step(CP(vecT[:, :], b[:, 0:32]))
            TT(hT[:, :, :], hT[:, :, :], bc(vecT[:, 0:8], 2, [P, KD, T]), ALU.mult).then_inc(dve_done, 1)
            b = job("prm", 0)
            step(CP(prmT[:, :, :], b[:, 0:64].rearrange("p (i j) -> p i j", i=4)))
            v.sem_inc(dve_done, 1)
            b = job("x0", 0)
            CP(x0T[:, :, :, :].rearrange("p c b j -> p c (b j)"), b[:, 0:256].rearrange("p (c r) -> p c r", c=2)).then_inc(dve_done, 1)

            step(nc.vector.memset(at(I0, 4096), 0.0))
            fre, fim = bc(prmT[:, 2, :], 2, [P, NJ, GH]), bc(prmT[:, 3, :], 2, [P, NJ, GH])
            for c, (pad, ta, tb, op) in enumerate([(padr, 0, 1, ALU.subtract), (padi, 1, 0, ALU.add)]):
                step(TT(t16a, bin_[:, ta], fre, ALU.mult))
                step(TT(t16b, bin_[:, tb], fim, ALU.mult))
                pv = pad[:, :, :].rearrange("p (c j) q -> p c j q", c=NCT)
                ta4, tb4 = (q.rearrange("p (c j) h -> p c j h", c=NCT) for q in (t16a, t16b))
                for a in range(2):
                    for j in range(4):
                        o = (2 * j + a) * GH
                        pr = slice(64 * a, 64 * a + 64)
                        ins = TT(pv[pr, :, j, o:o + GH], ta4[pr, :, j, :], tb4[pr, :, j, :], op)
                step(ins)
            v.sem_inc(s_Bpad, 1)

            qt = at(I0 + 4096, 4, 256)
            for t, (t0, n) in enumerate(TILES):
                cs, sn_ = (C(q, n)[:, t * 32:(t + 1) * 32].unsqueeze(1).to_broadcast([n, 8, 32]) for q in ("ropec", "ropes"))
                for c in range(3):
                    b = job("qkv", 3 * t + c)
                    if c == 2:
                        CP(vt[0:n, t, :], b[0:n, :]).then_inc(dve_done, 1)
                        continue
                    pv = b[0:n, :].rearrange("p (g w i) -> p g w i", w=2, i=32)
                    qv = qk[0:n, c, t, :].rearrange("p (g w i) -> p g w i", w=2, i=32)
                    ta, tb, tc, td = (qt[0:n, i, :].rearrange("p (g i) -> p g i", i=32) for i in range(4))
                    TT(ta, pv[:, :, 0, :], cs, ALU.mult)
                    TT(tb, pv[:, :, 1, :], sn_, ALU.mult)
                    TT(tc, pv[:, :, 1, :], cs, ALU.mult)
                    step(TT(td, pv[:, :, 0, :], sn_, ALU.mult))
                    TT(qv[:, :, 0, :], ta, tb, ALU.subtract)
                    step(TT(qv[:, :, 1, :], tc, td, ALU.add))
                    v.sem_inc(dve_done, 1)
            v.wait_ge(vs, n_step[0])
            v.sem_inc(s_kvtok, 1)

            for i in range(8):
                b = job("B", i)
                CP(bbT[:, i // 4, 4 * (i % 4):4 * (i % 4) + 4, :], b.rearrange("p (j q) -> p j q", j=4)).then_inc(dve_done, 1)
            for c in range(2):
                b = job("C", c).rearrange("p (c q) -> p c q", c=NCT)
                pv = (padr, padi)[c][:, :, :].rearrange("p (c j) q -> p c j q", c=NCT)
                for a in range(2):
                    for j in range(4):
                        o = (2 * j + a) * GH
                        pr = slice(64 * a, 64 * a + 64)
                        ins = TS(pv[pr, :, j, o:o + GH], b[pr, :, o:o + GH], 1.0 if c == 0 else -1.0, None, ALU.mult)
                ins.then_inc(dve_done, 1)

            v.wait_ge(act_done, ACT_JOB["z0"])
            for k in range(8):
                v.wait_ge(freed[k], 1)
            for ct in range(NCT):
                J = slice(4 * ct, 4 * ct + 4)
                tau = C("tau").unsqueeze(1).to_broadcast([P, 4, W5])
                fr = bc(prmT[:, 1, J], 2, [P, 4, W5])
                step(TT(t2, tau, fr, ALU.mult))
                step(TS(t4, t2, RND, RND, ALU.add, ALU.subtract))
                TT(cosT, t2, t4, ALU.subtract).then_inc(s_angT, 1)
                TT(dec, C("keep").unsqueeze(1).to_broadcast([P, 4, W5]), bc(prmT[:, 0, J], 2, [P, 4, W5]), ALU.mult)
                for c, z in enumerate((zr, zi)):
                    ins = CP(z[:, :, SEQ:W5].rearrange("p j (b s) -> p j b s", s=NS + 1)[:, :, :, 0],
                             x0T[:, c, :, J].rearrange("p b j -> p j b"))
                step(ins)
                v.wait_ge(s_tabT, ct + 1)
                v.wait_ge(act_done, ACT_JOB[f"z{ct}"] + 8)
                if ct:
                    v.wait_ge(dve_full, DVE_JOB["y"] + ct)
                TT(t1, cosT, zr, ALU.mult)
                TT(t2, sinT, zi, ALU.mult)
                TT(t3, cosT, zi, ALU.mult)
                step(TT(t4, sinT, zr, ALU.mult))
                TT(t1, t1, t2, ALU.add)
                step(TT(t3, t3, t4, ALU.subtract))

                def flat(a):
                    return a.rearrange("p j w -> p (j w)")
                nc.vector.tensor_tensor_scan(flat(zr), flat(dec), flat(t1), 0.0, ALU.mult, ALU.add)
                step(nc.vector.tensor_tensor_scan(flat(zi), flat(dec), flat(t3), 0.0, ALU.mult, ALU.add))
                TT(t1, cosT, zr, ALU.mult)
                TT(t2, sinT, zi, ALU.mult)
                TT(t3, cosT, zi, ALU.mult)
                step(TT(t4, sinT, zr, ALU.mult))
                v.sem_inc(s_zfree, 1)
                TT(t1, t1, t2, ALU.subtract)
                step(TT(t3, t3, t4, ALU.add))
                v.sem_inc(s_xT5, 1)
                for c, q in enumerate((t1, t3)):
                    CP(finp[:, c, J], q[:, :, SEQ - 1])
                    ins = CP(fins[:, c, :, J].rearrange("p b j -> p j b"),
                             q[:, :, SEQ:W5].rearrange("p j (b s) -> p j b s", s=NS + 1)[:, :, :, NS])
                step(ins)
                b = job("y", ct)
                d = vecT[:, 28 + ct:29 + ct]
                if ct == 0:
                    v.wait_ge(s_zero, 16)
                STT(yT[:, ct, 0:SEQ], uT[:, ct, 0:SEQ], d, b[:, 0:SEQ], ALU.mult, ALU.add)
                step(STT(yT[:, ct, SEQ:T].rearrange("p (b s) -> p b s", s=NS), uT[:, ct, SEQ:T].rearrange("p (b s) -> p b s", s=NS),
                         d, b[:, SEQ:W5].rearrange("p (b s) -> p b s", s=NS + 1)[:, :, 1:], ALU.mult, ALU.add))
                v.sem_inc(dve_done, 1)
            v.sem_inc(s_s5, 1)
            b = job("fin", 0)
            CP(frow[0:NJ, 0:2, :], b[0:NJ, 0:256].rearrange("p (c q) -> p c q", c=2))
            step(CP(frow[:, 2:4, :], b[:, 256:512].rearrange("p (c q) -> p c q", c=2)))
            v.sem_inc(s_fin, 1)
            v.sem_inc(dve_done, 1)

            v.wait_ge(act_full, ACT_JOB["wT"])
            step(nc.vector.memset(qz, 0.0))
            for t, (t0, n) in enumerate(TILES):
                b = job("qk", 2 * t)[:, 0:H * n].rearrange("p (h q) -> p h q", h=H)
                CP(qz[0:64, :, 0, t0:t0 + n], b[0:64])
                CP(qz[64:128, :, 1, t0:t0 + n], b[64:128]).then_inc(dve_done, 1)
                b = job("qk", 2 * t + 1)[:, 0:H * n].rearrange("p (h q) -> p h q", h=H)
                CP(kT[:, :, t0:t0 + n], b).then_inc(dve_done, 1)

            def p_first(n):
                w = 128 * (n // 4 + 1)
                b = job("s", n)[:, 0:2 * w].rearrange("p (c k) -> p c k", c=2)
                m = C("causal")[:, 256 - w:256].unsqueeze(1).to_broadcast([P, 2, w])
                step(TT(pS[:, n % 2, :, 0:w], b, m, ALU.add))
                v.sem_inc(dve_done, 1)
                step(nc.vector.tensor_reduce(st4[:, n % 2, 0:2], pS[:, n % 2, :, 0:w], AX.X, ALU.max))
                step(TS(st4[:, n % 2, 0:2], st4[:, n % 2, 0:2], -SCALE, None, ALU.mult))
                v.sem_inc(s_nb, 1)

            def p_second(n):
                w = 128 * (n // 4 + 1)
                v.wait_ge(s_pexp, n + 1)
                if n >= 2:
                    v.wait_ge(act_full, ACT_JOB["wT"] + n - 1)
                r = st4[:, 2 + n % 2, 0:2]
                step(nc.vector.reciprocal(r, st4[:, n % 2, 2:4]))
                step(TT(r[:, 1:2], r[:, 1:2], sc[:, 11:12], ALU.mult))
                step(TS(pW[:, n % 2, 0:w], pE[:, n % 2, 0, 0:w], r[:, 0:1], None, ALU.mult))
                STT(pW[:, n % 2, 0:w], pE[:, n % 2, 1, 0:w], r[:, 1:2], pW[:, n % 2, 0:w], ALU.mult, ALU.add).then_inc(s_w, 1)

            p_first(0)
            for n in range(8):
                if n + 1 < 8:
                    p_first(n + 1)
                p_second(n)
                if n in (4, 7):
                    i = n // 5
                    v.wait_ge(s_pv, 4 * (i + 1))
                    CP(ot[:, i, :], psum[:, 7, :]).then_inc(s_pvr, 1)
            v.wait_ge(s_late, 64)
            step(TS(subg, subg, 1.0 - LAM_INIT, None, ALU.mult))

            def head_norm(t, n):
                o = ot[0:n, t, :].rearrange("p (h d) -> p h d", h=H)
                sq = tmp2[0:n, :].rearrange("p (h d) -> p h d", h=H)
                step(TT(sq, o, o, ALU.mult))
                nc.vector.tensor_reduce(st4[0:n, 0, :], sq, AX.X, ALU.add).then_inc(s_hsum, 1)
                v.wait_ge(s_hrms, t + 1)
                inverse(st4[0:n, 1, :], st4[0:n, 2, :])
                step(TT(o, o, bc(st4[0:n, 1, :], 2, [n, H, DV]), ALU.mult))
                TT(o, o, subg[0:n, :].unsqueeze(1).to_broadcast([n, H, DV]), ALU.mult).then_inc(s_ln, 1)

            v.wait_ge(s_pvr, 2)
            STEPS = 6

            def cstep(ins, base, k):
                ins.then_inc(s_chain, 1)
                v.wait_ge(s_chain, base + (k + 1))

            def q_block(i):
                if not isinstance(i, int):
                    v.wait_ge(s_sc, i)
                CP(qb[:, :, :].rearrange("p h (c s) -> p h c s", c=2), qz[:, :, :, ds(i * NS + SEQ, NS)]).then_inc(s_qb, 1)

            def copy_max(i, base, k):
                v.wait_ge(s_sc, i + 1)
                cstep(CP(s_sb.rearrange("p g c -> p (g c)"), psum[:, 4, :]), base, k)
                cstep(TT(sn[:, :], psum[0:NSMP, 5, 0:32], C("newmask", NSMP)[:, ds(i * 32, 32)], ALU.add), base, k + 1)
                nc.vector.tensor_reduce(mx[:, :], s_sb.rearrange("p g c -> p c g"), AX.X, ALU.max).then_inc(s_mx, 1)

            def softmax(j, base, k):
                v.wait_ge(s_mxT, j + 1)
                cstep(nc.vector.tensor_reduce(mcol, psum[0:32, 6, 0:160], AX.X, ALU.max), base, k)
                TS(diag, ident[0:32, 0:32], mcol[:, 0:1], None, ALU.mult).then_inc(s_diag, 1)
                v.wait_ge(s_mb, j + 1)
                TT(s_sb, s_sb, psum[:, 6, 160:192].unsqueeze(1).to_broadcast([P, NPG, 32]), ALU.subtract)
                cstep(TT(sn[:, :], sn[:, :], psum[0:32, 6, 160:192], ALU.subtract), base, k + 1)
                v.sem_inc(s_sh, 1)
                v.wait_ge(s_ex, j + 1)
                nc.vector.tensor_reduce(Es, E.rearrange("p g c -> p c g"), AX.X, ALU.add).then_inc(s_Es, 1)

            def finish(j, base, k):
                v.wait_ge(s_den, j + 1)
                cstep(nc.vector.reciprocal(rden, psum[:, 6, 192:224]), base, k)
                v.wait_ge(s_dpv, j + 1)
                cstep(TT(on.rearrange("p h c s -> p (h c s)"), psum[:, 7, 0:32], rden, ALU.mult), base, k + 1)
                STT(oTs[:, :, ds(j * NS, NS)], on[:, :, 1, :], sc[:, 11:12], on[:, :, 0, :], ALU.mult, ALU.add).then_inc(s_do, 1)

            for t in range(2):
                head_norm(t, 128)
            q_block(0)
            copy_max(0, 0, 0)
            with v.Fori(1, NB) as i:
                base = (i - 1) * STEPS + 2
                q_block(i)
                softmax(i - 1, base, 0)
                copy_max(i, base, 2)
                finish(i - 1, base, 4)
            softmax(NB - 1, 2 + (NB - 1) * STEPS, 0)
            finish(NB - 1, 2 + (NB - 1) * STEPS, 2)

            step(CP(ot[0:NSMP, 2, :], job("oS", 0)[0:NSMP, :]))
            v.sem_inc(dve_done, 1)
            head_norm(2, NSMP)
            for t, (t0, n) in enumerate(TILES):
                CP(oT[:, :, t0:t0 + n], job("oT", t)[:, 0:H * n].rearrange("p (h q) -> p h q", h=H)).then_inc(dve_done, 1)
            v.wait_ge(act_done, ACT_JOB["glu"] + 4)
            TT(yT, yT, sg, ALU.mult).then_inc(s_yglu, 1)
            for i in range(KD):
                TT(mg[:, i, :], gates[:, i, :], job("bs", i)[:, 0:T], ALU.mult).then_inc(dve_done, 1)
            for i in range(KD):
                step(TT(tmp, gates[:, KD + i, :], job("ba", i)[:, 0:T], ALU.mult))
                v.sem_inc(dve_done, 1)
                step(TT(mg[:, i, :], mg[:, i, :], tmp, ALU.add))
            v.sem_inc(s_mg, 1)
            v.wait_ge(s_xagain, 48)
            for t, (t0, n) in enumerate(TILES):
                for half in range(2):
                    xx = x[0:n, t, half * 512:(half + 1) * 512]
                    step(TT(xx, xx, job("out", 2 * t + half)[0:n, :], ALU.add))
                    v.sem_inc(dve_done, 1)
                v.sem_inc(s_xres, 1)
            for t, (t0, n) in enumerate(TILES):
                v.wait_ge(s_ssq2, t + 1)
                inverse(sc[0:n, 3:4], sc[0:n, t:t + 1])
                step(STT(h2[0:n, t, :], x[0:n, t, :], sc[0:n, 3:4], gvec[0:n, :], ALU.mult, ALU.mult))
                v.sem_inc(s_h2, 1)
            for t, (t0, n) in enumerate(TILES):
                v.wait_ge(s_h2h, t + 1)
                TT(h2s[0:n, 1, t, :], h2[0:n, t, :], h2s[0:n, 0, t, :], ALU.subtract).then_inc(s_h2s, 1)
            at_h = 0
            for t, (t0, n) in enumerate(TILES):
                for half in range(2 if n == 128 else 1):
                    kk = 4 if n == 128 else 8
                    CP(h2T[:, 4 * half:4 * half + kk, t0:t0 + n],
                       job("h2T", at_h)[:, 0:kk * n].rearrange("p (k q) -> p k q", k=kk)).then_inc(dve_done, 1)
                    at_h += 1
            for t, (t0, n) in enumerate(TILES):
                step(TT(lg[0:n, t, :], job("lg", t)[0:n, 0:NE], brt[0:n, :], ALU.add))
                v.sem_inc(dve_done, 1)
                step(nc.vector.max(mx8[0:n, t, :], lg[0:n, t, :]))
                step(nc.vector.max_index(eight[0:n, t, :], mx8[0:n, t, :], lg[0:n, t, :]))
                TS(nmx[0:n, t, :], mx8[0:n, t, 0:1], -1.0, None, ALU.mult).then_inc(s_nmx, 1)
                step(CP(idxf[0:n, t, :], eight[0:n, t, 0:TOPK]))
                step(TT(oneh[0:n, t], C("iota", n)[:, 0:NE].unsqueeze(1).to_broadcast([n, TOPK, NE]),
                        bc(idxf[0:n, t, :], 2, [n, TOPK, NE]), ALU.is_equal))
                step(nc.vector.tensor_reduce(mask[0:n, t, :], oneh[0:n, t].rearrange("p k e -> p e k"), AX.X, ALU.add))
                v.sem_inc(s_mask, 1)
            for t, (t0, n) in enumerate(TILES):
                v.wait_ge(s_gexp, t + 1)
                step(nc.vector.reciprocal(gsum[0:n, t, :], gsum[0:n, t, :]))
                TS(gk[0:n, t, :], gk[0:n, t, :], gsum[0:n, t, :], None, ALU.mult)
            for t, (t0, n) in enumerate(TILES):
                b = job("pos", t)[0:n, 0:NE]
                step(STT(posm[0:n, t, 0:NE], b, 1.0, mask[0:n, t, :], ALU.add, ALU.mult))
                TS(posm[0:n, t, 0:NE], posm[0:n, t, 0:NE], -1.0, None, ALU.add)
                nc.vector.memset(posm[0:n, t, NE:NE + 2], -1.0)
                step(TT(tk[0:n, t], oneh[0:n, t], b.unsqueeze(1).to_broadcast([n, TOPK, NE]), ALU.mult))
                v.sem_inc(dve_done, 1)
                step(nc.vector.tensor_reduce(slotk[0:n, t, :], tk[0:n, t], AX.X, ALU.add))
            step(CP(cnt[:, 0, :], job("cnt", 0)[:, 0:NE]))
            v.sem_inc(dve_done, 1)
            step(TS(cnt[:, 1, :], cnt[:, 0, :], float(CAP), None, ALU.is_gt))
            for m in range(2, 5):
                step(STT(cnt[:, 1, :], cnt[:, 0, :], float(m * CAP), cnt[:, 1, :], ALU.is_gt, ALU.add))
            step(nc.vector.tensor_tensor_scan(cnt[:, 2, :], C("ones")[:, 0:NE], cnt[:, 1, :], 0.0, ALU.mult, ALU.add))
            step(TT(cnt[:, 3, :], cnt[:, 2, :], cnt[:, 1, :], ALU.subtract))
            jobs, full = C("jobs"), [P, NOVER, NE]
            step(TT(ytab, bc(jobs, 2, full), cnt[:, 2, :].unsqueeze(1).to_broadcast(full), ALU.is_ge))
            step(nc.vector.tensor_reduce(jobf[:, 0:NOVER], ytab, AX.X, ALU.add))
            step(TT(ytab, ytab, cnt[:, 1, :].unsqueeze(1).to_broadcast(full), ALU.mult))
            step(nc.vector.tensor_reduce(jobf[:, NOVER:2 * NOVER], ytab, AX.X, ALU.add))
            step(TT(jobf[:, NOVER:2 * NOVER], jobs, jobf[:, NOVER:2 * NOVER], ALU.subtract))
            step(TS(jobf[:, NOVER:2 * NOVER], jobf[:, NOVER:2 * NOVER], 1.0, 4.0, ALU.add, ALU.min))
            step(TS(jobf[:, 0:NOVER], jobf[:, 0:NOVER], NE - 1.0, None, ALU.min))
            step(CP(jobf[:, 2 * NOVER:2 * NOVER + 1], cnt[:, 2, NE - 1:NE]))
            step(CP(jobi[:, :], jobf[:, :]))
            for t, (t0, n) in enumerate(TILES):
                step(TT(tk[0:n, t], oneh[0:n, t], cnt[0:n, 3, :].unsqueeze(1).to_broadcast([n, TOPK, NE]), ALU.mult))
                step(nc.vector.tensor_reduce(basek[0:n, t, :], tk[0:n, t], AX.X, ALU.add))
                step(TS(big[0:n, t, :], slotk[0:n, t, :], float(CAP), None, ALU.is_ge))
                step(STT(basek[0:n, t, :], basek[0:n, t, :], float(NE - 1), idxf[0:n, t, :], ALU.add, ALU.subtract))
                step(TT(basek[0:n, t, :], basek[0:n, t, :], big[0:n, t, :], ALU.mult))
                step(TT(basek[0:n, t, :], basek[0:n, t, :], idxf[0:n, t, :], ALU.add))
                step(STT(rowf[0:n, t, :], basek[0:n, t, :], float(CAP), slotk[0:n, t, :], ALU.mult, ALU.add))
                step(CP(rowi[0:n, t, :], rowf[0:n, t, :]))
            v.wait_ge(s_bias, 64)
            step(CP(bias_s[:, :], braw))
            step(TT(bias_s[32:64, :], braw[32:64, :], bias_s[32:64, :], ALU.subtract))
            v.sem_inc(s_bsplit, 1)
            v.sem_inc(s_route, 1)

            def select(j, e, t=None, shift=0):
                if not (isinstance(j, int) and j == 0):
                    v.wait_ge(e_gath, j + shift)
                for s, (t0, n) in enumerate(TILES):
                    if t is None:
                        ins = TS(sel[0:n, s, :], C("iota", n), posm[0:n, s, ds(e, 1)], None, ALU.is_equal)
                    else:
                        ins = TS(sel[0:n, s, :], C("iota", n), C("tile0", n)[:, ds(t, 1)], posm[0:n, s, ds(e, 1)],
                                 ALU.add, ALU.is_equal)
                ins.then_inc(e_sel, 1)

            def bias_row(out, e, done):
                TS(out[:, :], C("upper", 64), C("expert", 64)[:, ds(e, 1)], None, ALU.mult).then_inc(done, 1)

            def low(q, i):
                if i in POOL_CHUNKS:
                    return
                v.wait_ge(c_hi, q * 12 + (i - 3))
                TT(wlo[:, i % NSPLIT, :], ring[:, chunk_raw(i), :], whi[:, i % NSPLIT, :], ALU.subtract).then_inc(c_lov, 1)

            def clamp(j):
                v.wait_ge(e_guL, j + 1)
                TT(gus.rearrange("p (b n) -> p b n", b=4), psum[0:CAP, 0:4, :], guL.rearrange("p (b n) -> p b n", b=4),
                   ALU.add).then_inc(e_sum, 1)
                v.wait_ge(e_sum, j + 1)
                TS(gg, gus[:, 0::2], LIMIT, None, ALU.min).then_inc(e_g, 1)
                TS(uu, gus[:, 1::2], LIMIT, -LIMIT, ALU.min, ALU.max).then_inc(e_u, 1)

            def activate(j):
                v.wait_ge(e_sig, j + 1)
                v.wait_ge(e_u, j + 1)
                TT(gg, gg, sig, ALU.mult).then_inc(e_m, 1)
                v.wait_ge(e_m, j + 1)
                STT(xa[CAP:P, :], uu, 1.0, gg, ALU.add, ALU.mult).then_inc(e_act, 1)

            def low_x(j, shift=0):
                v.wait_ge(e_xh, j + (1 + shift))
                TT(xs_[:, :, CAP:], turned_x, xs_[:, :, 0:CAP], ALU.subtract).then_inc(e_xs, 1)

            def low_a(j):
                v.wait_ge(e_ah, j + 1)
                TT(as2[:, :, CAP:], turned_a, as2[:, :, 0:CAP], ALU.subtract).then_inc(e_as, 1)

            def sum_y(j):
                v.wait_ge(e_yL, j + 1)
                v.wait_ge(e_out, j * 16)
                TT(yS.rearrange("p (b n) -> p b n", b=2), psum[0:CAP, 4:6, :], yL.rearrange("p (b n) -> p b n", b=2),
                   ALU.add).then_inc(e_y, 1)

            step(nc.vector.memset(xa[CAP:P, :], 0.0))
            select(0, 0)
            bias_row(bsg, 0, e_bg)
            bias_row(bsd, 0, e_bd)
            for c in range(NSPLIT):
                low(0, 4 + c)
            low_x(0)
            select(1, 1)
            for c in range(NSPLIT, 6):
                low(0, 4 + c)
            select(2, 2)
            for c in range(6, 8):
                low(0, 4 + c)
            clamp(0)
            bias_row(bsg, 1, e_bg)
            low_x(1)
            low(1, 0)
            activate(0)
            low(1, 1)
            with v.Fori(1, NE) as j:
                for i in (2, 3, 4, 5):
                    low(j, i)
                select(j + 2, j + 2)
                low(j, 6)
                low_a(j - 1)
                for i in (7, 8, 9, 10):
                    low(j, i)
                clamp(j)
                bias_row(bsg, j + 1, e_bg)
                low_x(j + 1)
                low(j, 11)
                activate(j)
                low(j + 1, 0)
                low(j + 1, 1)
                sum_y(j - 1)
                bias_row(bsd, j, e_bd)
            low_a(NE - 1)
            for i in (2, 3):
                low(NE, i)
            sum_y(NE - 1)
            most = extra_jobs(v)
            with v.Fori(0, NOVER) as o:
                with v.If(most > o):
                    j = v.snap(o + NE)
                    e = v.value_load(jobi[0:1, ds(o, 1)], min_val=0, max_val=NE - 1)
                    t = v.value_load(jobi[0:1, ds(o + NOVER, 1)], min_val=0, max_val=4)
                    select(j, e, t, 1)
                    bias_row(bsg, e, e_bg)
                    bias_row(bsd, e, e_bd)
                    low_x(j, 1)
                    for c in range(12):
                        if c == 10:
                            clamp(j)
                            activate(j)
                            low_a(j)
                        low(o + (NE + (c + 4) // 12), (c + 4) % 12)
                    sum_y(j)
                with v.Else():
                    v.wait_ge(s_route, 1)

            for t, (t0, n) in enumerate(TILES):
                v.wait_ge(s_gath[t], 16 * TOPK)
                for k in range(TOPK):
                    step(STT(x[0:n, t, :], ycomb[0:n, t, k, :], gk[0:n, t, k:k + 1], x[0:n, t, :], ALU.mult, ALU.add))
                v.sem_inc(s_comb, 1)
            v.wait_ge(s_gfin, 16)
            for t, (t0, n) in enumerate(TILES):
                v.wait_ge(s_ssq2, 3 + t + 1)
                inverse(sc[0:n, 3:4], sc[0:n, t:t + 1])
                step(STT(x[0:n, t, :], x[0:n, t, :], sc[0:n, 3:4], gvec[0:n, :], ALU.mult, ALU.mult))
                v.sem_inc(s_ynorm, 1)


_UNUSED = ()
_OUTS = [
    ("o_y_prompt", (1, SEQ, D)), ("o_y_sample", (NB, NS, D)),
    ("o_k_prompt", (1, 1, SEQ, H, DV)), ("o_v_prompt", (1, 1, SEQ, H, DV)),
    ("o_re_prompt", (1, 1, G, SP_)), ("o_im_prompt", (1, 1, G, SP_)),
    ("o_k_sample", (1, NB, NS, H, DV)), ("o_v_sample", (1, NB, NS, H, DV)),
    ("o_re_sample", (1, NB, G, SP_)), ("o_im_sample", (1, NB, G, SP_)),
]


def kernel(**inputs):
    import concourse.bacc as bacc
    from concourse.bass_utils import run_bass_kernel_spmd as run

    nc = bacc.Bacc("TRN2", target_bir_lowering=False, num_devices=1)
    arrays, A = {}, {}
    for name, a in {**inputs, "consts": constants()}.items():
        arrays[f"in_{name}"] = a = np.ascontiguousarray(a)
        A[name] = nc.dram_tensor(f"in_{name}", a.shape, mybir.dt.from_np(a.dtype), kind="ExternalInput").ap()
    for name, shape in _OUTS:
        A[name] = nc.dram_tensor(name, shape, F32, kind="ExternalOutput").ap()
    build(nc, A)
    r = run(nc, [arrays], core_ids=[0])
    return tuple(r.results[0][name] for name, _ in _OUTS)
```

```python
import math
from contextlib import ExitStack

import numpy as np

import concourse.bass as bass
from concourse import mybir

ALU = mybir.AluOpType
ACT = mybir.ActivationFunctionType
AX = mybir.AxisListType
F32 = mybir.dt.float32
I32 = mybir.dt.int32
U32 = mybir.dt.uint32
ds = bass.ds

P = 128
D = 1024
KD = D // P
SEQ = 256
NB = 8
NS = 4
NSMP = NB * NS
T = SEQ + NSMP
TILES = [(0, 128), (128, 128), (256, 32)]
PAST = 2048
PAGE = 128
NPG = PAST // PAGE
H = 4
DV = 128
HD = 64
QC = 2 * NS
G, GH, SP_ = 32, 16, 64
NJ = G * SP_ // P
NCT = 4
W5 = SEQ + NB * (NS + 1)
NE = 32
TOPK = 4
CAP = 64
NOVER = 17
NJOB = NE + NOVER
LIMIT = 7.0
ALPHA = 1.702
EPS = 1e-6
LAM_INIT = 0.8 - 0.6 * math.exp(0.0)
RND = 12582912.0
SCALE = HD ** -0.5
NEG = -1e30
NSLOT = 12
E_STEP = 2
V_STEP = {3: (0, 3), 4: (3, 6), 5: (6, 9), 6: (9, 12), 7: (12, 16)}
N_SMALL = 15

CONST_COLS = {}
_at = 0
for _name, _n in [("ident", 128), ("tri", 128), ("iota", CAP), ("ropec", 96), ("ropes", 96), ("tau", W5), ("keep", W5),
                  ("causal", 256), ("newmask", NB * NSMP), ("ones", 128), ("tile0", 5), ("expert", NE + 1),
                  ("upper", P), ("jobs", NOVER)]:
    CONST_COLS[_name] = (_at, _n)
    _at += _n
NCONST = _at


def constants():
    c = np.zeros((P, NCONST), np.float32)

    def put(name, a):
        o, n = CONST_COLS[name]
        c[:a.shape[0], o:o + n] = a.reshape(a.shape[0], n)

    i = np.arange(P)
    put("ident", np.eye(P))
    put("tri", (i[:, None] < i[None, :]).astype(np.float32))
    put("iota", np.broadcast_to(np.arange(CAP), (P, CAP)))
    pos = np.concatenate([np.arange(SEQ), np.tile(PAST + np.arange(NS), NB)]).astype(np.float32)
    half = HD // 2
    inv = (np.float32(10000.0) ** (-np.arange(half, dtype=np.float32) / np.float32(half))).astype(np.float32)
    ang = (pos[:, None] * inv[None, :]).astype(np.float32)
    rc, rs = np.zeros((P, 3, half)), np.zeros((P, 3, half))
    for t, (t0, n) in enumerate(TILES):
        rc[:n, t], rs[:n, t] = np.cos(ang[t0:t0 + n].astype(np.float64)), np.sin(ang[t0:t0 + n].astype(np.float64))
    put("ropec", rc)
    put("ropes", rs)
    put("tau", np.broadcast_to(np.concatenate([np.arange(1, SEQ + 1), np.tile(np.arange(NS + 1), NB)]), (P, W5)))
    keep = np.ones(W5)
    keep[0] = 0
    keep[SEQ::NS + 1] = 0
    put("keep", np.broadcast_to(keep, (P, W5)))
    causal = np.zeros((P, 256))
    causal[:, 128:] = np.where(i[None, :] <= i[:, None], 0, NEG)
    put("causal", causal)
    key = np.arange(NSMP)
    m = np.full((H, 2, NS, NB, NSMP), NEG)
    for b in range(NB):
        for q in range(NS):
            m[:, :, q, b, (key // NS == b) & (key % NS <= q)] = 0
    put("newmask", m.reshape(H * QC, NB * NSMP))
    put("ones", np.ones((P, 128)))
    put("tile0", np.broadcast_to(np.arange(5) * CAP, (P, 5)))
    put("expert", (np.arange(64)[:, None] % NE == np.arange(NE + 1)[None, :]).astype(np.float32))
    put("upper", np.broadcast_to((i < CAP).astype(np.float32), (64, P)))
    put("jobs", np.broadcast_to(np.arange(NOVER), (P, NOVER)))
    return c


RING = [(f"w_in{k}", k, 1, 1) for k in range(8)]
RING += [(f"w_gate{k}", (8 + k) % 12, 1, 1) for k in range(8)]
RING += [(f"K{s}", s, 4, NB) for s in range(4)] + [(f"V{s}", 4 + s, 4, NB) for s in range(4)]
RING += [("w_glu", 8, 1, 1), ("w_bs0", 9, 1, 1), ("w_bs1", 10, 1, 1), ("w_ba0", 11, 1, 1), ("w_ba1", 0, 1, 1)]
RING += [(f"w_out{k}", 1 + k, 1, 1) for k in range(4)]
SLOT, USE0, LOAD0, NDMA = {}, {}, {}, {}
_uses, _loads = [0] * NSLOT, [0] * NSLOT
for _name, _s, _d, _r in RING:
    SLOT[_name], USE0[_name], LOAD0[_name], NDMA[_name] = _s, _uses[_s], _loads[_s], _d
    _uses[_s] += _r
    _loads[_s] += 16 * _d * _r


NRAW, NSPLIT = 6, 3
RAW0 = NSLOT - NRAW
POOL_CHUNKS = (3, 6, 11)


def chunk_raw(i):
    return RAW0 + i % NRAW


def chunk_loaded(q, i):
    return (q * 2 + (i // NRAW - (i % NRAW < 4))) * 16 + (_loads[chunk_raw(i)] + 16)


def chunk_used(q, i):
    return q * 12 + (i - 3)


def chunk_low(q, i):
    pool = i in POOL_CHUNKS
    mine = [k for k in range(12) if (k in POOL_CHUNKS) == pool]
    return pool, q * len(mine) + (mine.index(i) + 1 - sum(k < 4 for k in mine))


def loaded_at(name, i=0):
    return LOAD0[name] + 16 * NDMA[name] + i * (16 * NDMA[name])


def free_at(name, i=0):
    return USE0[name] + i


def numbered(stages):
    at, out = 0, {}
    for name, n in stages:
        out[name] = at
        at += n
    return out


ACT_JOB = numbered([("u", 4), ("z0", 8)] + [q for ct in range(4) for q in (
    [(f"gate{ct}", 4)] + [(f"z{ct + 1}", 8)] * (ct < 3))] + [("wT", 8), ("glu", 4), ("end", 0)])
DVE_JOB = numbered([("hT", 5), ("vec", 1), ("qkv0", 6), ("prm", 1), ("x0", 1), ("qkv", 3), ("B", 8), ("C", 2), ("y", 4), ("fin", 1),
                    ("qk", 6), ("s", 8), ("oS", 1), ("oT", 3), ("bs", 8), ("ba", 8), ("out", 6), ("h2T", 5), ("lg", 3),
                    ("pos", 3), ("cnt", 1), ("end", 0)])


def build(nc, A):
    with ExitStack() as ctx:
        def sb(name, shape, dt=F32):
            return ctx.enter_context(nc.sbuf_tensor(name, shape, dt))

        def sem(name):
            return ctx.enter_context(nc.semaphore(name))

        psum = ctx.enter_context(nc.psum_tensor("psum", [P, 8, 512], F32))
        def base():
            return (nc.sbuf_base + 31) // 32 * 32

        ring_at = base()
        ring = sb("ring", [P, NSLOT, 2048])
        arena_at = base()
        arena = sb("arena", [P, 25568])

        def rounded(name, byte, shape):
            return nc.alloc_sbuf_tensor_at(name, shape, mybir.dt.float32r, offset=byte)

        cst = sb("cst", [P, NCONST])
        ydram = nc.dram_tensor("expert_rows", (NJOB * CAP, D), F32, kind="Internal").ap()

        def C(name, n=P):
            o, w = CONST_COLS[name]
            return cst[0:n, o:o + w]

        ident, ones = C("ident"), C("ones")

        def at(off, *dims, n=P):
            size = math.prod(dims)
            v = arena[0:n, off:off + size]
            if len(dims) == 1:
                return v
            names = [f"d{i}" for i in range(len(dims))]
            return v.rearrange(f"p ({' '.join(names)}) -> p {' '.join(names)}", **dict(zip(names, dims)))

        hT = at(0, KD, T)
        qz = at(0, H, 2, T)
        h2T = at(0, KD, T)
        x = at(2304, 3, D)
        qk = at(2304, 2, 3, 512)
        vt = at(5376, 3, 512)
        uT = at(6912, NCT, T)
        oth = 8064
        gates = at(oth, 16, T)
        h2 = at(oth, 3, D)
        yT = at(12672, NCT, T)
        I0 = 13824
        padr, padi = at(I0, NJ, P), at(I0 + 2048, NJ, P)
        bbT = at(I0 + 4096, 2, NJ, P)
        rows = at(oth, P)
        prm_in = at(oth + 128, 2, P, n=16)
        logdt = at(oth + 384, 4, n=16)
        pw = at(oth + 400, 12, P, n=16)
        prm = at(oth + 2000, 4, P, n=16)
        lamv = at(oth + 2512, 4, HD)
        x0rows = at(oth + 2768, 2, P)
        bin_ = at(oth + 3024, 2, NJ, GH)
        cdup = at(oth + 3536, 2, NCT, P)
        t16a = at(I0 + 8192 - 1024, NJ, GH)
        t16b = at(I0 + 8192 - 512, NJ, GH)
        normj = at(I0, D)
        K0 = I0 + 8192
        cosT, sinT, dec = at(K0, 4, W5), at(K0 + 1184, 4, W5), at(K0 + 2368, 4, W5)
        kT = at(K0, H, T)
        gvec = at(K0 + 1152, D)
        wr = at(K0 + 2176, KD, NE)
        brt = at(K0 + 2432, NE)
        subg = at(K0 + 2464, DV)
        frow = at(K0 + 2592, 4, P)
        sw = ring[:, 4:8, :].rearrange("p s n -> p (s n)")
        S5 = [sw[:, i * 1184:(i + 1) * 1184].rearrange("p (j w) -> p j w", j=4) for i in range(6)]
        zr, zi, t1, t2, t3, t4 = S5
        pS = at(I0, 2, 2, 256)
        pE = at(I0 + 1024, 2, 2, 256)
        pW = at(I0 + 2048, 2, 256)
        pWT = at(I0 + 2560, 2, 2, P)
        keyh = rounded("keys_high", arena_at + 4 * 2304, [P, 2, H, 2 * P])
        keyl = rounded("keys_low", arena_at + 4 * (I0 + 3072), [P, 2, H, 2 * P])
        valh = rounded("values_high", arena_at + 4 * I0, [P, 3, 512])
        vall = rounded("values_low", arena_at + 4 * (I0 + 1536), [P, 3, 512])
        e2 = rounded("exps_split", arena_at + 4 * 6912, [P, NPG + 1, 2 * NSMP])
        vnh = rounded("new_values_high", arena_at + 4 * (I0 + 5120), [NSMP, 512])
        vnl = rounded("new_values_low", arena_at + 4 * (I0 + 5632), [NSMP, 512])
        oL = at(4352, 512, n=32)
        oS = at(4864, 512, n=32)
        ss = ring[0:32, 11, :]
        E = ring[0:32, 10, :]
        sm = I0 + 6144
        snw = at(sm, 32, n=32)
        En = at(sm + 32, 32, n=32)
        mx5 = at(sm + 64, 5, n=32)
        mcol = at(sm + 69, 1, n=32)
        nbias = at(sm + 70, 1, n=32)
        esum = at(sm + 71, 2, n=32)
        etot = at(sm + 73, 1, n=32)
        rden = at(sm + 74, 1, n=32)
        on = at(sm + 228, H, 2, NS)
        oTs = at(sm + 260, H, NSMP)
        st4 = at(sm + 388, 4, 4)
        ot = at(I0 + 6656, 3, 512)
        oT = at(I0, H, T)
        mg = at(I0 + 1152, KD, T)
        tmp = at(I0 + 3456, T)
        tmp2 = at(I0 + 2560, 512)
        sg = at(I0 + 4256, NCT, T)
        R = I0 + 6144
        lg = at(R, 3, NE)
        mx8 = at(R + 96, 3, 8)
        idxf = at(R + 120, 3, 4)
        oneh = at(R + 132, 3, TOPK, NE)
        tk = at(R + 516, 3, TOPK, NE)
        mask = at(R + 900, 3, NE)
        posm = at(R + 996, 3, NE + 2)
        slotk = at(R + 1098, 3, 4)
        gk = at(R + 1110, 3, 4)
        nmx = at(R + 1122, 3, 1)
        gsum = at(R + 1125, 3, 1)
        rowf = at(R + 1128, 3, 4)
        big = at(R + 1140, 3, 4)
        basek = at(R + 1152, 3, 4)
        cnt = at(R + 1164, 6, NE)
        ytab = at(5376, NOVER, NE)
        whi = rounded("w_high", ring_at, [P, NSPLIT, 2048])
        wlo = rounded("w_low", ring_at + NSPLIT * 8192, [P, NSPLIT, 2048])
        xs_ = rounded("x_split", arena_at, [P, KD, 2 * CAP])
        as2 = rounded("act_split", arena_at + 4 * 1024, [P, KD, 2 * CAP])
        sel = rounded("selection", arena_at + 4 * 2048, [P, 3, CAP])
        bias_s = rounded("bias_split", arena_at + 4 * 5376, [64, 3 * D])
        bsg = rounded("bias_of_gate_up", arena_at + 4 * 13568, [64, P])
        bsd = rounded("bias_of_down", arena_at + 4 * 13696, [64, P])
        h2s = rounded("h2_split", arena_at + 4 * I0, [P, 2, 3, D])
        braw = at(8448, 3 * D, n=64)
        guL = at(8448, 2 * D, n=CAP)
        sig = at(8448, D, n=CAP)
        xa = at(8448 + D, D)
        gus = at(10496, 2 * D, n=CAP)
        yL = at(10496, D, n=CAP)
        gg = at(12544, D, n=CAP)
        uu = at(K0 + 2176, D, n=CAP)
        yS = arena[CAP:P, 10496:10496 + D]
        zeros = yT.rearrange("p c t -> p (c t)")[0:64, 0:D]
        ycomb = ring[:, 0:6, :].rearrange("p s n -> p (s n)").rearrange("p (t k n) -> p t k n", t=3, k=4)
        junk = at(6912, D)

        eight = sb("eight", [P, 3, 8], U32)
        rowi = sb("rowi", [P, 3, 4], U32)
        jobi = sb("jobi", [P, 2 * NOVER + 1], I32)
        jobf = sb("jobf", [P, 2 * NOVER + 1])
        vecT = sb("vecT", [P, 32])
        qs = rounded("queries_split", arena_at + 4 * (K0 + 3104), [P, 72 * H + 32])
        knh = rounded("new_keys_high", arena_at + 4 * (K0 + 3424), [P, H, NSMP])
        knl = sb("new_keys_low", [P, H, NSMP], mybir.dt.float32r)
        prmT = sb("prmT", [P, 4, NJ])
        x0T = sb("x0T", [P, 2, NB, NJ])
        finp = sb("finp", [P, 2, NJ])
        fins = sb("fins", [P, 2, NB, NJ])
        sc = sb("sc", [P, 16])
        halfpi = sb("halfpi", [P, 1])
        epsc = sb("epsc", [P, 1])
        pages = sb("pages", [1, NB * NPG], I32)

        loaded = [sem(f"loaded{s}") for s in range(NSLOT)]
        freed = [sem(f"freed{s}") for s in range(NSLOT)]
        s_vec = sem("vectors_in")
        s_const, s_x, s_par, s_pages = sem("consts_in"), sem("x_in"), sem("params_in"), sem("pages_in")
        s_late, s_xagain, s_bias, s_gfin = sem("late_params_in"), sem("x_again_in"), sem("biases_in"), sem("final_gain_in")
        s_kvout, s_out, s_yout = sem("kv_written"), sem("outputs_written"), sem("expert_rows_written")
        act_full, act_done = sem("act_bank_full"), sem("act_bank_emptied")
        dve_full, dve_done = sem("dve_bank_full"), sem("dve_bank_emptied")
        vs, as_, ps = sem("vector_step"), sem("scalar_step"), sem("pool_step")
        s_ssq, s_ssq2, s_gelu = sem("squares_summed"), sem("squares2_summed"), sem("gelu_done")
        s_rowf, s_hsum, s_hrms = sem("row_numbers"), sem("head_squares_summed"), sem("head_rms_ready")
        s_rows, s_ynorm, s_chain = sem("expert_rows_ready"), sem("y_normed"), sem("sample_vector_step")
        s_xn, s_dt, s_mag, s_fr, s_trig = sem("x_normed"), sem("dt_ready"), sem("decay_ready"), sem("angle_ready"), sem("trig_ready")
        s_lre = sem("decay_exponent_ready")
        s_prm, s_lamd, s_lame = sem("s5_params_ready"), sem("lambda_dots"), sem("lambda_exps")
        s_Bpad, s_angT, s_tabT, s_zfree, s_xT5, s_x5read = (sem("b_blocks_ready"), sem("table_angles"), sem("tables_ready"),
                                                            sem("z_used"), sem("states_ready"), sem("states_read"))
        s_s5, s_kvtok, s_qzero, s_fin = sem("s5_done"), sem("kv_tokens_ready"), sem("qz_zeroed"), sem("final_states_ready")
        s_nb, s_pexp, s_w, s_wt, s_pv, s_pvr = (sem("prompt_max"), sem("prompt_exps"), sem("prompt_weights"), sem("wT_read"),
                                                sem("prompt_pv"), sem("prompt_pv_read"))
        p_turned, p_keyh, p_keyl, s_group = sem("page_turned"), sem("page_high"), sem("page_low"), sem("group_scored")
        p_valh, p_vall, p_vallv, p_used = (sem("values_page_high"), sem("even_values_page_low"), sem("odd_values_page_low"),
                                           sem("values_page_used"))
        s_qb, s_newkv, s_new, s_low, s_sum, s_nbias, s_ex, s_rden = (
            sem("q_block"), sem("new_kv_split"), sem("new_scores_done"), sem("scores_low_copied"), sem("scores_summed"),
            sem("max_ready"), sem("sample_exps"), sem("denominators"))
        s_eT, s_eh, s_el, s_pvd, s_oL, s_oS, s_oT, s_do = (
            sem("exps_turned"), sem("exps_high"), sem("exps_low"), sem("sample_pv"), sem("pv_low_copied"), sem("pv_summed"),
            sem("pv_turned"), sem("sample_out"))
        s_ln, s_sg, s_yglu, s_mg = sem("heads_normed"), sem("glu_gate"), sem("glu_done"), sem("merged")
        s_h2, s_xres, s_gexp, s_mask, s_route = (sem("h2_ready"), sem("residual_done"), sem("gate_exps"), sem("mask_ready"),
                                                 sem("routing_ready"))
        s_nmx = sem("router_max")
        s_comb, s_gath = sem("combined"), [sem(f"rows_gathered{t}") for t in range(3)]

        s_zero, s_h2h, s_h2s, s_bsplit = (sem("rows_zeroed"), sem("h2_high"), sem("h2_split_done"), sem("bias_split_done"))
        s_tab = sem("job_table_step")
        e_sel, e_bg, e_bd, e_gath, e_xg, e_xh, e_xs = (sem("selection_ready"), sem("gate_bias_row_ready"), sem("down_bias_row_ready"),
                                                             sem("rows_selected"), sem("rows_copied"),
                                                             sem("x_high"), sem("x_split_ready"))
        e_guL, e_sum, e_g, e_u, e_sig, e_m, e_act, e_turn, e_ah, e_as = (
            sem("gate_up_low_copied"), sem("gate_up_summed"), sem("gate_clamped"), sem("up_clamped"), sem("sigmoid_done"),
            sem("gate_times_sigmoid"), sem("activation_ready"), sem("rows_turned"), sem("act_high"), sem("act_split_ready"))
        e_extra = sem("extra_job_done")
        e_yL, e_y, e_out = sem("down_low_copied"), sem("rows_summed"), sem("rows_written")
        c_hi, c_lov, c_lop, c_free = sem("chunk_high"), sem("chunk_low_by_vector"), sem("chunk_low_by_gpsimd"), sem("chunk_used")

        block = ctx.enter_context(nc.Block())

        def slot(name):
            return ring[:, SLOT[name], :]

        def wait_loaded(eng, name, i=0):
            eng.wait_ge(loaded[SLOT[name]], loaded_at(name, i))

        ck = A["cache_k"][0].rearrange("n p h d -> n p (h d)")
        cv = A["cache_v"][0].rearrange("n p h d -> n p (h d)")
        wgu = A["w_gate_up"][0].rearrange("e (k p) n -> e k p n", p=P)
        wdn = A["w_down"][0].rearrange("e (c k p) n -> e c p k n", p=P, k=2)

        turned = psum[:, 6:8, :].rearrange("p b (k c) -> p (b k) c", c=P)
        turned_x, turned_a = turned[:, :, 0:CAP], turned[:, :, CAP:]

        def wait_low(eng, q, i):
            pool, n = chunk_low(q, i)
            eng.wait_ge(c_lop if pool else c_lov, n)

        def extra_jobs(eng):
            eng.wait_ge(s_route, 1)
            return eng.value_load(jobi[0:1, 2 * NOVER:2 * NOVER + 1], min_val=0, max_val=NOVER)

        xp, xs = A["x_prompt"][0], A["x_sample"].rearrange("b s d -> (b s) d")
        xin = [xp[0:128, :], xp[128:256, :], xs]

        @block.sync
        def _(sp):
            def load(name, src, dst=None):
                if free_at(name):
                    sp.wait_ge(freed[SLOT[name]], free_at(name))
                sp.dma_start(slot(name) if dst is None else dst, src).then_inc(loaded[SLOT[name]], 16)

            for t, (t0, n) in enumerate(TILES):
                sp.dma_start(x[0:n, t, :], xin[t]).then_inc(s_x, 16)
            sp.dma_start(pages[:, :], A["page_table"].rearrange("a b -> (a b)").unsqueeze(0)).then_inc(s_pages, 16)
            for k in range(8):
                load(f"w_in{k}", A["w_in"][0, k * P:(k + 1) * P, :])
            for k in range(8):
                load(f"w_gate{k}", A["w_gate"][0, k * P:(k + 1) * P, :])
            sp.wait_ge(s_pages, 16)

            def pages_of(kind, cache, b):
                for s in range(4):
                    name = f"{kind}{s}"
                    sp.wait_ge(freed[SLOT[name]], free_at(name, b))
                    for j in range(4):
                        page = sp.value_load(pages[0:1, ds(b * NPG + (4 * s + j), 1)], min_val=0, max_val=159)
                        sp.dma_start(ring[:, SLOT[name], j * 512:(j + 1) * 512],
                                     cache[ds(page, 1), :, :].rearrange("o p n -> p (o n)")).then_inc(loaded[SLOT[name]], 16)

            pages_of("K", ck, 0)
            load("w_glu", A["ssm_w_glu"][0].rearrange("(k p) n -> p k n", p=P),
                 slot("w_glu").rearrange("p (k n) -> p k n", k=4))
            load("w_bs0", A["w_branch_ssm"][0, 0:256, :].rearrange("(k p) n -> p k n", p=P),
                 slot("w_bs0").rearrange("p (k n) -> p k n", k=2))
            sp.wait_ge(s_s5, 1)
            with sp.Fori(0, NB - 1) as b:
                pages_of("K", ck, b + 1)
                pages_of("V", cv, b)
            pages_of("V", cv, NB - 1)
            sp.wait_ge(s_eT, NB)
            load("w_bs1", A["w_branch_ssm"][0, 256:512, :].rearrange("(k p) n -> p k n", p=P),
                 slot("w_bs1").rearrange("p (k n) -> p k n", k=2))
            load("w_ba0", A["w_branch_attn"][0, 0:256, :].rearrange("(k p) n -> p k n", p=P),
                 slot("w_ba0").rearrange("p (k n) -> p k n", k=2))
            load("w_ba1", A["w_branch_attn"][0, 256:512, :].rearrange("(k p) n -> p k n", p=P),
                 slot("w_ba1").rearrange("p (k n) -> p k n", k=2))
            for i in range(4):
                load(f"w_out{i}", A["w_out"][0, i * 256:(i + 1) * 256, :].rearrange("(k p) n -> p k n", p=P),
                     slot(f"w_out{i}").rearrange("p (k n) -> p k n", k=2))

            def chunk(q, i, e):
                s = chunk_raw(i)
                qq, ii = (q, i - NRAW) if i >= NRAW else (q - 1, i + NRAW)
                wait_low(sp, qq, ii)
                if i < 8:
                    sp.dma_start(ring[:, s, :], wgu[ds(e, 1), i, :, :].rearrange("o p n -> p (o n)")).then_inc(loaded[s], 16)
                else:
                    sp.dma_start(ring[:, s, :].rearrange("p (k n) -> p k n", k=2),
                                 wdn[ds(e, 1), i - 8, :, :, :].rearrange("o p k n -> p (o k) n")).then_inc(loaded[s], 16)

            def first_chunk(c):
                s = chunk_raw(c + 4)
                if c < NRAW:
                    sp.wait_ge(freed[s], _uses[s])
                else:
                    wait_low(sp, 0, c + 4 - NRAW)
                sp.dma_start(ring[:, s, :], wgu[0, c, :, :]).then_inc(loaded[s], 16)

            for c in range(8):
                first_chunk(c)
            with sp.Fori(1, NE) as e:
                for i in range(8):
                    chunk(e, i, e)
                for i in range(8, 12):
                    chunk(e, i, e - 1)
            for i in range(4):
                s = chunk_raw(i)
                wait_low(sp, NE - 1, i + NRAW)
                sp.dma_start(ring[:, s, :].rearrange("p (k n) -> p k n", k=2), wdn[NE - 1, i, :, :, :]).then_inc(loaded[s], 16)
            extra = extra_jobs(sp)
            with sp.Fori(0, NOVER) as o:
                with sp.If(extra > o):
                    e = sp.value_load(jobi[0:1, ds(o, 1)], min_val=0, max_val=NE - 1)
                    for c in range(12):
                        i, q = (c + 4) % 12, o + (NE + (c + 4) // 12)
                        s = chunk_raw(i)
                        wait_low(sp, *((q, i - NRAW) if i >= NRAW else (q - 1, i + NRAW)))
                        if c < 8:
                            sp.dma_start(ring[:, s, :], wgu[ds(e, 1), c, :, :].rearrange("o p n -> p (o n)")).then_inc(loaded[s], 16)
                        else:
                            sp.dma_start(ring[:, s, :].rearrange("p (k n) -> p k n", k=2),
                                         wdn[ds(e, 1), c - 8, :, :, :].rearrange("o p k n -> p (o k) n")).then_inc(loaded[s], 16)
                with sp.Else():
                    sp.wait_ge(s_route, 1)

        @block.scalar
        def _(act):
            n_step = [0]

            def step(ins):
                n_step[0] += 1
                ins.then_inc(as_, 1)
                act.wait_ge(as_, n_step[0])

            act.dma_start(cst[:, :], A["consts"]).then_inc(s_const, 16)
            small = [
                (rows[0:8, :], A["norm_mix_g"][0].rearrange("(r n) -> r n", n=P)),
                (rows[8:24, :], A["b_gate"][0].rearrange("(r n) -> r n", n=P)),
                (rows[24:28, :], A["ssm_b_glu"][0].rearrange("(r n) -> r n", n=P)),
                (rows[28:32, :], A["ssm_d"][0].rearrange("(r a) h -> r (a h)", r=4)),
                (prm_in[:, 0, :], A["ssm_lambda_re"][0].rearrange("(j a) p -> j (a p)", a=2)),
                (prm_in[:, 1, :], A["ssm_lambda_im"][0].rearrange("(j a) p -> j (a p)", a=2)),
                (logdt[:, 0:2], A["ssm_log_dt"][0].rearrange("(j a) -> j a", a=2)),
                (x0rows[:, 0, :], A["state_ssm_re"][0].rearrange("b (j a) p -> (b j) (a p)", a=2)),
                (x0rows[:, 1, :], A["state_ssm_im"][0].rearrange("b (j a) p -> (b j) (a p)", a=2)),
                (bin_[:, 0], A["ssm_b_re"][0].rearrange("(j a) p h -> (a p) j h", a=2)),
                (bin_[:, 1], A["ssm_b_im"][0].rearrange("(j a) p h -> (a p) j h", a=2)),
            ]
            for i, name in enumerate(["ssm_c_re", "ssm_c_im"]):
                src = A[name][0].rearrange("(c g) h p -> (g h) c p", c=NCT)
                for a in range(2):
                    small.append((cdup[:, i, :, a * 64:(a + 1) * 64], src))
            for i, name in enumerate(["lambda_q1", "lambda_k1", "lambda_q2", "lambda_k2"]):
                small.append((lamv[:, i, :], A[name][0].partition_broadcast(P)))
            for dst, src in small[:4]:
                act.dma_start(dst, src).then_inc(s_vec, 16)
            assert len(small) == N_SMALL + 4

            act.wait_ge(s_x, 48)
            act.wait_ge(ps, 2)

            def rms(t, n, dump, done):
                step(nc.scalar.activation(dump[0:n, :], x[0:n, t, :], ACT.Square, accum_out=sc[0:n, t:t + 1]))
                nc.scalar.activation(sc[0:n, t:t + 1], sc[0:n, t:t + 1], ACT.Sqrt, scale=1.0 / D, bias=epsc[0:n, :]).then_inc(done, 1)

            for t, (t0, n) in enumerate(TILES):
                rms(t, n, normj, s_ssq)

            wait_loaded(act, "w_in5")
            for dst, src in small[4:]:
                act.dma_start(dst, src).then_inc(s_par, 16)
            act.wait_ge(s_par, 16 * N_SMALL)
            nc.scalar.activation(logdt[:, 2:4], logdt[:, 0:2], ACT.Exp).then_inc(s_dt, 1)
            act.wait_ge(s_lre, 1)
            nc.scalar.activation(prm[:, 0, :], pw[:, 1, :], ACT.Exp).then_inc(s_mag, 1)
            act.wait_ge(s_lamd, 1)
            nc.scalar.activation(sc[:, 8:10], sc[:, 6:8], ACT.Exp).then_inc(s_lame, 1)
            act.wait_ge(s_fr, 1)
            nc.scalar.activation(pw[:, 4, :], prm[:, 1, :], ACT.Sin, scale=2 * math.pi * (1 - 2e-7))
            step(nc.scalar.activation(pw[:, 5, :], prm[:, 1, :], ACT.Abs))
            nc.scalar.activation(pw[:, 6, :], pw[:, 5, :], ACT.Sin, bias=halfpi[0:16, :], scale=-2 * math.pi * (1 - 2e-7)
                                 ).then_inc(s_trig, 1)

            def job(i):
                act.wait_ge(act_full, i + 1)
                return psum[:, i % 4, :]

            def tables(ct):
                act.wait_ge(s_angT, ct + 1)
                nc.scalar.activation(sinT[:, :, :], cosT[:, :, :], ACT.Sin, scale=2 * math.pi * (1 - 2e-7))
                step(nc.scalar.activation(cosT[:, :, :], cosT[:, :, :], ACT.Abs))
                nc.scalar.activation(cosT[:, :, :], cosT[:, :, :], ACT.Sin, bias=halfpi[:, :],
                                     scale=-2 * math.pi * (1 - 2e-7)).then_inc(s_tabT, 1)

            for i in range(4):
                nc.scalar.activation(uT[:, i, :], job(ACT_JOB["u"] + i)[:, 0:T], ACT.Copy).then_inc(act_done, 1)
            act.wait_ge(s_prm, 1)

            def inputs(ct):
                if ct:
                    act.wait_ge(s_zfree, ct)
                for jj in range(4):
                    for c, z in enumerate((zr, zi)):
                        pz = job(ACT_JOB[f"z{ct}"] + 2 * jj + c)
                        nc.scalar.activation(z[:, jj, 0:SEQ], pz[:, 0:SEQ], ACT.Copy)
                        nc.scalar.activation(z[:, jj, SEQ:W5].rearrange("p (b s) -> p b s", s=NS + 1)[:, :, 1:],
                                             pz[:, SEQ:T].rearrange("p (b s) -> p b s", s=NS), ACT.Copy).then_inc(act_done, 1)

            tables(0)
            inputs(0)
            for ct in range(NCT):
                for i in range(4 * ct, 4 * ct + 4):
                    nc.scalar.activation(gates[:, i, :], job(ACT_JOB[f"gate{ct}"] + i % 4)[:, 0:T], ACT.Sigmoid,
                                         bias=vecT[:, 8 + i:9 + i]).then_inc(act_done, 1)
                if ct + 1 < NCT:
                    inputs(ct + 1)
                    tables(ct + 1)

            act.wait_ge(s_kvtok, 1)
            kvo = [(A["o_k_prompt"], A["o_k_sample"], qk[:, 1]), (A["o_v_prompt"], A["o_v_sample"], vt)]
            for o_p, o_s, src in kvo:
                op = o_p[0, 0].rearrange("s h d -> s (h d)")
                for t in range(2):
                    act.dma_start(op[t * 128:(t + 1) * 128, :], src[:, t, :]).then_inc(s_kvout, 16)
                act.dma_start(o_s[0].rearrange("b s h d -> (b s) (h d)"), src[0:NSMP, 2, :]).then_inc(s_kvout, 16)
            act.wait_ge(s_fin, 1)
            for c, (o_p, o_s) in enumerate([(A["o_re_prompt"], A["o_re_sample"]), (A["o_im_prompt"], A["o_im_sample"])]):
                act.dma_start(o_p[0, 0].rearrange("(j a) p -> j (a p)", a=2), frow[0:NJ, c, :]).then_inc(s_out, 16)
                act.dma_start(o_s[0].rearrange("b (j a) p -> (b j) (a p)", a=2), frow[:, 2 + c, :]).then_inc(s_out, 16)
            act.wait_ge(s_s5, 1)
            late = [(gvec, A["norm_ffn_g"][0].partition_broadcast(P)),
                    (wr, A["w_router"][0].rearrange("(k p) n -> p k n", p=P)),
                    (brt, A["b_router"][0].partition_broadcast(P)),
                    (subg, A["attn_subln_g"][0].partition_broadcast(P))]
            for dst, src in late:
                act.dma_start(dst, src).then_inc(s_late, 16)

            nc.scalar.activation(yT[:, :, :], yT[:, :, :], ACT.Gelu_apprx_tanh).then_inc(s_gelu, 1)

            def p_exp(n):
                act.wait_ge(s_nb, n + 1)
                w = 128 * (n // 4 + 1)
                for c in range(2):
                    ins = nc.scalar.activation(pE[:, n % 2, c, 0:w], pS[:, n % 2, c, 0:w], ACT.Exp, scale=SCALE,
                                               bias=st4[:, n % 2, c:c + 1], accum_out=st4[:, n % 2, 2 + c:3 + c])
                step(ins)
                nc.scalar.activation(sc[:, 14:15], C("ones")[:, 0:1], ACT.Copy).then_inc(s_pexp, 1)

            p_exp(0)
            for n in range(8):
                if n + 1 < 8:
                    p_exp(n + 1)
                w = 128 * (n // 4 + 1)
                nc.scalar.activation(pWT[:, n % 2, 0:w // 128, :],
                                     job(ACT_JOB["wT"] + n)[:, 0:w].rearrange("p (k q) -> p k q", q=P),
                                     ACT.Copy).then_inc(act_done, 1)

            def key_high(i, pg):
                g = pg // 2
                act.wait_ge(p_turned, i * NPG + (pg + 1))
                if pg % 2 == 0 and not (isinstance(i, int) and g < 2):
                    act.wait_ge(s_group, i * (NPG // 2) + (g - 1))
                nc.scalar.activation(keyh[:, g % 2, :, (pg % 2) * P:(pg % 2 + 1) * P],
                                     psum[:, pg % 2, :].rearrange("p (h c) -> p h c", h=H), ACT.Copy).then_inc(p_keyh, 1)

            def scores_low(i, b):
                act.wait_ge(s_group, i * (NPG // 2) + (2 * b + 2))
                nc.scalar.activation(ss[:, b * 512:(b + 1) * 512], psum[32:64, 2 + b, :], ACT.Copy).then_inc(s_low, 1)

            def new_low(i):
                act.wait_ge(s_new, i + 1)
                nc.scalar.activation(snw[:, :], psum[32:64, 6, 0:NSMP], ACT.Copy).then_inc(s_low, 1)

            def exps(j):
                act.wait_ge(s_nbias, j + 1)
                nc.scalar.activation(En, snw, ACT.Exp, scale=SCALE, bias=nbias, accum_out=esum[:, 1:2])
                nc.scalar.activation(E, ss, ACT.Exp, scale=SCALE, bias=nbias, accum_out=esum[:, 0:1]).then_inc(s_ex, 1)

            def exps_high(j):
                act.wait_ge(s_eT, j + 1)
                nc.scalar.activation(e2[0:NSMP, NPG, 0:32], psum[0:NSMP, 7, 0:32], ACT.Copy)
                nc.scalar.activation(e2[:, 0:NPG, 0:32], psum[:, 6, :].rearrange("p (g c) -> p g c", g=NPG),
                                     ACT.Copy).then_inc(s_eh, 1)

            def value_high(j, pg):
                if pg % 4 == 0:
                    act.wait_ge(loaded[SLOT[f"V{pg // 4}"]], loaded_at(f"V{pg // 4}", j))
                if pg >= 3:
                    act.wait_ge(p_used, j * NPG + (pg - 2))
                nc.scalar.activation(valh[:, pg % 3, :], ring[:, SLOT[f"V{pg // 4}"], (pg % 4) * 512:(pg % 4 + 1) * 512],
                                     ACT.Copy).then_inc(p_valh, 1)

            def out_low(j):
                act.wait_ge(s_pvd, j + 1)
                nc.scalar.activation(oL, psum[32:64, 7, :], ACT.Copy).then_inc(s_oL, 1)

            def batch(i, j):
                for g in range(NPG // 2):
                    key_high(i, 2 * g)
                    key_high(i, 2 * g + 1)
                    if j is not None and g == 0:
                        exps(j)
                    if j is not None and g == 1:
                        for pg in range(3):
                            value_high(j, pg)
                    if j is not None and g == E_STEP:
                        exps_high(j)
                    if g in (2, 4, 6):
                        scores_low(i, g // 2 - 1)
                    if j is not None and g in V_STEP:
                        for pg in range(3 + V_STEP[g][0], min(NPG, 3 + V_STEP[g][1])):
                            value_high(j, pg)
                if j is not None:
                    out_low(j)
                scores_low(i, 3)
                new_low(i)

            def head_rms(t, n):
                act.wait_ge(s_hsum, t + 1)
                nc.scalar.activation(st4[0:n, 2, :], st4[0:n, 0, :], ACT.Sqrt, scale=1.0 / DV, bias=epsc[0:n, :]).then_inc(s_hrms, 1)

            for t in range(2):
                head_rms(t, 128)
            act.wait_ge(s_kvout, 96)
            act.wait_ge(dve_done, DVE_JOB["s"])
            batch(0, None)
            with act.Fori(1, NB) as i:
                batch(i, act.snap(i - 1))
            exps(NB - 1)
            for pg in range(3):
                value_high(NB - 1, pg)
            exps_high(NB - 1)
            for pg in range(3, NPG):
                value_high(NB - 1, pg)
            out_low(NB - 1)
            head_rms(2, NSMP)

            act.wait_ge(s_do, NB)
            for t, (t0, n) in enumerate(TILES):
                act.dma_start(x[0:n, t, :], xin[t]).then_inc(s_xagain, 16)
            for i in range(4):
                nc.scalar.activation(sg[:, i, :], job(ACT_JOB["glu"] + i)[:, 0:T], ACT.Sigmoid,
                                     bias=vecT[:, 24 + i:25 + i]).then_inc(act_done, 1)

            for t, (t0, n) in enumerate(TILES):
                act.wait_ge(s_xres, t + 1)
                rms(t, n, junk, s_ssq2)
            for t, (t0, n) in enumerate(TILES):
                act.wait_ge(s_h2, t + 1)
                nc.scalar.activation(h2s[0:n, 0, t, :], h2[0:n, t, :], ACT.Copy).then_inc(s_h2h, 1)
            act.wait_ge(s_h2, 3)
            act.dma_start(gvec, A["norm_final_g"].partition_broadcast(P)).then_inc(s_gfin, 16)
            act.wait_ge(dve_done, DVE_JOB["lg"])
            act.wait_ge(s_h2s, 3)
            for half in range(2):
                act.dma_start(braw[32 * half:32 * half + 32, 0:2 * D], A["b_gate_up"][0]).then_inc(s_bias, 16)
                act.dma_start(braw[32 * half:32 * half + 32, 2 * D:3 * D], A["b_down"][0]).then_inc(s_bias, 16)
            for t, (t0, n) in enumerate(TILES):
                act.wait_ge(s_nmx, t + 1)
                step(nc.scalar.activation(gk[0:n, t, :], mx8[0:n, t, 0:TOPK], ACT.Exp, bias=nmx[0:n, t, :],
                                          accum_out=gsum[0:n, t, :]))
                nc.scalar.activation(sc[:, 14:15], C("ones")[:, 0:1], ACT.Copy).then_inc(s_gexp, 1)

            def high(q, i):
                act.wait_ge(loaded[chunk_raw(i)], chunk_loaded(q, i))
                if not (isinstance(q, int) and q * 12 + i < 4 + NSPLIT):
                    act.wait_ge(c_free, q * 12 + (i - 3 - NSPLIT))
                nc.scalar.activation(whi[:, i % NSPLIT, :], ring[:, chunk_raw(i), :], ACT.Copy).then_inc(c_hi, 1)

            def copy_gu(q, i):
                act.wait_ge(c_free, chunk_used(q, i))
                nc.scalar.activation(guL.rearrange("p (b n) -> p b n", b=4), psum[CAP:P, 0:4, :], ACT.Copy).then_inc(e_guL, 1)

            def sigm(j):
                act.wait_ge(e_g, j + 1)
                nc.scalar.activation(sig, gg, ACT.Sigmoid, scale=ALPHA).then_inc(e_sig, 1)

            def copy_x(j, shift=0):
                act.wait_ge(e_gath, j + (1 + shift))
                nc.scalar.activation(xa[0:CAP, :].rearrange("p (b n) -> p b n", b=2), psum[0:CAP, 6:8, :], ACT.Copy).then_inc(e_xg, 1)

            def high_x(turn):
                act.wait_ge(e_turn, turn)
                nc.scalar.activation(xs_[:, :, 0:CAP], turned_x, ACT.Copy).then_inc(e_xh, 1)

            def high_a(turn):
                act.wait_ge(e_turn, turn)
                nc.scalar.activation(as2[:, :, 0:CAP], turned_a, ACT.Copy).then_inc(e_ah, 1)

            def copy_y(q, i):
                act.wait_ge(c_free, chunk_used(q, i))
                nc.scalar.activation(yL.rearrange("p (b n) -> p b n", b=2), psum[CAP:P, 4:6, :], ACT.Copy).then_inc(e_yL, 1)

            act.wait_ge(s_mg, 1)
            act.wait_ge(dve_done, DVE_JOB["h2T"])
            for c in range(NSPLIT):
                high(0, 4 + c)
            copy_x(0)
            high_x(1)
            high(0, 4 + NSPLIT)
            copy_x(1)
            for c in range(NSPLIT + 1, 8):
                high(0, 4 + c)
            copy_gu(0, 11)
            high_x(2)
            high(1, 0)
            sigm(0)
            high(1, 1)
            with act.Fori(1, NE) as j:
                high(j, 2)
                high(j, 3)
                copy_x(j + 1)
                for i in (4, 5, 6):
                    high(j, i)
                high_a(j + 2)
                for i in (7, 8, 9, 10):
                    high(j, i)
                copy_gu(j, 7)
                act.wait_ge(e_as, j)
                high_x(j + 2)
                high(j, 11)
                sigm(j)
                high(j + 1, 0)
                high(j + 1, 1)
                act.wait_ge(e_u, j + 1)
                copy_y(j, 11)
            high_a(NE + 2)
            for i in (2, 3):
                high(NE, i)
            copy_y(NE, 3)
            extra = extra_jobs(act)
            with act.Fori(0, NOVER) as o:
                with act.If(extra > o):
                    j = act.snap(o + NE)
                    copy_x(j, 1)
                    turn = act.snap(o * 2 + (NE + 3))
                    high_x(turn)
                    for c in range(12):
                        if c == 10:
                            copy_gu(o + NE, 11)
                            sigm(j)
                            high_a(turn + 1)
                        i = (c + 4) % 12
                        high(o + (NE + (c + 4) // 12), i)
                    copy_y(o + (NE + 1), 3)
                with act.Else():
                    act.wait_ge(s_route, 1)
            for t, (t0, n) in enumerate(TILES):
                act.wait_ge(s_comb, t + 1)
                rms(t, n, junk, s_ssq2)
            outs = [A["o_y_prompt"][0, 0:128, :], A["o_y_prompt"][0, 128:256, :], A["o_y_sample"].rearrange("b s d -> (b s) d")]
            for t, (t0, n) in enumerate(TILES):
                act.wait_ge(s_ynorm, t + 1)
                act.dma_start(outs[t], x[0:n, t, :]).then_inc(s_out, 16)
            act.wait_ge(s_kvout, 96)
            act.wait_ge(s_out, 16 * 7)

        @block.gpsimd
        def _(pool):
            pool.memset(halfpi[:, :], math.pi / 2).then_inc(ps, 1)
            pool.memset(epsc[:, :], EPS).then_inc(ps, 1)

            pool.memset(zeros, 0.0).then_inc(ps, 1)
            pool.wait_ge(ps, 3)
            pool.dma_start(ydram[NE * CAP:, :].rearrange("(p a) n -> p a n", p=64),
                           zeros.unsqueeze(1).to_broadcast([64, NOVER, D])).then_inc(s_zero, 16)
            pool.wait_ge(s_zero, 16)
            with pool.Fori(0, NB) as j:
                for pg in range(0, NPG, 2):
                    pool.wait_ge(p_valh, j * NPG + (pg + 1))
                    nc.gpsimd.tensor_tensor(vall[:, pg % 3, :], ring[:, SLOT[f"V{pg // 4}"], (pg % 4) * 512:(pg % 4 + 1) * 512],
                                            valh[:, pg % 3, :], ALU.subtract).then_inc(p_vall, 1)

            def low(q, i):
                pool.wait_ge(c_hi, q * 12 + (i - 3))
                nc.gpsimd.tensor_tensor(wlo[:, i % NSPLIT, :], ring[:, chunk_raw(i), :], whi[:, i % NSPLIT, :],
                                        ALU.subtract).then_inc(c_lop, 1)

            def rows_out(j):
                pool.wait_ge(e_y, j + 1)
                pool.dma_start(ydram[ds(j * CAP, CAP), :], yS).then_inc(e_out, 16)

            for i in POOL_CHUNKS:
                if i >= 4:
                    low(0, i)
            with pool.Fori(1, NE) as j:
                for i in POOL_CHUNKS:
                    low(j, i)
                rows_out(j - 1)
            for i in POOL_CHUNKS:
                if i < 4:
                    low(NE, i)
            rows_out(NE - 1)
            extra = extra_jobs(pool)
            with pool.Fori(0, NOVER) as o:
                with pool.If(extra > o):
                    for c in range(12):
                        if (c + 4) % 12 in POOL_CHUNKS:
                            low(o + (NE + (c + 4) // 12), (c + 4) % 12)
                    rows_out(o + NE)
                    pool.wait_ge(e_out, o * 16 + 16 * (NE + 1))
                    pool.sem_inc(e_extra, 1)
                with pool.Else():
                    pool.sem_inc(e_extra, 1)
            pool.wait_ge(e_out, 16 * NE)
            pool.wait_ge(e_extra, NOVER)
            for t, (t0, n) in enumerate(TILES):
                for k in range(TOPK):
                    pool.indirect_dma_start(ycomb[0:n, t, k, :], None, ydram,
                                            bass.IndirectOffsetOnAxis(rowi[0:n, t, k:k + 1], 0),
                                            bounds_check=NJOB * CAP - 1).then_inc(s_gath[t], 16)

        @block.tensor
        def _(pe):
            na, nd = [0], [0]

            def abank():
                i = na[0]
                na[0] += 1
                if i >= 4:
                    pe.wait_ge(act_done, i - 3)
                return psum[:, i % 4, :]

            def dbank():
                i = nd[0]
                nd[0] += 1
                if i >= 3:
                    pe.wait_ge(dve_done, i - 2)
                return psum[:, 4 + i % 3, :]

            def mm(out, a, b, start, stop):
                return nc.tensor.matmul(out, lhsT=a, rhs=b, start=start, stop=stop, skip_group_check=True)

            def tr(out, in_, n=P):
                return nc.tensor.transpose(out, in_, ident[0:n, 0:n])

            pe.wait_ge(s_const, 16)
            for t, (t0, n) in enumerate(TILES):
                pe.wait_ge(s_xn, t + 1)
                for half in range(2 if n == 128 else 1):
                    b = dbank()
                    ks = range(4 * half, 4 * half + 4) if n == 128 else range(8)
                    for i, k in enumerate(ks):
                        last = tr(b[:, i * n:(i + 1) * n], x[0:n, t, k * P:(k + 1) * P], n)
                    last.then_inc(dve_full, 1)
            pe.wait_ge(s_vec, 64)
            tr(dbank()[:, 0:32], rows[0:32, :], 32).then_inc(dve_full, 1)
            pe.wait_ge(dve_done, DVE_JOB["qkv0"])
            for i in range(4):
                b = abank()
                for k in range(KD):
                    if i == 0:
                        wait_loaded(pe, f"w_in{k}")
                    last = mm(b[:, 0:T], slot(f"w_in{k}")[:, i * P:(i + 1) * P], hT[:, k, :], k == 0, k == KD - 1)
                last.then_inc(act_full, 1)
            def qkv(t):
                t0, n = TILES[t]
                for c in range(3):
                    b = dbank()
                    for k in range(KD):
                        last = mm(b[0:n, :], hT[:, k, t0:t0 + n], slot(f"w_in{k}")[:, 512 * (c + 1):512 * (c + 2)],
                                  k == 0, k == KD - 1)
                        if t == 2 and c == 2 and k < KD - 1:
                            last.then_inc(freed[SLOT[f"w_in{k}"]], 1)
                    last.then_inc(dve_full, 1)
            qkv(0)
            qkv(1)
            pe.wait_ge(s_prm, 1)
            b = dbank()
            for i in range(4):
                last = tr(b[:, i * 16:(i + 1) * 16], prm[:, i, :], 16)
            last.then_inc(dve_full, 1)
            b = dbank()
            for i in range(2):
                last = tr(b[:, i * P:(i + 1) * P], x0rows[:, i, :])
            last.then_inc(dve_full, 1)
            qkv(2)
            pe.wait_ge(dve_full, nd[0])
            pe.sem_inc(freed[SLOT["w_in7"]], 1)
            for c in range(2):
                for q in range(4):
                    b = dbank()
                    pe.wait_ge(s_Bpad, 1)
                    for i in range(4):
                        last = tr(b[:, i * P:(i + 1) * P], (padr, padi)[c][:, 4 * q + i, :])
                    last.then_inc(dve_full, 1)
            for c in range(2):
                b = dbank()
                for i in range(4):
                    last = tr(b[:, i * P:(i + 1) * P], cdup[:, c, i, :])
                last.then_inc(dve_full, 1)
            pe.wait_ge(act_done, ACT_JOB["z0"])
            pe.wait_ge(dve_done, DVE_JOB["C"])

            def s5_in(ct):
                for j in range(4 * ct, 4 * ct + 4):
                    for c in range(2):
                        mm(abank()[:, 0:T], bbT[:, c, j, :], uT[:, ct, :], True, True).then_inc(act_full, 1)

            def s5_out(ct):
                b = dbank()
                pe.wait_ge(s_xT5, ct + 1)
                for jj in range(4):
                    j = 4 * ct + jj
                    mm(b[:, 0:W5], padr[:, j, :], t1[:, jj, :], jj == 0, False)
                    last = mm(b[:, 0:W5], padi[:, j, :], t3[:, jj, :], False, jj == 3)
                last.then_inc(dve_full, 1)

            s5_in(0)
            for k in range(8):
                wait_loaded(pe, f"w_gate{k}")
            for i in range(16):
                b = abank()
                for k in range(KD):
                    last = mm(b[:, 0:T], slot(f"w_gate{k}")[:, i * P:(i + 1) * P], hT[:, k, :], k == 0, k == KD - 1)
                    if i == 15 and k < KD - 1:
                        last.then_inc(freed[SLOT[f"w_gate{k}"]], 1)
                last.then_inc(act_full, 1)
                if i % 4 == 3:
                    ct = i // 4
                    if ct + 1 < NCT:
                        s5_in(ct + 1)
                    if ct + 1 == NCT:
                        n_gate = na[0]
                    s5_out(ct)
            pe.wait_ge(act_full, n_gate)
            pe.sem_inc(freed[SLOT["w_gate7"]], 1)
            pe.wait_ge(dve_done, DVE_JOB["fin"])
            b = dbank()
            for c in range(2):
                tr(b[0:NJ, c * P:(c + 1) * P], finp[:, c, :])
            for c in range(2):
                last = tr(b[:, (2 + c) * P:(3 + c) * P], fins[:, c].rearrange("p b j -> p (b j)"))
            last.then_inc(dve_full, 1)
            for t, (t0, n) in enumerate(TILES):
                for c in range(2):
                    b = dbank()
                    for h in range(H):
                        last = tr(b[:, h * n:(h + 1) * n], qk[0:n, c, t, h * P:(h + 1) * P], n)
                    last.then_inc(dve_full, 1)

            def p_scores(n):
                i, h = divmod(n, 4)
                b = dbank()
                w = 128 * (i + 1)
                for c in range(2):
                    last = mm(b[:, c * w:(c + 1) * w], qz[:, h, c, i * P:(i + 1) * P], kT[:, h, 0:w], True, True)
                last.then_inc(dve_full, 1)

            pe.wait_ge(dve_done, DVE_JOB["s"])
            p_scores(0)
            p_scores(1)
            for n in range(8):
                i, h = divmod(n, 4)
                if n + 2 < 8:
                    p_scores(n + 2)
                b = abank()
                pe.wait_ge(s_w, n + 1)
                for k in range(i + 1):
                    last = tr(b[:, k * P:(k + 1) * P], pW[:, n % 2, k * P:(k + 1) * P])
                last.then_inc(act_full, 1)
                pe.wait_ge(act_done, ACT_JOB["wT"] + n + 1)
                if n == 4:
                    pe.wait_ge(s_pvr, 1)
                for k in range(i + 1):
                    last = mm(psum[:, 7, h * P:(h + 1) * P], pWT[:, n % 2, k, :], vt[:, k, h * P:(h + 1) * P], k == 0, k == i)
                last.then_inc(s_pv, 1)

            def keys_turn(i, pg):
                if pg % 4 == 0:
                    pe.wait_ge(loaded[SLOT[f"K{pg // 4}"]], loaded_at(f"K{pg // 4}", i))
                if not (isinstance(i, int) and pg < 2):
                    pe.wait_ge(p_keyl, i * NPG + (pg - 1))
                for h in range(H):
                    last = tr(psum[:, pg % 2, h * P:(h + 1) * P], ring[:, SLOT[f"K{pg // 4}"], (pg % 4) * 512 + h * P:(pg % 4) * 512 + (h + 1) * P])
                last.then_inc(p_turned, 1)

            def query(h):
                return qs[:, h * 64:(h + 1) * 64]

            def scores(i, g):
                b = g // 2
                if g == 0:
                    pe.wait_ge(s_qb, i + 1)
                if g % 2 == 0 and not isinstance(i, int):
                    pe.wait_ge(s_sum, i * 5 + (b - 4))
                pe.wait_ge(p_keyl, i * NPG + (2 * g + 2))
                for h in range(H):
                    for p, part in enumerate((keyh, keyl)):
                        last = mm(psum[0:64, 2 + b, (g % 2) * 256:(g % 2 + 1) * 256], query(h), part[:, g % 2, h, :],
                                  h == 0 and p == 0, h == H - 1 and p == 1)
                        if g % 2 == 1 and h == 0 and p == 0:
                            last.then_inc(freed[SLOT[f"K{g // 2}"]], 1)
                last.then_inc(s_group, 1)

            def new_scores(i):
                for h in range(H):
                    for p, part in enumerate((knh, knl)):
                        last = mm(psum[0:64, 6, 0:NSMP], query(h), part[:, h, :], h == 0 and p == 0, h == H - 1 and p == 1)
                last.then_inc(s_new, 1)

            def exps_turn():
                for pg in range(NPG):
                    tr(psum[:, 6, pg * 32:(pg + 1) * 32], E[:, pg * P:(pg + 1) * P], 32)
                tr(psum[0:NSMP, 7, 0:32], En, 32).then_inc(s_eT, 1)

            def values(j, pg):
                if pg == 0:
                    pe.wait_ge(s_el, j + 1)
                pe.wait_ge(p_vallv if pg % 2 else p_vall, j * (NPG // 2) + (pg // 2 + 1))
                first = mm(psum[0:64, 7, :], e2[:, pg, :], valh[:, pg % 3, :], pg == 0, False)
                if pg % 4 == 3:
                    first.then_inc(freed[SLOT[f"V{pg // 4}"]], 1)
                mm(psum[0:64, 7, :], e2[:, pg, :], vall[:, pg % 3, :], False, False).then_inc(p_used, 1)

            def new_values():
                mm(psum[0:64, 7, :], e2[0:NSMP, NPG, :], vnh[:, :], False, False)
                mm(psum[0:64, 7, :], e2[0:NSMP, NPG, :], vnl[:, :], False, True).then_inc(s_pvd, 1)

            def out_turn():
                for h in range(H):
                    last = tr(psum[:, 7, h * 32:(h + 1) * 32], oS[:, h * P:(h + 1) * P], 32)
                last.then_inc(s_oT, 1)

            def batch(i, j):
                for g in range(NPG // 2):
                    keys_turn(i, 2 * g)
                    keys_turn(i, 2 * g + 1)
                    if j is not None and g == E_STEP:
                        pe.wait_ge(s_ex, j + 1)
                        pe.wait_ge(s_do, j)
                    if g:
                        scores(i, g - 1)
                    if j is not None and g == E_STEP:
                        exps_turn()
                    if j is not None and g in V_STEP:
                        for pg in range(*V_STEP[g]):
                            values(j, pg)
                if j is not None:
                    new_values()
                scores(i, NPG // 2 - 1)
                if j is not None:
                    pe.wait_ge(s_oS, j + 1)
                new_scores(i)
                if j is not None:
                    out_turn()

            pe.wait_ge(s_pvr, 2)
            pe.wait_ge(act_done, ACT_JOB["glu"])
            pe.wait_ge(dve_done, DVE_JOB["oS"])
            pe.wait_ge(s_newkv, 1)
            batch(0, None)
            with pe.Fori(1, NB) as i:
                batch(i, pe.snap(i - 1))
            pe.wait_ge(s_ex, NB)
            pe.wait_ge(s_do, NB - 1)
            exps_turn()
            for pg in range(NPG):
                values(NB - 1, pg)
            new_values()
            pe.wait_ge(s_oS, NB)
            out_turn()

            pe.wait_ge(s_do, NB)
            b = dbank()
            for h in range(H):
                last = tr(b[0:NSMP, h * P:(h + 1) * P], oTs[:, h, :])
            last.then_inc(dve_full, 1)
            wait_loaded(pe, "w_glu")
            pe.wait_ge(s_gelu, 1)
            for i in range(4):
                b = abank()
                for k in range(4):
                    last = mm(b[:, 0:T], slot("w_glu")[:, k * 512 + i * P:k * 512 + (i + 1) * P], yT[:, k, :], k == 0, k == 3)
                last.then_inc(act_full, 1)
            for t, (t0, n) in enumerate(TILES):
                pe.wait_ge(s_ln, t + 1)
                b = dbank()
                for h in range(H):
                    last = tr(b[:, h * n:(h + 1) * n], ot[0:n, t, h * P:(h + 1) * P], n)
                last.then_inc(dve_full, 1)
            for name, src, ready in (("w_bs", yT, 1), ("w_ba", oT, None)):
                wait_loaded(pe, name + "0")
                wait_loaded(pe, name + "1")
                if ready:
                    pe.wait_ge(s_yglu, ready)
                else:
                    pe.wait_ge(dve_done, DVE_JOB["bs"])
                for i in range(KD):
                    b = dbank()
                    for k in range(4):
                        last = mm(b[:, 0:T], slot(f"{name}{k // 2}")[:, (k % 2) * D + i * P:(k % 2) * D + (i + 1) * P],
                                  src[:, k, :], k == 0, k == 3)
                    last.then_inc(dve_full, 1)
            pe.wait_ge(s_mg, 1)
            pe.sem_inc(freed[SLOT["w_glu"]], 1)
            for name in ("w_bs0", "w_bs1", "w_ba0", "w_ba1"):
                pe.sem_inc(freed[SLOT[name]], 1)
            for i in range(4):
                wait_loaded(pe, f"w_out{i}")
            for t, (t0, n) in enumerate(TILES):
                for half in range(2):
                    b = dbank()
                    for k in range(KD):
                        last = mm(b[0:n, :], mg[:, k, t0:t0 + n],
                                  slot(f"w_out{k // 2}")[:, (k % 2) * D + half * 512:(k % 2) * D + (half + 1) * 512],
                                  k == 0, k == KD - 1)
                    last.then_inc(dve_full, 1)
            pe.wait_ge(dve_done, DVE_JOB["h2T"])
            for i in range(4):
                pe.sem_inc(freed[SLOT[f"w_out{i}"]], 1)
            for t, (t0, n) in enumerate(TILES):
                pe.wait_ge(s_h2, t + 1)
                for half in range(2 if n == 128 else 1):
                    b = dbank()
                    ks = range(4 * half, 4 * half + 4) if n == 128 else range(8)
                    for i, k in enumerate(ks):
                        last = tr(b[:, i * n:(i + 1) * n], h2[0:n, t, k * P:(k + 1) * P], n)
                    last.then_inc(dve_full, 1)
            pe.wait_ge(s_late, 64)
            pe.wait_ge(dve_done, DVE_JOB["lg"])
            for t, (t0, n) in enumerate(TILES):
                b = dbank()
                for k in range(KD):
                    last = mm(b[0:n, 0:NE], h2T[:, k, t0:t0 + n], wr[:, k, :], k == 0, k == KD - 1)
                last.then_inc(dve_full, 1)
            for t, (t0, n) in enumerate(TILES):
                b = dbank()
                pe.wait_ge(s_mask, 3)
                for s in range(t):
                    mm(b[0:n, 0:NE], ones[:, 0:n], mask[:, s, :], s == 0, False)
                mm(b[0:n, 0:NE], C("tri", n)[:, 0:n], mask[0:n, t, :], t == 0, True).then_inc(dve_full, 1)
            b = dbank()
            for t, (t0, n) in enumerate(TILES):
                last = mm(b[:, 0:NE], ones[0:n, :], mask[0:n, t, :], t == 0, t == 2)
            last.then_inc(dve_full, 1)
            def select(j, shift=0):
                pe.wait_ge(e_sel, j + (1 + 2 * shift))
                for t, (t0, n) in enumerate(TILES):
                    for p in range(2):
                        for half in range(2):
                            last = mm(psum[0:CAP, 6 + half, :], sel[0:n, t, :], h2s[0:n, p, t, half * 512:(half + 1) * 512],
                                      t == 0 and p == 0, t == 2 and p == 1)
                last.then_inc(e_gath, 1)

            def turn(j, shift=0):
                pe.wait_ge(e_xg, j + (1 + shift))
                for k in range(KD):
                    last = tr(turned[:, k, :], xa[:, k * P:(k + 1) * P])
                last.then_inc(e_turn, 1)

            def products(q, i, out, stat, steps, end=False):
                wait_low(pe, q, i)
                for r in range(steps):
                    for p, w in enumerate((whi, wlo)):
                        for b in range(4 // steps):
                            last = mm(psum[:, out + b, :], stat[:, r, :],
                                      w[:, i % NSPLIT, (r * (4 // steps) + b) * 512:(r * (4 // steps) + b + 1) * 512],
                                      False, end and r == steps - 1 and p == 1)
                last.then_inc(c_free, 1)

            def gate_up(j, chunks, shift=0, ahead=True):
                pe.wait_ge(e_xs, j + (1 + shift))
                pe.wait_ge(e_bg, j + (1 + shift))
                if not isinstance(j, int):
                    pe.wait_ge(e_sum, j)
                for b in range(4):
                    mm(psum[:, b, :], bsg[:, :], bias_s[:, b * 512:(b + 1) * 512], True, False)
                for k, (q, i) in enumerate(chunks):
                    if ahead and k == 2:
                        select(j + 1)
                    if ahead and k == 5:
                        if not isinstance(j, int):
                            pe.wait_ge(e_act, j)
                        turn(j + 1)
                    products(q, i, 0, xs_[:, k:k + 1, :], 1, k == KD - 1)

            def down(j, chunks):
                pe.wait_ge(e_as, j + 1)
                pe.wait_ge(e_bd, j + 1)
                pe.wait_ge(e_y, j)
                for b in range(2):
                    mm(psum[:, 4 + b, :], bsd[:, :], bias_s[:, (4 + b) * 512:(5 + b) * 512], True, False)
                for k, (q, i) in enumerate(chunks):
                    products(q, i, 4, as2[:, 2 * k:2 * k + 2, :], 2, k == 3)

            pe.wait_ge(act_done, ACT_JOB["end"])
            pe.wait_ge(dve_done, DVE_JOB["end"])
            pe.wait_ge(s_bsplit, 1)
            select(0)
            turn(0)
            gate_up(0, [(0, 4 + c) for c in range(8)])
            with pe.Fori(1, NE) as j:
                gate_up(j, [(j, i) for i in range(8)])
                down(j - 1, [(j, i) for i in range(8, 12)])
            pe.wait_ge(e_act, NE)
            turn(NE)
            down(NE - 1, [(NE, i) for i in range(4)])
            extra = extra_jobs(pe)
            with pe.Fori(0, NOVER) as o:
                with pe.If(extra > o):
                    j = pe.snap(o + NE)
                    pe.wait_ge(e_y, j)
                    select(j, 1)
                    turn(j, 1)
                    gate_up(j, [(o + (NE + (c + 4) // 12), (c + 4) % 12) for c in range(8)], 1, False)
                    pe.wait_ge(e_act, j + 1)
                    turn(j, 1)
                    down(j, [(o + (NE + (c + 4) // 12), (c + 4) % 12) for c in range(8, 12)])
                with pe.Else():
                    pe.wait_ge(s_route, 1)

        @block.vector
        def _(v):
            n_step, n_bank = [0], [0]

            def step(ins):
                n_step[0] += 1
                ins.then_inc(vs, 1)
                v.wait_ge(vs, n_step[0])

            def job(stage, i):
                assert DVE_JOB[stage] + i == n_bank[0], (stage, i, n_bank[0])
                v.wait_ge(dve_full, n_bank[0] + 1)
                b = psum[:, 4 + n_bank[0] % 3, :]
                n_bank[0] += 1
                return b

            TT, TS, STT, CP = nc.vector.tensor_tensor, nc.vector.tensor_scalar, nc.vector.scalar_tensor_tensor, nc.vector.tensor_copy

            def bc(ap, axis, shape):
                return ap.unsqueeze(axis).to_broadcast(shape)

            def inverse(out, in_):
                step(nc.vector.reciprocal(out, in_))

            v.wait_ge(s_const, 16)
            for t, (t0, n) in enumerate(TILES):
                v.wait_ge(s_ssq, t + 1)
                inverse(sc[0:n, 3 + t:4 + t], sc[0:n, t:t + 1])
                TS(x[0:n, t, :], x[0:n, t, :], sc[0:n, 3 + t:4 + t], None, ALU.mult).then_inc(s_xn, 1)

            at_h = 0
            for t, (t0, n) in enumerate(TILES):
                for half in range(2 if n == 128 else 1):
                    b = job("hT", at_h)
                    kk = 4 if n == 128 else 8
                    CP(hT[:, 4 * half:4 * half + kk, t0:t0 + n], b[:, 0:kk * n].rearrange("p (k q) -> p k q", k=kk)
                       ).then_inc(dve_done, 1)
                    at_h += 1
            b = job("vec", 0)
            v.wait_ge(dve_done, 5)
            step(CP(vecT[:, :], b[:, 0:32]))
            TT(hT[:, :, :], hT[:, :, :], bc(vecT[:, 0:8], 2, [P, KD, T]), ALU.mult).then_inc(dve_done, 1)

            qt = at(I0 + 4096, 4, 256)

            def rotate(t):
                n = TILES[t][1]
                cs, sn_ = (C(q, n)[:, t * 32:(t + 1) * 32].unsqueeze(1).to_broadcast([n, 8, 32]) for q in ("ropec", "ropes"))
                for c in range(3):
                    b = job("qkv", c) if t == 2 else job("qkv0", 3 * t + c)
                    if c == 2:
                        CP(vt[0:n, t, :], b[0:n, :]).then_inc(dve_done, 1)
                        continue
                    pv = b[0:n, :].rearrange("p (g w i) -> p g w i", w=2, i=32)
                    qv = qk[0:n, c, t, :].rearrange("p (g w i) -> p g w i", w=2, i=32)
                    ta, tb, tc, td = (qt[0:n, i, :].rearrange("p (g i) -> p g i", i=32) for i in range(4))
                    TT(ta, pv[:, :, 0, :], cs, ALU.mult)
                    TT(tb, pv[:, :, 1, :], sn_, ALU.mult)
                    TT(tc, pv[:, :, 1, :], cs, ALU.mult)
                    step(TT(td, pv[:, :, 0, :], sn_, ALU.mult))
                    TT(qv[:, :, 0, :], ta, tb, ALU.subtract)
                    step(TT(qv[:, :, 1, :], tc, td, ALU.add))
                    v.sem_inc(dve_done, 1)
            rotate(0)

            lr_, li_ = prm_in[:, 0, :], prm_in[:, 1, :]
            v.wait_ge(s_dt, 1)
            step(CP(pw[:, 0, :].rearrange("p (a q) -> p a q", a=2), bc(logdt[:, 2:4], 2, [16, 2, 64])))
            TT(pw[:, 1, :], lr_, pw[:, 0, :], ALU.mult).then_inc(s_lre, 1)
            step(STT(pw[:, 2, :], li_, 1.0 / (2 * math.pi), pw[:, 0, :], ALU.mult, ALU.mult))
            step(TS(pw[:, 3, :], pw[:, 2, :], RND, RND, ALU.add, ALU.subtract))
            TT(prm[:, 1, :], pw[:, 2, :], pw[:, 3, :], ALU.subtract).then_inc(s_fr, 1)
            lw = pw[:, 7:9, :]
            v.wait_ge(s_par, 16 * N_SMALL)
            step(TT(lamv[:, 0:3:2, :], lamv[:, 0:3:2, :], lamv[:, 1:4:2, :], ALU.mult))
            nc.vector.tensor_reduce(sc[:, 6:8], lamv[:, 0:3:2, :], AX.X, ALU.add).then_inc(s_lamd, 1)
            v.wait_ge(s_lame, 1)
            step(TT(sc[:, 10:11], sc[:, 8:9], sc[:, 9:10], ALU.subtract))
            step(TS(sc[:, 11:12], sc[:, 10:11], LAM_INIT, -1.0, ALU.add, ALU.mult))
            v.wait_ge(s_mag, 1)
            v.wait_ge(s_trig, 1)
            mag, sin1, cos1 = prm[:, 0, :], pw[:, 4, :], pw[:, 6, :]
            are, aim, t7, t8, den = pw[:, 7, :], pw[:, 8, :], pw[:, 9, :], pw[:, 10, :], pw[:, 11, :]
            step(TT(are, mag, cos1, ALU.mult))
            step(TS(are, are, -1.0, None, ALU.add))
            step(TT(aim, mag, sin1, ALU.mult))
            step(TT(t7, lr_, lr_, ALU.mult))
            step(TT(t8, li_, li_, ALU.mult))
            step(TT(t7, t7, t8, ALU.add))
            step(nc.vector.reciprocal(den, t7))
            step(TT(t7, are, lr_, ALU.mult))
            step(TT(t8, aim, li_, ALU.mult))
            step(TT(t7, t7, t8, ALU.add))
            step(TT(prm[:, 2, :], t7, den, ALU.mult))
            step(TT(t7, aim, lr_, ALU.mult))
            step(TT(t8, are, li_, ALU.mult))
            step(TT(t7, t7, t8, ALU.subtract))
            TT(prm[:, 3, :], t7, den, ALU.mult).then_inc(s_prm, 1)
            rotate(1)
            b = job("prm", 0)
            step(CP(prmT[:, :, :], b[:, 0:64].rearrange("p (i j) -> p i j", i=4)))
            v.sem_inc(dve_done, 1)
            b = job("x0", 0)
            CP(x0T[:, :, :, :].rearrange("p c b j -> p c (b j)"), b[:, 0:256].rearrange("p (c r) -> p c r", c=2)).then_inc(dve_done, 1)

            step(nc.vector.memset(at(I0, 4096), 0.0))
            fre, fim = bc(prmT[:, 2, :], 2, [P, NJ, GH]), bc(prmT[:, 3, :], 2, [P, NJ, GH])
            for c, (pad, ta, tb, op) in enumerate([(padr, 0, 1, ALU.subtract), (padi, 1, 0, ALU.add)]):
                step(TT(t16a, bin_[:, ta], fre, ALU.mult))
                step(TT(t16b, bin_[:, tb], fim, ALU.mult))
                pv = pad[:, :, :].rearrange("p (c j) q -> p c j q", c=NCT)
                ta4, tb4 = (q.rearrange("p (c j) h -> p c j h", c=NCT) for q in (t16a, t16b))
                for a in range(2):
                    for j in range(4):
                        o = (2 * j + a) * GH
                        pr = slice(64 * a, 64 * a + 64)
                        ins = TT(pv[pr, :, j, o:o + GH], ta4[pr, :, j, :], tb4[pr, :, j, :], op)
                step(ins)
            v.sem_inc(s_Bpad, 1)

            rotate(2)
            v.wait_ge(vs, n_step[0])
            v.sem_inc(s_kvtok, 1)

            for i in range(8):
                b = job("B", i)
                CP(bbT[:, i // 4, 4 * (i % 4):4 * (i % 4) + 4, :], b.rearrange("p (j q) -> p j q", j=4)).then_inc(dve_done, 1)
            for c in range(2):
                b = job("C", c).rearrange("p (c q) -> p c q", c=NCT)
                pv = (padr, padi)[c][:, :, :].rearrange("p (c j) q -> p c j q", c=NCT)
                for a in range(2):
                    for j in range(4):
                        o = (2 * j + a) * GH
                        pr = slice(64 * a, 64 * a + 64)
                        ins = TS(pv[pr, :, j, o:o + GH], b[pr, :, o:o + GH], 1.0 if c == 0 else -1.0, None, ALU.mult)
                ins.then_inc(dve_done, 1)

            v.wait_ge(act_done, ACT_JOB["z0"])
            for k in range(8):
                v.wait_ge(freed[k], 1)
            for ct in range(NCT):
                J = slice(4 * ct, 4 * ct + 4)
                tau = C("tau").unsqueeze(1).to_broadcast([P, 4, W5])
                fr = bc(prmT[:, 1, J], 2, [P, 4, W5])
                step(TT(t2, tau, fr, ALU.mult))
                step(TS(t4, t2, RND, RND, ALU.add, ALU.subtract))
                TT(cosT, t2, t4, ALU.subtract).then_inc(s_angT, 1)
                TT(dec, C("keep").unsqueeze(1).to_broadcast([P, 4, W5]), bc(prmT[:, 0, J], 2, [P, 4, W5]), ALU.mult)
                for c, z in enumerate((zr, zi)):
                    ins = CP(z[:, :, SEQ:W5].rearrange("p j (b s) -> p j b s", s=NS + 1)[:, :, :, 0],
                             x0T[:, c, :, J].rearrange("p b j -> p j b"))
                step(ins)
                v.wait_ge(s_tabT, ct + 1)
                v.wait_ge(act_done, ACT_JOB[f"z{ct}"] + 8)
                if ct:
                    v.wait_ge(dve_full, DVE_JOB["y"] + ct)
                TT(t1, cosT, zr, ALU.mult)
                TT(t2, sinT, zi, ALU.mult)
                TT(t3, cosT, zi, ALU.mult)
                step(TT(t4, sinT, zr, ALU.mult))
                TT(t1, t1, t2, ALU.add)
                step(TT(t3, t3, t4, ALU.subtract))

                def flat(a):
                    return a.rearrange("p j w -> p (j w)")
                nc.vector.tensor_tensor_scan(flat(zr), flat(dec), flat(t1), 0.0, ALU.mult, ALU.add)
                step(nc.vector.tensor_tensor_scan(flat(zi), flat(dec), flat(t3), 0.0, ALU.mult, ALU.add))
                TT(t1, cosT, zr, ALU.mult)
                TT(t2, sinT, zi, ALU.mult)
                TT(t3, cosT, zi, ALU.mult)
                step(TT(t4, sinT, zr, ALU.mult))
                v.sem_inc(s_zfree, 1)
                TT(t1, t1, t2, ALU.subtract)
                step(TT(t3, t3, t4, ALU.add))
                v.sem_inc(s_xT5, 1)
                for c, q in enumerate((t1, t3)):
                    CP(finp[:, c, J], q[:, :, SEQ - 1])
                    ins = CP(fins[:, c, :, J].rearrange("p b j -> p j b"),
                             q[:, :, SEQ:W5].rearrange("p j (b s) -> p j b s", s=NS + 1)[:, :, :, NS])
                step(ins)
                b = job("y", ct)
                d = vecT[:, 28 + ct:29 + ct]
                if ct == 0:
                    v.wait_ge(s_zero, 16)
                STT(yT[:, ct, 0:SEQ], uT[:, ct, 0:SEQ], d, b[:, 0:SEQ], ALU.mult, ALU.add)
                step(STT(yT[:, ct, SEQ:T].rearrange("p (b s) -> p b s", s=NS), uT[:, ct, SEQ:T].rearrange("p (b s) -> p b s", s=NS),
                         d, b[:, SEQ:W5].rearrange("p (b s) -> p b s", s=NS + 1)[:, :, 1:], ALU.mult, ALU.add))
                v.sem_inc(dve_done, 1)
            v.sem_inc(s_s5, 1)
            b = job("fin", 0)
            CP(frow[0:NJ, 0:2, :], b[0:NJ, 0:256].rearrange("p (c q) -> p c q", c=2))
            step(CP(frow[:, 2:4, :], b[:, 256:512].rearrange("p (c q) -> p c q", c=2)))
            v.sem_inc(s_fin, 1)
            v.sem_inc(dve_done, 1)

            v.wait_ge(act_full, ACT_JOB["wT"])
            step(nc.vector.memset(qz, 0.0))
            for t, (t0, n) in enumerate(TILES):
                b = job("qk", 2 * t)[:, 0:H * n].rearrange("p (h q) -> p h q", h=H)
                CP(qz[0:64, :, 0, t0:t0 + n], b[0:64])
                CP(qz[64:128, :, 1, t0:t0 + n], b[64:128]).then_inc(dve_done, 1)
                b = job("qk", 2 * t + 1)[:, 0:H * n].rearrange("p (h q) -> p h q", h=H)
                CP(kT[:, :, t0:t0 + n], b).then_inc(dve_done, 1)

            def p_first(n):
                w = 128 * (n // 4 + 1)
                b = job("s", n)[:, 0:2 * w].rearrange("p (c k) -> p c k", c=2)
                m = C("causal")[:, 256 - w:256].unsqueeze(1).to_broadcast([P, 2, w])
                step(TT(pS[:, n % 2, :, 0:w], b, m, ALU.add))
                v.sem_inc(dve_done, 1)
                step(nc.vector.tensor_reduce(st4[:, n % 2, 0:2], pS[:, n % 2, :, 0:w], AX.X, ALU.max))
                step(TS(st4[:, n % 2, 0:2], st4[:, n % 2, 0:2], -SCALE, None, ALU.mult))
                v.sem_inc(s_nb, 1)

            def p_second(n):
                w = 128 * (n // 4 + 1)
                v.wait_ge(s_pexp, n + 1)
                if n >= 2:
                    v.wait_ge(act_full, ACT_JOB["wT"] + n - 1)
                r = st4[:, 2 + n % 2, 0:2]
                step(nc.vector.reciprocal(r, st4[:, n % 2, 2:4]))
                step(TT(r[:, 1:2], r[:, 1:2], sc[:, 11:12], ALU.mult))
                step(TS(pW[:, n % 2, 0:w], pE[:, n % 2, 0, 0:w], r[:, 0:1], None, ALU.mult))
                STT(pW[:, n % 2, 0:w], pE[:, n % 2, 1, 0:w], r[:, 1:2], pW[:, n % 2, 0:w], ALU.mult, ALU.add).then_inc(s_w, 1)

            p_first(0)
            for n in range(8):
                if n + 1 < 8:
                    p_first(n + 1)
                p_second(n)
                if n in (4, 7):
                    i = n // 5
                    v.wait_ge(s_pv, 4 * (i + 1))
                    CP(ot[:, i, :], psum[:, 7, :]).then_inc(s_pvr, 1)
            v.wait_ge(s_late, 64)
            step(TS(subg, subg, 1.0 - LAM_INIT, None, ALU.mult))

            def head_norm(t, n):
                o = ot[0:n, t, :].rearrange("p (h d) -> p h d", h=H)
                sq = tmp2[0:n, :].rearrange("p (h d) -> p h d", h=H)
                step(TT(sq, o, o, ALU.mult))
                nc.vector.tensor_reduce(st4[0:n, 0, :], sq, AX.X, ALU.add).then_inc(s_hsum, 1)
                v.wait_ge(s_hrms, t + 1)
                inverse(st4[0:n, 1, :], st4[0:n, 2, :])
                step(TT(o, o, bc(st4[0:n, 1, :], 2, [n, H, DV]), ALU.mult))
                TT(o, o, subg[0:n, :].unsqueeze(1).to_broadcast([n, H, DV]), ALU.mult).then_inc(s_ln, 1)

            v.wait_ge(s_pvr, 2)
            STEPS = 7

            class Chain:
                def __init__(self, base):
                    self.base, self.k = base, 0

                def __call__(self, ins):
                    self.k += 1
                    ins.then_inc(s_chain, 1)
                    v.wait_ge(s_chain, self.base + self.k)

            def q_block(i, own):
                if not isinstance(i, int):
                    v.wait_ge(s_new, i)
                q = qz[:, :, :, ds(i * NS + SEQ, NS)]
                high, low = (qs[:, o:o + 72 * H].rearrange("p (h c) -> p h c", h=H)[:, :, 0:QC].rearrange(
                    "p h (c s) -> p h c s", c=2) for o in (0, 32))
                own(CP(high, q))
                TT(low, q, high, ALU.subtract).then_inc(s_qb, 1)

            def key_low(i, pg):
                v.wait_ge(p_keyh, i * NPG + (pg + 1))
                place = (slice(None), (pg // 2) % 2, slice(None), slice((pg % 2) * P, (pg % 2 + 1) * P))
                TT(keyl[place], psum[:, pg % 2, :].rearrange("p (h c) -> p h c", h=H), keyh[place], ALU.subtract).then_inc(p_keyl, 1)

            def value_low(j, pg):
                v.wait_ge(p_valh, j * NPG + (pg + 1))
                TT(vall[:, pg % 3, :], ring[:, SLOT[f"V{pg // 4}"], (pg % 4) * 512:(pg % 4 + 1) * 512], valh[:, pg % 3, :],
                   ALU.subtract).then_inc(p_vallv, 1)

            def bank_sum(i, b):
                v.wait_ge(s_low, i * 5 + (b + 1))
                q = ss[:, b * 512:(b + 1) * 512]
                TT(q, psum[0:32, 2 + b, :], q, ALU.add).then_inc(s_sum, 1)
                v.wait_ge(s_sum, i * 5 + (b + 1))
                nc.vector.tensor_reduce(mx5[:, b:b + 1], q, AX.X, ALU.max)

            def new_sum(i, own):
                v.wait_ge(s_low, i * 5 + 5)
                TT(snw, psum[0:32, 6, 0:NSMP], snw, ALU.add).then_inc(s_sum, 1)
                v.wait_ge(s_sum, i * 5 + 5)
                own(TT(snw, snw, C("newmask", 32)[:, ds(i * NSMP, NSMP)], ALU.add))
                own(nc.vector.tensor_reduce(mx5[:, 4:5], snw, AX.X, ALU.max))
                own(nc.vector.tensor_reduce(mcol, mx5, AX.X, ALU.max))
                TS(nbias, mcol, -SCALE, None, ALU.mult).then_inc(s_nbias, 1)

            def denominators(j, own):
                v.wait_ge(s_ex, j + 1)
                own(TT(etot, esum[:, 0:1], esum[:, 1:2], ALU.add))
                nc.vector.reciprocal(rden, etot).then_inc(s_rden, 1)

            def exps_low(j):
                v.wait_ge(s_eh, j + 1)
                TT(e2[0:NSMP, NPG, 32:64], psum[0:NSMP, 7, 0:32], e2[0:NSMP, NPG, 0:32], ALU.subtract)
                TT(e2[:, 0:NPG, 32:64], psum[:, 6, :].rearrange("p (g c) -> p g c", g=NPG), e2[:, 0:NPG, 0:32],
                   ALU.subtract).then_inc(s_el, 1)

            def out_sum(j, own):
                v.wait_ge(s_oL, j + 1)
                own(TT(oS, psum[0:32, 7, :], oL, ALU.add))
                v.wait_ge(s_rden, j + 1)
                TS(oS, oS, rden, None, ALU.mult).then_inc(s_oS, 1)

            def out_heads(j, own):
                v.wait_ge(s_oT, j + 1)
                own(CP(on.rearrange("p h c s -> p h (c s)"), psum[:, 7, 0:40 * H].rearrange("p (h c) -> p h c", h=H)[:, :, 0:QC]))
                STT(oTs[:, :, ds(j * NS, NS)], on[:, :, 1, :], sc[:, 11:12], on[:, :, 0, :], ALU.mult, ALU.add).then_inc(s_do, 1)

            def batch(i, j, own):
                q_block(i, own)
                for g in range(NPG // 2):
                    key_low(i, 2 * g)
                    key_low(i, 2 * g + 1)
                    if j is not None and g == 1:
                        value_low(j, 1)
                    if j is not None and g == E_STEP:
                        exps_low(j)
                        denominators(j, own)
                    if g in (2, 4, 6):
                        bank_sum(i, g // 2 - 1)
                    if j is not None and g in V_STEP:
                        for pg in range(3 + V_STEP[g][0], min(NPG, 3 + V_STEP[g][1])):
                            if pg % 2:
                                value_low(j, pg)
                if j is not None:
                    out_sum(j, own)
                bank_sum(i, 3)
                new_sum(i, own)
                if j is not None:
                    out_heads(j, own)

            for t in range(2):
                head_norm(t, 128)
            step(TS(qs[:, :], cst[:, 0:72 * H + 32], 0.0, None, ALU.mult))
            step(CP(knh[:, :, :], kT[:, :, SEQ:T]))
            step(CP(vnh[:, :], vt[0:NSMP, 2, :]))
            step(TT(knl[:, :, :], kT[:, :, SEQ:T], knh[:, :, :], ALU.subtract))
            step(TT(vnl[:, :], vt[0:NSMP, 2, :], vnh[:, :], ALU.subtract))
            v.sem_inc(s_newkv, 1)
            batch(0, None, Chain(0))
            with v.Fori(1, NB) as i:
                batch(i, v.snap(i - 1), Chain(v.snap(i * STEPS + (4 - STEPS))))
            own = Chain((NB - 1) * STEPS + 4)
            value_low(NB - 1, 1)
            exps_low(NB - 1)
            denominators(NB - 1, own)
            for pg in range(3, NPG, 2):
                value_low(NB - 1, pg)
            out_sum(NB - 1, own)
            out_heads(NB - 1, own)

            step(CP(ot[0:NSMP, 2, :], job("oS", 0)[0:NSMP, :]))
            v.sem_inc(dve_done, 1)
            head_norm(2, NSMP)
            for t, (t0, n) in enumerate(TILES):
                CP(oT[:, :, t0:t0 + n], job("oT", t)[:, 0:H * n].rearrange("p (h q) -> p h q", h=H)).then_inc(dve_done, 1)
            v.wait_ge(act_done, ACT_JOB["glu"] + 4)
            TT(yT, yT, sg, ALU.mult).then_inc(s_yglu, 1)
            for i in range(KD):
                TT(mg[:, i, :], gates[:, i, :], job("bs", i)[:, 0:T], ALU.mult).then_inc(dve_done, 1)
            for i in range(KD):
                step(TT(tmp, gates[:, KD + i, :], job("ba", i)[:, 0:T], ALU.mult))
                v.sem_inc(dve_done, 1)
                step(TT(mg[:, i, :], mg[:, i, :], tmp, ALU.add))
            v.sem_inc(s_mg, 1)
            v.wait_ge(s_xagain, 48)
            for t, (t0, n) in enumerate(TILES):
                for half in range(2):
                    xx = x[0:n, t, half * 512:(half + 1) * 512]
                    step(TT(xx, xx, job("out", 2 * t + half)[0:n, :], ALU.add))
                    v.sem_inc(dve_done, 1)
                v.sem_inc(s_xres, 1)
            for t, (t0, n) in enumerate(TILES):
                v.wait_ge(s_ssq2, t + 1)
                inverse(sc[0:n, 3:4], sc[0:n, t:t + 1])
                step(STT(h2[0:n, t, :], x[0:n, t, :], sc[0:n, 3:4], gvec[0:n, :], ALU.mult, ALU.mult))
                v.sem_inc(s_h2, 1)
            for t, (t0, n) in enumerate(TILES):
                v.wait_ge(s_h2h, t + 1)
                TT(h2s[0:n, 1, t, :], h2[0:n, t, :], h2s[0:n, 0, t, :], ALU.subtract).then_inc(s_h2s, 1)
            at_h = 0
            for t, (t0, n) in enumerate(TILES):
                for half in range(2 if n == 128 else 1):
                    kk = 4 if n == 128 else 8
                    CP(h2T[:, 4 * half:4 * half + kk, t0:t0 + n],
                       job("h2T", at_h)[:, 0:kk * n].rearrange("p (k q) -> p k q", k=kk)).then_inc(dve_done, 1)
                    at_h += 1
            for t, (t0, n) in enumerate(TILES):
                step(TT(lg[0:n, t, :], job("lg", t)[0:n, 0:NE], brt[0:n, :], ALU.add))
                v.sem_inc(dve_done, 1)
                step(nc.vector.max(mx8[0:n, t, :], lg[0:n, t, :]))
                step(nc.vector.max_index(eight[0:n, t, :], mx8[0:n, t, :], lg[0:n, t, :]))
                TS(nmx[0:n, t, :], mx8[0:n, t, 0:1], -1.0, None, ALU.mult).then_inc(s_nmx, 1)
                step(CP(idxf[0:n, t, :], eight[0:n, t, 0:TOPK]))
                step(TT(oneh[0:n, t], C("iota", n)[:, 0:NE].unsqueeze(1).to_broadcast([n, TOPK, NE]),
                        bc(idxf[0:n, t, :], 2, [n, TOPK, NE]), ALU.is_equal))
                step(nc.vector.tensor_reduce(mask[0:n, t, :], oneh[0:n, t].rearrange("p k e -> p e k"), AX.X, ALU.add))
                v.sem_inc(s_mask, 1)
            for t, (t0, n) in enumerate(TILES):
                v.wait_ge(s_gexp, t + 1)
                step(nc.vector.reciprocal(gsum[0:n, t, :], gsum[0:n, t, :]))
                TS(gk[0:n, t, :], gk[0:n, t, :], gsum[0:n, t, :], None, ALU.mult)
            for t, (t0, n) in enumerate(TILES):
                b = job("pos", t)[0:n, 0:NE]
                step(STT(posm[0:n, t, 0:NE], b, 1.0, mask[0:n, t, :], ALU.add, ALU.mult))
                TS(posm[0:n, t, 0:NE], posm[0:n, t, 0:NE], -1.0, None, ALU.add)
                nc.vector.memset(posm[0:n, t, NE:NE + 2], -1.0)
                step(TT(tk[0:n, t], oneh[0:n, t], b.unsqueeze(1).to_broadcast([n, TOPK, NE]), ALU.mult))
                v.sem_inc(dve_done, 1)
                step(nc.vector.tensor_reduce(slotk[0:n, t, :], tk[0:n, t], AX.X, ALU.add))
            step(CP(cnt[:, 0, :], job("cnt", 0)[:, 0:NE]))
            v.sem_inc(dve_done, 1)
            step(TS(cnt[:, 1, :], cnt[:, 0, :], float(CAP), None, ALU.is_gt))
            for m in range(2, 5):
                step(STT(cnt[:, 1, :], cnt[:, 0, :], float(m * CAP), cnt[:, 1, :], ALU.is_gt, ALU.add))
            step(nc.vector.tensor_tensor_scan(cnt[:, 2, :], C("ones")[:, 0:NE], cnt[:, 1, :], 0.0, ALU.mult, ALU.add))
            step(TT(cnt[:, 3, :], cnt[:, 2, :], cnt[:, 1, :], ALU.subtract))
            jobs, full = C("jobs"), [P, NOVER, NE]
            step(TT(ytab, bc(jobs, 2, full), cnt[:, 2, :].unsqueeze(1).to_broadcast(full), ALU.is_ge))
            step(nc.vector.tensor_reduce(jobf[:, 0:NOVER], ytab, AX.X, ALU.add))
            step(TT(ytab, ytab, cnt[:, 1, :].unsqueeze(1).to_broadcast(full), ALU.mult))
            step(nc.vector.tensor_reduce(jobf[:, NOVER:2 * NOVER], ytab, AX.X, ALU.add))
            step(TT(jobf[:, NOVER:2 * NOVER], jobs, jobf[:, NOVER:2 * NOVER], ALU.subtract))
            step(TS(jobf[:, NOVER:2 * NOVER], jobf[:, NOVER:2 * NOVER], 1.0, 4.0, ALU.add, ALU.min))
            step(TS(jobf[:, 0:NOVER], jobf[:, 0:NOVER], NE - 1.0, None, ALU.min))
            step(CP(jobf[:, 2 * NOVER:2 * NOVER + 1], cnt[:, 2, NE - 1:NE]))
            step(CP(jobi[:, :], jobf[:, :]))
            for t, (t0, n) in enumerate(TILES):
                step(TT(tk[0:n, t], oneh[0:n, t], cnt[0:n, 3, :].unsqueeze(1).to_broadcast([n, TOPK, NE]), ALU.mult))
                step(nc.vector.tensor_reduce(basek[0:n, t, :], tk[0:n, t], AX.X, ALU.add))
                step(TS(big[0:n, t, :], slotk[0:n, t, :], float(CAP), None, ALU.is_ge))
                step(STT(basek[0:n, t, :], basek[0:n, t, :], float(NE - 1), idxf[0:n, t, :], ALU.add, ALU.subtract))
                step(TT(basek[0:n, t, :], basek[0:n, t, :], big[0:n, t, :], ALU.mult))
                step(TT(basek[0:n, t, :], basek[0:n, t, :], idxf[0:n, t, :], ALU.add))
                step(STT(rowf[0:n, t, :], basek[0:n, t, :], float(CAP), slotk[0:n, t, :], ALU.mult, ALU.add))
                step(CP(rowi[0:n, t, :], rowf[0:n, t, :]))
            v.wait_ge(s_bias, 64)
            step(CP(bias_s[:, :], braw))
            step(TT(bias_s[32:64, :], braw[32:64, :], bias_s[32:64, :], ALU.subtract))
            v.sem_inc(s_bsplit, 1)
            v.sem_inc(s_route, 1)

            def select(j, e, t=None, shift=0):
                if not (isinstance(j, int) and j == 0):
                    v.wait_ge(e_gath, j + shift)
                for s, (t0, n) in enumerate(TILES):
                    if t is None:
                        ins = TS(sel[0:n, s, :], C("iota", n), posm[0:n, s, ds(e, 1)], None, ALU.is_equal)
                    else:
                        ins = TS(sel[0:n, s, :], C("iota", n), C("tile0", n)[:, ds(t, 1)], posm[0:n, s, ds(e, 1)],
                                 ALU.add, ALU.is_equal)
                ins.then_inc(e_sel, 1)

            def bias_row(out, e, done):
                TS(out[:, :], C("upper", 64), C("expert", 64)[:, ds(e, 1)], None, ALU.mult).then_inc(done, 1)

            def low(q, i):
                if i in POOL_CHUNKS:
                    return
                v.wait_ge(c_hi, q * 12 + (i - 3))
                TT(wlo[:, i % NSPLIT, :], ring[:, chunk_raw(i), :], whi[:, i % NSPLIT, :], ALU.subtract).then_inc(c_lov, 1)

            def clamp(j):
                v.wait_ge(e_guL, j + 1)
                TT(gus.rearrange("p (b n) -> p b n", b=4), psum[0:CAP, 0:4, :], guL.rearrange("p (b n) -> p b n", b=4),
                   ALU.add).then_inc(e_sum, 1)
                v.wait_ge(e_sum, j + 1)
                TS(gg, gus[:, 0::2], LIMIT, None, ALU.min).then_inc(e_g, 1)
                TS(uu, gus[:, 1::2], LIMIT, -LIMIT, ALU.min, ALU.max).then_inc(e_u, 1)

            def activate(j):
                v.wait_ge(e_sig, j + 1)
                v.wait_ge(e_u, j + 1)
                TT(gg, gg, sig, ALU.mult).then_inc(e_m, 1)
                v.wait_ge(e_m, j + 1)
                STT(xa[CAP:P, :], uu, 1.0, gg, ALU.add, ALU.mult).then_inc(e_act, 1)

            def low_x(j, shift=0):
                v.wait_ge(e_xh, j + (1 + shift))
                TT(xs_[:, :, CAP:], turned_x, xs_[:, :, 0:CAP], ALU.subtract).then_inc(e_xs, 1)

            def low_a(j):
                v.wait_ge(e_ah, j + 1)
                TT(as2[:, :, CAP:], turned_a, as2[:, :, 0:CAP], ALU.subtract).then_inc(e_as, 1)

            def sum_y(j):
                v.wait_ge(e_yL, j + 1)
                v.wait_ge(e_out, j * 16)
                TT(yS.rearrange("p (b n) -> p b n", b=2), psum[0:CAP, 4:6, :], yL.rearrange("p (b n) -> p b n", b=2),
                   ALU.add).then_inc(e_y, 1)

            step(nc.vector.memset(xa[CAP:P, :], 0.0))
            select(0, 0)
            bias_row(bsg, 0, e_bg)
            bias_row(bsd, 0, e_bd)
            for c in range(NSPLIT):
                low(0, 4 + c)
            low_x(0)
            select(1, 1)
            for c in range(NSPLIT, 6):
                low(0, 4 + c)
            select(2, 2)
            for c in range(6, 8):
                low(0, 4 + c)
            clamp(0)
            bias_row(bsg, 1, e_bg)
            low_x(1)
            low(1, 0)
            activate(0)
            low(1, 1)
            with v.Fori(1, NE) as j:
                for i in (2, 3, 4, 5):
                    low(j, i)
                select(j + 2, j + 2)
                low(j, 6)
                low_a(j - 1)
                for i in (7, 8, 9, 10):
                    low(j, i)
                clamp(j)
                bias_row(bsg, j + 1, e_bg)
                low_x(j + 1)
                low(j, 11)
                activate(j)
                low(j + 1, 0)
                low(j + 1, 1)
                sum_y(j - 1)
                bias_row(bsd, j, e_bd)
            low_a(NE - 1)
            for i in (2, 3):
                low(NE, i)
            sum_y(NE - 1)
            most = extra_jobs(v)
            with v.Fori(0, NOVER) as o:
                with v.If(most > o):
                    j = v.snap(o + NE)
                    e = v.value_load(jobi[0:1, ds(o, 1)], min_val=0, max_val=NE - 1)
                    t = v.value_load(jobi[0:1, ds(o + NOVER, 1)], min_val=0, max_val=4)
                    select(j, e, t, 1)
                    bias_row(bsg, e, e_bg)
                    bias_row(bsd, e, e_bd)
                    low_x(j, 1)
                    for c in range(12):
                        if c == 10:
                            clamp(j)
                            activate(j)
                            low_a(j)
                        low(o + (NE + (c + 4) // 12), (c + 4) % 12)
                    sum_y(j)
                with v.Else():
                    v.wait_ge(s_route, 1)

            for t, (t0, n) in enumerate(TILES):
                v.wait_ge(s_gath[t], 16 * TOPK)
                for k in range(TOPK):
                    step(STT(x[0:n, t, :], ycomb[0:n, t, k, :], gk[0:n, t, k:k + 1], x[0:n, t, :], ALU.mult, ALU.add))
                v.sem_inc(s_comb, 1)
            v.wait_ge(s_gfin, 16)
            for t, (t0, n) in enumerate(TILES):
                v.wait_ge(s_ssq2, 3 + t + 1)
                inverse(sc[0:n, 3:4], sc[0:n, t:t + 1])
                step(STT(x[0:n, t, :], x[0:n, t, :], sc[0:n, 3:4], gvec[0:n, :], ALU.mult, ALU.mult))
                v.sem_inc(s_ynorm, 1)


_UNUSED = ()
_OUTS = [
    ("o_y_prompt", (1, SEQ, D)), ("o_y_sample", (NB, NS, D)),
    ("o_k_prompt", (1, 1, SEQ, H, DV)), ("o_v_prompt", (1, 1, SEQ, H, DV)),
    ("o_re_prompt", (1, 1, G, SP_)), ("o_im_prompt", (1, 1, G, SP_)),
    ("o_k_sample", (1, NB, NS, H, DV)), ("o_v_sample", (1, NB, NS, H, DV)),
    ("o_re_sample", (1, NB, G, SP_)), ("o_im_sample", (1, NB, G, SP_)),
]


def kernel(**inputs):
    import concourse.bacc as bacc
    from concourse.bass_utils import run_bass_kernel_spmd as run

    nc = bacc.Bacc("TRN2", target_bir_lowering=False, num_devices=1)
    arrays, A = {}, {}
    for name, a in {**inputs, "consts": constants()}.items():
        arrays[f"in_{name}"] = a = np.ascontiguousarray(a)
        A[name] = nc.dram_tensor(f"in_{name}", a.shape, mybir.dt.from_np(a.dtype), kind="ExternalInput").ap()
    for name, shape in _OUTS:
        A[name] = nc.dram_tensor(name, shape, F32, kind="ExternalOutput").ap()
    build(nc, A)
    r = run(nc, [arrays], core_ids=[0])
    return tuple(r.results[0][name] for name, _ in _OUTS)
```
